# Optimizing a Trainium2 kernel written in Bass

```python
import math
import jax, jax.numpy as jnp
from jax import lax
import numpy as np

D_MODEL = 1024
BATCH = 1
SEQ = 512
DEPTH = 1
DEC_BATCH = 8
DEC_SEQ = 1
PAST_LEN = 2048
PAGE_SIZE = 128

HEAD_DIM = 64
N_HEADS = 8
N_KV_HEADS = 2
GROUP = N_HEADS // N_KV_HEADS
ATTN_WIDTH = N_HEADS * HEAD_DIM
KV_WIDTH = N_KV_HEADS * HEAD_DIM
POOL_WIDTH = D_MODEL - ATTN_WIDTH
POOL_WINDOWS = (2, 4, 8, 16)
POOL_GROUP = POOL_WIDTH // len(POOL_WINDOWS)
POOL_BUF = max(POOL_WINDOWS) - 1
IN_WIDTH = ATTN_WIDTH + 2 * KV_WIDTH + POOL_WIDTH
WINDOW = 128
ATTN_BLOCK = 128
N_BUCKETS = 32
MAX_EXACT = 16
REL_MAX_DIST = 128
N_EXPERTS = 32
TOP_K = 4
D_FF = D_MODEL
SWIGLU_LIMIT = 7.0
SWIGLU_ALPHA = 1.702
MOE_BLOCK = 128
EPS = 1e-6
NEG_INF = -1e30

kernel_name = "hybrid_swa_pool_moe_adaln_step"

def rms_norm(x, g):
    xf = x.astype(jnp.float32)
    y = xf * lax.rsqrt(jnp.mean(xf * xf, axis=-1, keepdims=True) + EPS)
    return (y * g.astype(jnp.float32)).astype(x.dtype)

def modulate(x, shift, scale):
    return x * (1 + scale[:, None, :]) + shift[:, None, :]

def modulation(c, w_ada, b_ada):
    return jnp.split(jax.nn.silu(c) @ w_ada + b_ada, 6, axis=-1)

def t5_bucket(rel):
    n = jnp.maximum(rel, 0)
    nf = jnp.maximum(n, 1).astype(jnp.float32)
    large = MAX_EXACT + (jnp.log(nf / MAX_EXACT) / math.log(REL_MAX_DIST / MAX_EXACT)
                         * (N_BUCKETS - MAX_EXACT)).astype(jnp.int32)
    large = jnp.minimum(large, N_BUCKETS - 1)
    return jnp.where(n < MAX_EXACT, n, large)

def attend(q, k, v, rel, valid, sinks, rel_table):
    s = jnp.einsum('...qkgd,...skd->...kgqs', q, k).astype(jnp.float32) * (HEAD_DIM ** -0.5)
    bias = rel_table[t5_bucket(rel)].astype(jnp.float32)
    bias = bias.reshape(rel.shape + (N_KV_HEADS, GROUP)).transpose(2, 3, 0, 1)
    s = jnp.where(valid[..., None, None, :, :], s + bias, NEG_INF)
    sink = jnp.broadcast_to(sinks.astype(jnp.float32).reshape(N_KV_HEADS, GROUP, 1, 1),
                            s.shape[:-1] + (1,))
    p = jax.nn.softmax(jnp.concatenate([s, sink], axis=-1), axis=-1)[..., :-1]
    return jnp.einsum('...kgqs,...skd->...qkgd', p.astype(v.dtype), v)

def swa_prompt(q, k, v, sinks, rel_table):
    B, S = q.shape[:2]
    nblk = S // ATTN_BLOCK
    qb = q.reshape(B, nblk, ATTN_BLOCK, N_KV_HEADS, GROUP, HEAD_DIM)
    kb = k.reshape(B, nblk, ATTN_BLOCK, N_KV_HEADS, HEAD_DIM)
    vb = v.reshape(B, nblk, ATTN_BLOCK, N_KV_HEADS, HEAD_DIM)

    def band(t):
        prev = jnp.concatenate([jnp.zeros_like(t[:, :1]), t[:, :-1]], axis=1)
        return jnp.concatenate([prev, t], axis=2)

    qi = jnp.arange(ATTN_BLOCK, dtype=jnp.int32)[:, None]
    si = jnp.arange(2 * ATTN_BLOCK, dtype=jnp.int32)[None, :]
    rel = qi + ATTN_BLOCK - si
    kpos = (jnp.arange(nblk, dtype=jnp.int32)[:, None] - 1) * ATTN_BLOCK + si
    valid = ((rel >= 0) & (rel < WINDOW))[None] & (kpos >= 0)[:, None, :]
    out = attend(qb, band(kb), band(vb), rel, valid, sinks, rel_table)
    return out.reshape(B, S, ATTN_WIDTH)

def swa_sample(q, k_new, v_new, cache_k, cache_v, sinks, rel_table):
    Bd, T = q.shape[:2]
    W = cache_k.shape[1]
    kk = jnp.concatenate([cache_k, k_new], axis=1)
    vv = jnp.concatenate([cache_v, v_new], axis=1)
    rel = jnp.arange(T, dtype=jnp.int32)[:, None] + W - jnp.arange(W + T, dtype=jnp.int32)[None, :]
    valid = (rel >= 0) & (rel < WINDOW)
    out = attend(q, kk, vv, rel, valid, sinks, rel_table)
    return out.reshape(Bd, T, ATTN_WIDTH), kk[:, -W:], vv[:, -W:]

def pool_mixer(ext, pos0, w_pool, pool_scale):
    B, L, C = ext.shape
    T = L - POOL_BUF
    e32 = ext.astype(jnp.float32)
    cs = jnp.concatenate([jnp.zeros((B, 1, C), jnp.float32), jnp.cumsum(e32, axis=1)], axis=1)
    hi = cs[:, POOL_BUF + 1:]
    u = e32[:, POOL_BUF:]
    pos = pos0 + jnp.arange(T, dtype=jnp.int32)
    outs = []
    for g, w in enumerate(POOL_WINDOWS):
        sl = slice(g * POOL_GROUP, (g + 1) * POOL_GROUP)
        lo = cs[:, POOL_BUF + 1 - w: POOL_BUF + 1 - w + T, sl]
        cnt = jnp.minimum(pos + 1, w).astype(jnp.float32)[None, :, None]
        d = (hi[..., sl] - lo) / cnt - u[..., sl]
        outs.append(d.astype(ext.dtype) @ w_pool[g])
    return jnp.concatenate(outs, axis=-1) * pool_scale

def moe_ffn(h, w_router, b_router, w1, b1, w2, b2):
    N, D = h.shape
    logits = (h @ w_router + b_router).astype(jnp.float32)
    topv, topi = lax.top_k(logits, TOP_K)
    gates = jax.nn.softmax(topv, axis=-1)
    NK = N * TOP_K
    flat_e = topi.reshape(NK)
    flat_g = gates.reshape(NK)
    flat_t = jnp.repeat(jnp.arange(N, dtype=jnp.int32), TOP_K)
    order = jnp.argsort(flat_e)
    se, st, sg = flat_e[order], flat_t[order], flat_g[order]
    counts = jnp.bincount(flat_e, length=N_EXPERTS)
    starts = jnp.cumsum(counts) - counts
    padded = (counts + MOE_BLOCK - 1) // MOE_BLOCK * MOE_BLOCK
    pad_end = jnp.cumsum(padded)
    pad_start = pad_end - padded
    dest = pad_start[se] + (jnp.arange(NK, dtype=jnp.int32) - starts[se])
    n_blocks = -(-NK // MOE_BLOCK) + N_EXPERTS
    P = n_blocks * MOE_BLOCK
    buf_t = jnp.zeros((P,), jnp.int32).at[dest].set(st)
    buf_g = jnp.zeros((P,), jnp.float32).at[dest].set(sg)
    block_e = jnp.minimum(jnp.searchsorted(pad_end, jnp.arange(n_blocks, dtype=jnp.int32) * MOE_BLOCK,
                                           side='right'), N_EXPERTS - 1)

    def run_block(args):
        tok, e = args
        xb = h[tok]
        gu = xb @ w1[e] + b1[e]
        gate, up = gu[:, :D_FF], gu[:, D_FF:]
        gate = jnp.minimum(gate, SWIGLU_LIMIT)
        up = jnp.clip(up, -SWIGLU_LIMIT, SWIGLU_LIMIT)
        act = (up + 1) * (gate * jax.nn.sigmoid(SWIGLU_ALPHA * gate))
        return act @ w2[e] + b2[e]

    out = lax.map(run_block, (buf_t.reshape(n_blocks, MOE_BLOCK), block_e)).reshape(P, D)
    out = out * buf_g[:, None].astype(out.dtype)
    return jnp.zeros_like(h).at[buf_t].add(out)

def mixer_inputs(x, shift, scale, norm_mix, w_in, q_norm, k_norm):
    B, T, _ = x.shape
    h = modulate(rms_norm(x, norm_mix), shift, scale)
    z = h @ w_in
    q, k, v, u = jnp.split(z, [ATTN_WIDTH, ATTN_WIDTH + KV_WIDTH, ATTN_WIDTH + 2 * KV_WIDTH], axis=-1)
    q = rms_norm(q.reshape(B, T, N_KV_HEADS, GROUP, HEAD_DIM), q_norm)
    k = rms_norm(k.reshape(B, T, N_KV_HEADS, HEAD_DIM), k_norm)
    v = v.reshape(B, T, N_KV_HEADS, HEAD_DIM)
    return q, k, v, u

def block_output(x, attn, pool, gate_mix, shift_ffn, scale_ffn, gate_ffn, w_out, norm_ffn,
                 w_router, b_router, w1, b1, w2, b2):
    x = x + gate_mix[:, None, :] * (jnp.concatenate([attn, pool], axis=-1) @ w_out)
    h = modulate(rms_norm(x, norm_ffn), shift_ffn, scale_ffn)
    B, T, D = h.shape
    y = moe_ffn(h.reshape(B * T, D), w_router, b_router, w1, b1, w2, b2).reshape(B, T, D)
    return x + gate_ffn[:, None, :] * y

def setup_inputs(seed: int = 0) -> dict:
    key = jax.random.key(seed)
    ks = jax.random.split(key, 26)

    def nrm(k, shape, scale):
        return jax.random.normal(k, shape, jnp.float32) * scale

    W_BUF = min(WINDOW, PAST_LEN)
    D = D_MODEL
    return {
        'x_prompt': nrm(ks[0], (BATCH, SEQ, D), 1.0),
        'x_sample': nrm(ks[1], (DEC_BATCH, DEC_SEQ, D), 1.0),
        'cache_k': nrm(ks[2], (DEPTH, DEC_BATCH, W_BUF, N_KV_HEADS, HEAD_DIM), 1.0),
        'cache_v': nrm(ks[3], (DEPTH, DEC_BATCH, W_BUF, N_KV_HEADS, HEAD_DIM), 1.0),
        'state_pool': nrm(ks[4], (DEPTH, DEC_BATCH, POOL_BUF, POOL_WIDTH), 1.0),
        'c_prompt': nrm(ks[5], (BATCH, D), 1.0),
        'c_sample': nrm(ks[6], (DEC_BATCH, D), 1.0),
        'rel_bias': nrm(ks[7], (N_BUCKETS, N_HEADS), 0.5),
        'norm_mix': 1.0 + nrm(ks[8], (DEPTH, D), 0.1),
        'w_ada': nrm(ks[9], (DEPTH, D, 6 * D), D ** -0.5),
        'b_ada': nrm(ks[10], (DEPTH, 6 * D), 0.02),
        'w_in': nrm(ks[11], (DEPTH, D, IN_WIDTH), D ** -0.5),
        'q_norm': 1.0 + nrm(ks[12], (DEPTH, HEAD_DIM), 0.1),
        'k_norm': 1.0 + nrm(ks[13], (DEPTH, HEAD_DIM), 0.1),
        'sinks': nrm(ks[14], (DEPTH, N_HEADS), 1.0),
        'w_pool': nrm(ks[15], (DEPTH, len(POOL_WINDOWS), POOL_GROUP, POOL_GROUP), POOL_GROUP ** -0.5),
        'pool_scale': 0.5 + nrm(ks[16], (DEPTH, POOL_WIDTH), 0.1),
        'w_out': nrm(ks[17], (DEPTH, D, D), D ** -0.5),
        'norm_ffn': 1.0 + nrm(ks[18], (DEPTH, D), 0.1),
        'w_router': nrm(ks[19], (DEPTH, D, N_EXPERTS), D ** -0.5),
        'b_router': nrm(ks[20], (DEPTH, N_EXPERTS), 0.01),
        'w1': nrm(ks[21], (DEPTH, N_EXPERTS, D, 2 * D_FF), D ** -0.5),
        'b1': nrm(ks[22], (DEPTH, N_EXPERTS, 2 * D_FF), 0.01),
        'w2': nrm(ks[23], (DEPTH, N_EXPERTS, D_FF, D), D_FF ** -0.5),
        'b2': nrm(ks[24], (DEPTH, N_EXPERTS, D), 0.01),
    }

def reference(x_prompt, x_sample, cache_k, cache_v, state_pool, c_prompt, c_sample, rel_bias,
              norm_mix, w_ada, b_ada, w_in, q_norm, k_norm, sinks, w_pool, pool_scale, w_out,
              norm_ffn, w_router, b_router, w1, b1, w2, b2):
    xp, xs = x_prompt, x_sample
    S = xp.shape[1]
    w_keep_p = min(WINDOW, S)
    nkp, nvp, npp, nks, nvs, nps = [], [], [], [], [], []
    for l in range(DEPTH):
        sh_m, sc_m, g_m, sh_f, sc_f, g_f = modulation(c_prompt, w_ada[l], b_ada[l])
        q, k, v, u = mixer_inputs(xp, sh_m, sc_m, norm_mix[l], w_in[l], q_norm[l], k_norm[l])
        attn = swa_prompt(q, k, v, sinks[l], rel_bias)
        ext = jnp.concatenate([jnp.zeros((u.shape[0], POOL_BUF, POOL_WIDTH), u.dtype), u], axis=1)
        pool = pool_mixer(ext, 0, w_pool[l], pool_scale[l])
        nkp.append(k[:, -w_keep_p:])
        nvp.append(v[:, -w_keep_p:])
        npp.append(ext[:, -POOL_BUF:])
        xp = block_output(xp, attn, pool, g_m, sh_f, sc_f, g_f, w_out[l], norm_ffn[l],
                          w_router[l], b_router[l], w1[l], b1[l], w2[l], b2[l])
        sh_m, sc_m, g_m, sh_f, sc_f, g_f = modulation(c_sample, w_ada[l], b_ada[l])
        q, k, v, u = mixer_inputs(xs, sh_m, sc_m, norm_mix[l], w_in[l], q_norm[l], k_norm[l])
        attn, k_win, v_win = swa_sample(q, k, v, cache_k[l], cache_v[l], sinks[l], rel_bias)
        ext = jnp.concatenate([state_pool[l], u], axis=1)
        pool = pool_mixer(ext, PAST_LEN, w_pool[l], pool_scale[l])
        nks.append(k_win)
        nvs.append(v_win)
        nps.append(ext[:, -POOL_BUF:])
        xs = block_output(xs, attn, pool, g_m, sh_f, sc_f, g_f, w_out[l], norm_ffn[l],
                          w_router[l], b_router[l], w1[l], b1[l], w2[l], b2[l])
    return (xp, xs, jnp.stack(nkp), jnp.stack(nvp), jnp.stack(npp),
            jnp.stack(nks), jnp.stack(nvs), jnp.stack(nps))


_drawn_inputs = setup_inputs


def setup_inputs(seed=0):
    import zlib

    import numpy as np

    out = dict(_drawn_inputs(seed))
    spreads = {}
    factors = {'b1': 8.0, 'b2': 8.0}
    for name, (base, spread) in spreads.items():
        noise = np.random.default_rng([zlib.crc32(name.encode()), seed]).standard_normal(out[name].shape)
        drawn = base * np.exp(spread * noise) if base else spread * noise
        out[name] = __import__('jax').numpy.asarray(drawn.astype(out[name].dtype))
    for name, factor in factors.items():
        out[name] = (out[name] * factor).astype(out[name].dtype)
    return out
```

```python
from contextlib import ExitStack

import numpy as np
import concourse.bass as bass
from concourse import mybir
from concourse.alu_op_type import AluOpType as ALU

ACT = mybir.ActivationFunctionType
AX_X = mybir.AxisListType.X
F32, F32R, BF16, I32, U32 = (mybir.dt.float32, mybir.dt.float32r, mybir.dt.bfloat16, mybir.dt.int32,
                             mybir.dt.uint32)

P = 128
D = 1024
SEQ, NS = 512, 8
TOK = SEQ + NS
HD, NH, NKV, GROUP = 64, 8, 2, 4
AW, KVW, PW = 512, 128, 512
IN_W = AW + 2 * KVW + PW
WINDOWS = (2, 4, 8, 16)
BUF = 15
NE, TOPK, DFF = 32, 4, 1024
LIMIT, ALPHA, EPS, NEG = 7.0, 1.702, 1e-6, -1e30
TP = SEQ // P
TT = TP + 1
ROWS = [P] * TP + [NS]
KC = D // P
SL = P
NOVER = (TOK * TOPK) // (SL + 1)
NPASS = NE + NOVER
NCOL = NPASS + 2
OOB = 1 << 20
LINE = 3 * P - 1
UNITS, W1_UNITS = 12, 8
HL = 4
ADA_SLOTS = 3


def ds(i, n=1):
    return bass.ds(i, n)


class Record:
    pass


def build(nc, i, o):
    m = Record()
    m.i, m.o = i, o
    with ExitStack() as ctx:
        def sem(name):
            return ctx.enter_context(nc.semaphore(name))

        m.sem = sem

        def dram(name, shape, dt):
            return nc.dram_tensor(name, shape, dt).ap()

        base = (nc.sbuf_base + 63) // 64 * 64
        size = {F32: 4, F32R: 4, BF16: 2, I32: 4, U32: 4}

        def at(name, shape, dt, offset):
            return nc.alloc_sbuf_tensor_at(name, shape, dt, offset=offset)

        kept = [base]

        def small(name, shape, dt=F32):
            t = at(name, shape, dt, kept[0])
            kept[0] += (int(np.prod(shape[1:])) * size[dt] + 31) // 32 * 32
            return t

        m.bank = [ctx.enter_context(nc.psum_tensor(f"bank{b}", [P, 512], F32)) for b in range(8)]

        m.ident = small("ident", [P, P])
        m.vecsT = small("vecsT", [P, 68])
        m.modT = small("modT", [P, 48, 9])
        m.g1T = small("g1T", [P, KC, 9])
        m.cT = small("cT", [P, KC, 9])
        m.eps = small("eps", [P, 1])
        m.ssq = small("ssq", [P, TT])
        m.rstd = small("rstd", [P, TT])
        m.hss = small("hss", [P, 10])
        m.hrs = small("hrs", [P, 10])
        m.m8 = small("m8", [P, NH])
        m.negm = small("negm", [P, NH])
        m.esink = small("esink", [P, NH])
        m.den = small("den", [P, NH])
        m.rden = small("rden", [P, NH])
        m.sinks_bc = small("sinks_bc", [P, NH])
        m.s64 = small("s64", [64, 8])
        m.qn_bc = small("qn_bc", [P, HD])
        m.kn_bc = small("kn_bc", [P, HD])
        m.ss2 = small("ss2", [P, TT])
        m.rs2 = small("rs2", [P, TT])
        m.logits = small("logits", [P, TT, NE])
        m.br_bc = small("br_bc", [P, NE])
        m.tab = small("tab", [P, NCOL, 2], I32)
        m.eid = small("eid", [1, NCOL + 1], I32)
        m.qsT = small("qsT", [P, NKV, NS, GROUP])
        m.bias64 = small("bias64", [64, P + 1])
        m.rec = small("rec_sb", [P, 4, BUF + 1])
        m.dTs = small("dTs", [P, 4, NS])
        kept_end = kept[0]

        raw0 = (kept_end + 63) // 64 * 64
        SLOT = 2048 * 4
        m.raw = at("raw", [P, UNITS, 2048], F32, raw0)
        wproj0 = raw0 + 7 * SLOT
        m.w_in = at("w_in_sb", [P, KC, IN_W], F32, wproj0)
        m.w_out = at("w_out_sb", [P, KC, D], F32, wproj0)
        m.Kc = at("Kc", [P, NS, P], F32, raw0 + 6 * SLOT)
        m.relrep = at("relrep", [NE + 1, NH, P], F32, raw0 + 6 * SLOT)
        m.Vc = at("Vc", [P, NS, P], F32, raw0 + 6 * SLOT + 4096)
        H0 = raw0 + UNITS * SLOT

        s3 = raw0 + 3 * SLOT
        m.w_pool = at("w_pool_sb", [P, 4, P], F32, s3)
        m.sp = at("sp", [NS * BUF, PW], F32, s3 + 2048)
        m.spT = at("spT", [P, 4, NS, BUF], F32, s3 + 4096)
        m.oh_line = at("oh_line_sb", [NE + 1, 3 * P], F32, s3 + 6144)
        m.vrow = at("vrow", [68, P], F32, s3 + 7680)
        m.line = at("line", [P, NH, LINE], F32, raw0 + 4 * SLOT)
        m.crow = at("crow", [9, D], F32, raw0 + 4 * SLOT + 12288)
        m.xs = at("xs", [P, TT, D], F32, H0)
        m.hT = at("hT", [P, KC, TOK], F32, H0 + 20480)
        m.mixT = at("mixT", [P, KC, TOK], F32, H0 + 20480)
        m.zero = at("zero", [P, D], F32, H0 + 37120)
        m.qT = at("qT", [P, 4, TOK], F32, H0 + 37120)
        m.kT = at("kT", [P, NKV, TOK], F32, H0 + 45440)
        m.vt = at("vt", [P, TT, KVW], F32, H0 + 49600)
        m.U = at("U", [P, 4, BUF + SEQ], F32, H0 + 52160)
        m.Us = at("Us", [P, 4, NS], F32, H0 + 60608)
        m.xn = at("xn", [P, 2, D], F32, H0 + 60736)
        m.bias = at("bias", [P, NH, 2 * P], F32, H0 + 60736)
        m.gm_s = at("gm_s", [NS, D], F32, H0 + 60736)
        m.g2_s = at("g2_s", [NS, D], F32, H0 + 64832)
        m.bb = at("bb", [NE, 3 * D], F32, H0 + 68928)
        m.bb_lo = at("bb_lo", [NE, 3 * D], F32R, H0 + 68928)
        m.Pb = at("Pb", [P, NH, 2 * P], F32, H0 + 68928)
        m.KcT = at("KcT", [P, NS, P], F32, H0 + 68928)
        m.h2 = at("h2", [P, 2, D], F32, H0 + 68928)
        m.PT = at("PT", [P, 2, 512], F32, H0 + 77120)
        m.sT = at("sT", [P, 64], F32, H0 + 77120)
        m.P64 = at("P64", [64, P], F32, H0 + 77376)
        m.PTs = at("PTs", [P, 64], F32, H0 + 77888)
        m.attn = at("attn", [P, NH * HD], F32, H0 + 81216)
        m.sq = at("sq", [P, 640], F32, H0 + 83264)
        m.qn = at("qn", [P, 512], F32, H0 + 85824)
        m.kd = at("kd", [P, NKV, 2, HD], F32, H0 + 87872)
        m.la = at("la", [P, BUF + SEQ], F32, H0 + 83264)
        m.lb = at("lb", [P, BUF + SEQ], F32, H0 + 85376)
        m.dT = at("dT", [P, SEQ], F32, H0 + 87488)
        m.s2_s = at("s2_s", [NS, D], F32, H0 + 83264)
        m.bb_hi = at("bb_hi", [NE, 3 * D], F32R, H0 + 89600)
        m.gm_bc = at("gm_bc", [P, D], F32, H0 + 89600)
        m.g2_bc = at("g2_bc", [P, D], F32, H0 + 93696)
        m.s2_bc = at("s2_bc", [P, D], F32, H0 + 97792)
        m.mrow = at("mrow", [9, D], F32, H0 + 101888)
        m.ulast = at("ulast", [BUF, PW], F32, H0 + 101888)
        m.uslast = at("uslast", [NS, PW], F32, H0 + 103936)
        m.w_router = at("w_router_sb", [P, KC, NE], F32, H0 + 87488)
        m.oh_s = at("oh_s_sb", [NE + 1, P + 1], F32, H0 + 105984)
        m.relb = at("relb", [NE + 1, NH], F32, H0 + 106528)
        m.rel64 = at("rel64", [NE + 1, NS, NH], F32, H0 + 106560)
        m.kn = at("kn", [P, 2, KVW], F32, H0 + 105984)
        m.h2T = at("h2T", [P, KC, P], F32, H0 + 37120)
        m.junk = at("junk", [P, D], F32, H0 + 41216)
        r_at = [H0 + 45440]

        def rt(name, shape, dt=F32):
            t = at(name, shape, dt, r_at[0])
            r_at[0] += (int(np.prod(shape[1:])) * size[dt] + 31) // 32 * 32
            return t

        m.ones_b = rt("ones_b", [P, P], BF16)
        m.tri = rt("tri", [P, P], BF16)
        m.iota_e = rt("iota_e", [P, NE])
        m.tok_no = rt("tok_no", [P, TT], I32)
        m.v8 = rt("v8", [P, TT, 8])
        m.i8 = rt("i8", [P, TT, 8], U32)
        m.idx = rt("idx", [P, TT, TOPK])
        m.ohk = rt("ohk", [P, TOPK, TT * NE])
        m.mask = rt("mask", [P, TT * NE], BF16)
        m.pos = rt("pos", [P, TT * NE])
        m.blk = rt("blk", [P, TT * NE])
        m.flat = rt("flat", [P, TT * NE])
        m.rtmp = rt("rtmp", [P, TT * NE])
        m.cnt = rt("cnt", [P, NE])
        m.nov = rt("nov", [P, NE])
        m.ends = rt("ends", [P, NE])
        m.adj = rt("adj", [P, NE])
        m.zero_e = rt("zero_e", [P, NE])
        m.gates = rt("gates", [P, TT, TOPK])
        m.gsum = rt("gsum", [P, TT])
        m.dest_f = rt("dest_f", [P, TOPK, TT])
        m.dest = rt("dest", [P, TOPK, TT], I32)
        m.pay = rt("pay", [P, TT, TOPK, 2], I32)
        m.ovc = rt("ovc", [1, NOVER + 1, NE])
        m.ovf = rt("ovf", [1, NOVER + 1])
        m.iota_o = rt("iota_o", [1, NOVER + 1])
        assert r_at[0] <= H0 + 60736, r_at[0] - H0

        m.hi = at("hi", [P, HL, 2048], F32R, H0)
        m.lo = at("lo", [P, HL, 2048], F32R, H0 + 4 * SLOT)
        m.xg = at("xg", [P, D], F32, H0 + 65536)
        m.xTh = at("xTh", [P, KC, P], F32R, H0 + 69632)
        m.xTl = at("xTl", [P, KC, P], F32R, H0 + 73728)
        m.aTh = at("aTh", [P, KC, P], F32R, H0 + 77824)
        m.aTl = at("aTl", [P, KC, P], F32R, H0 + 81920)
        m.gate = at("gate", [P, 512], F32, H0 + 86016)
        m.up = at("up", [P, 512], F32, H0 + 88064)
        m.ost = at("ost", [P, D], F32, H0 + 90112)
        m.bhl = at("bhl", [2, 3 * D], F32R, H0 + 94208)
        m.ones2 = at("ones2", [2, P], F32R, H0 + 106496)
        m.col_s = at("col_s", [P, 2], I32, H0 + 107008)
        m.idx_g = at("idx_g", [P, 1], I32, H0 + 107040)
        m.xf = at("xf", [P, TT, D], F32, raw0)
        m.yf = at("yf", [P, TT, D], F32, raw0 + 20480)
        m.gf = at("gf", [P, 2, D], F32, raw0 + 40960)
        assert H0 + 107072 <= nc.sbuf_usable_end

        m.h2d = dram("h2d", [TOK, D], F32)
        m.x1d = dram("x1d", [TOK, D], F32)
        m.yd = dram("yd", [TOK, D], F32)
        m.tabd = dram("tabd", [P, NCOL * 2], I32)
        m.skew = dram("skew", [NH, P * LINE], F32)
        m.modd = dram("modd", [4, 9, D], F32)
        m.bd = dram("bd", [NE, 2, 3 * D], F32R)
        m.raw_in = [sem(f"raw_in{u}") for u in range(UNITS)]
        m.eid_ready = sem("eid_ready")
        head_sems = head(nc, m)
        nc.clear_and_free_semaphores(head_sems)
        nc.all_engine_barrier()
        experts(nc, m)


def head(nc, m):
    i, o, bank, sem = m.i, m.o, m.bank, m.sem
    sems = []

    def signal(name):
        sems.append(nc.alloc_semaphore(name=name))
        return sems[-1]

    s = Record()
    s.vecs_in = signal("vecs_in")
    s.c_in = signal("c_in")
    s.small_in = signal("small_in")
    s.bb_in = signal("bb_in")
    s.win_in = signal("win_in")
    s.wout_in = signal("wout_in")
    s.kv_in = signal("kv_in")
    s.newkv_in = signal("newkv_in")
    s.ident_ready = signal("ident_ready")
    s.zeros_ready = signal("zeros_ready")
    s.zero_out = signal("zero_out")
    s.vecs_tr = signal("vecs_tr")
    s.vecs_ready = signal("vecs_ready")
    s.c_act = signal("c_act")
    s.c_tr = signal("c_tr")
    s.cT_ready = signal("cT_ready")
    s.ssq_ready = signal("ssq_ready")
    s.rms_ready = signal("rms_ready")
    s.rstd_ready = signal("rstd_ready")
    s.xn_ready = signal("xn_ready")
    s.x_tr = signal("x_tr")
    s.xT_act = signal("xT_act")
    s.xT_dve = signal("xT_dve")
    s.ada_used = signal("ada_used")
    s.mod_ready = signal("mod_ready")
    s.g1_ready = signal("g1_ready")
    s.hT_half = signal("hT_half")
    s.h_ready = signal("h_ready")
    s.rel_ready = signal("rel_ready")
    s.line_tr = signal("line_tr")
    s.line_ready = signal("line_ready")
    s.skew_out = signal("skew_out")
    s.bias_in = signal("bias_in")
    s.bias64_tr = signal("bias64_tr")
    s.bias64_ready = signal("bias64_ready")
    s.bb_hi_done = signal("bb_hi_done")
    s.bb_lo_done = signal("bb_lo_done")
    s.bb_out = signal("bb_out")
    s.z_ready = signal("z_ready")
    s.sq_ready = signal("sq_ready")
    s.vt_ready = signal("vt_ready")
    s.hss_ready = signal("hss_ready")
    s.hrms_ready = signal("hrms_ready")
    s.hrs_ready = signal("hrs_ready")
    s.qn_raw = signal("qn_raw")
    s.kn_raw = signal("kn_raw")
    s.qk_ready = signal("qk_ready")
    s.qk_tr = signal("qk_tr")
    s.qT_ready = signal("qT_ready")
    s.kT_ready = signal("kT_ready")
    s.u_ready = signal("u_ready")
    s.U_ready = signal("U_ready")
    s.Us_ready = signal("Us_ready")
    s.pad_ready = signal("pad_ready")
    s.pool_step = signal("pool_step")
    s.pooled = signal("pooled")
    s.sp_tr = signal("sp_tr")
    s.spT_ready = signal("spT_ready")
    s.spool_step = signal("spool_step")
    s.dTs_ready = signal("dTs_ready")
    s.pm_ready = signal("pm_ready")
    s.pm_done = signal("pm_done")
    s.pms_ready = signal("pms_ready")
    s.pms_done = signal("pms_done")
    s.sc_ready = signal("sc_ready")
    s.sc_used = signal("sc_used")
    s.mx_step = signal("mx_step")
    s.sm_ready = signal("sm_ready")
    s.p_ready = signal("p_ready")
    s.e_ready = signal("e_ready")
    s.pt_tr = signal("pt_tr")
    s.pt_ev = signal("pt_ev")
    s.pv_done = signal("pv_done")
    s.o_ready = signal("o_ready")
    s.eps_ready = signal("eps_ready")
    s.attn_ready = signal("attn_ready")
    s.at_tr = signal("at_tr")
    s.at_ev = signal("at_ev")
    s.kc_tr = signal("kc_tr")
    s.kcT_ready = signal("kcT_ready")
    s.qs_ready = signal("qs_ready")
    s.s_sc = signal("s_sc")
    s.s_scT = signal("s_scT")
    s.s_tr = signal("s_tr")
    s.s_soft = signal("s_soft")
    s.s_step = signal("s_step")
    s.s_exp = signal("s_exp")
    s.s_norm = signal("s_norm")
    s.s_ptr = signal("s_ptr")
    s.s_pts = signal("s_pts")
    s.s_pv = signal("s_pv")
    s.s_mix = signal("s_mix")
    s.mr_tr = signal("mr_tr")
    s.mr_ready = signal("mr_ready")
    s.mod_out = signal("mod_out")
    s.bc_in = signal("bc_in")
    s.bcs_in = signal("bcs_in")
    s.wr_in = signal("wr_in")
    s.xo_ready = signal("xo_ready")
    s.x1_step = signal("x1_step")
    s.x1_ready = signal("x1_ready")
    s.ss2_ready = signal("ss2_ready")
    s.rms2_ready = signal("rms2_ready")
    s.rs2_ready = signal("rs2_ready")
    s.h2_ready = signal("h2_ready")
    s.x1_out = signal("x1_out")
    s.h2_tr = signal("h2_tr")
    s.h2T_ready = signal("h2T_ready")
    s.rt_ready = signal("rt_ready")
    s.logit_ready = signal("logit_ready")
    s.r_init = signal("r_init")
    s.top_ready = signal("top_ready")
    s.mask_ready = signal("mask_ready")
    s.cnt_ready = signal("cnt_ready")
    s.pos_ready = signal("pos_ready")
    s.gate_in = signal("gate_in")
    s.gate_exp = signal("gate_exp")
    s.pay_no = signal("pay_no")
    s.tab_init = signal("tab_init")
    s.tab_out = signal("tab_out")
    s.dest_ready = signal("dest_ready")
    s.scattered = signal("scattered")
    s.tab_in = signal("tab_in")
    s.g2_col = signal("g2_col")
    s.new_out = signal("new_out")
    s.ur_tr = signal("ur_tr")
    s.ur_ready = signal("ur_ready")
    s.den_sum = signal("den_sum")
    s.ulast_out = signal("ulast_out")
    x_in = [signal(f"x_in{t}") for t in range(TT)]
    ada_in = [signal(f"ada_in{n}") for n in range(ADA_SLOTS)]
    h2_free = [signal(f"h2_free{n}") for n in range(2)]
    w1, w2 = i["w1"][0], i["w2"][0]
    out_k, out_v, out_u = o["new_k_prompt"][0, 0], o["new_v_prompt"][0, 0], o["new_pool_prompt"][0, 0]
    sk, sv, su = o["new_k_sample"][0], o["new_v_sample"][0], o["new_pool_sample"][0]
    ck, cv = i["cache_k"][0], i["cache_v"][0]
    ADA = 3 * KC

    def tok(t):
        return slice(t * P, t * P + ROWS[t])

    def load_unit(sp, e, u):
        if u < W1_UNITS:
            j = u // 4
            for kk in range(2):
                k = 2 * (u % 4) + kk
                src = w1[ds(e), k * P:(k + 1) * P, :].rearrange("e p (h c) -> p (e h) c", h=2)
                sp.dma_start(m.raw[:, u, kk * D:(kk + 1) * D].rearrange("p (h c) -> p h c", h=2),
                             src[:, :, j * 512:(j + 1) * 512]).then_inc(m.raw_in[u], 16)
        else:
            f = 2 * (u - W1_UNITS)
            src = w2[ds(e), f * P:(f + 2) * P, :].rearrange("e (k p) n -> p (e k) n", k=2)
            sp.dma_start(m.raw[:, u, :].rearrange("p (k n) -> p k n", k=2), src).then_inc(m.raw_in[u], 16)

    m.load_unit = load_unit

    with nc.Block() as block:

        @block.sync
        def _(sp):
            sp.dma_start(m.crow[0:NS, :], i["c_sample"]).then_inc(s.c_in, 16)
            sp.dma_start(m.crow[NS:NS + 1, :], i["c_prompt"]).then_inc(s.c_in, 16)
            for t in range(TP):
                sp.dma_start(m.xs[:, t, :], i["x_prompt"][0, tok(t), :]).then_inc(x_in[t], 16)
            sp.dma_start(m.xs[0:NS, TP, :], i["x_sample"].rearrange("b t d -> (b t) d")).then_inc(x_in[TP], 16)

            def load_ada(n):
                ph, k = n // KC, n % KC
                if n >= ADA_SLOTS:
                    sp.wait_ge(s.ada_used, n - ADA_SLOTS + 1)
                sp.dma_start(m.raw[:, n % ADA_SLOTS, :],
                             i["w_ada"][0, k * P:(k + 1) * P, ph * 2048:(ph + 1) * 2048]
                             ).then_inc(ada_in[n % ADA_SLOTS], 16)

            for n in range(KC):
                load_ada(n)
            sp.dma_start(m.w_in[:], i["w_in"][0].rearrange("(k p) n -> p k n", p=P)).then_inc(s.win_in, 16)
            for n in range(KC, ADA):
                load_ada(n)
            sp.wait_ge(s.ada_used, ADA)
            for u in range(ADA_SLOTS):
                load_unit(sp, 0, u)
            sp.wait_ge(s.z_ready, TT)
            sp.wait_ge(s.u_ready, 5)
            sp.dma_start(m.w_out[:], i["w_out"][0].rearrange("(k p) n -> p k n", p=P)).then_inc(s.wout_in, 16)
            for k in range(4):
                sp.wait_ge(s.mr_ready, 2 * k + 2)
                sp.dma_start(m.modd[k], m.mrow[:]).then_inc(s.mod_out, 16)
            sp.wait_ge(s.mod_out, 64)
            sp.wait_ge(s.bb_out, 32)
            for k, dst in ((0, m.gm_bc), (2, m.g2_bc), (1, m.s2_bc)):
                sp.dma_start(dst[:], m.modd[k, NS:NS + 1, :].to_broadcast([P, D])).then_inc(s.bc_in, 16)
            sp.wait_ge(s.pms_ready, 1)
            sp.wait_ge(s.dTs_ready, 4)
            sp.wait_ge(s.bias64_tr, 1)
            load_unit(sp, 0, 3)
            sp.wait_ge(s.skew_out, 16)
            sp.wait_ge(s.c_tr, 1)
            load_unit(sp, 0, 4)
            load_unit(sp, 0, 5)
            sp.wait_ge(s.s_pv, 1)
            load_unit(sp, 0, 6)
            sp.wait_ge(s.ur_ready, 1)
            sp.dma_start(out_u, m.ulast[:]).then_inc(s.ulast_out, 16)
            sp.dma_start(su[:, BUF - 1], m.uslast[:]).then_inc(s.ulast_out, 16)

            def store_rows(t):
                sp.wait_ge(s.h2_ready, t + 1)
                sp.dma_start(m.h2d[tok(t), :], m.h2[0:ROWS[t], t % 2, :]).then_inc(h2_free[t % 2], 16)
                sp.dma_start(m.x1d[tok(t), :], m.xs[0:ROWS[t], t, :]).then_inc(s.x1_out, 16)

            for t in range(3):
                store_rows(t)
            sp.wait_ge(s.xo_ready, TT)
            for u in range(7, UNITS):
                load_unit(sp, 0, u)
            for t in range(3, TT):
                store_rows(t)
            sp.wait_ge(s.ulast_out, 32)
            sp.wait_ge(s.x1_out, TT * 16)
            sp.wait_ge(h2_free[0], 3 * 16)
            sp.wait_ge(h2_free[1], 2 * 16)

        @block.gpsimd
        def _(gp):
            gp.memset(m.ident[:], 0.0).then_inc(s.pad_ready, 1)
            gp.wait_ge(s.pad_ready, 1)
            gp.affine_select(out=m.ident[:], in_=m.ident[:], compare_op=ALU.not_equal, fill=1.0, base=0,
                             pattern=[[-1, P]], channel_multiplier=1).then_inc(s.ident_ready, 1)
            gp.wait_ge(s.ident_ready, 1)
            gp.memset(m.relb[NE:NE + 1, :], 1.0).then_inc(s.pad_ready, 1)
            for dst, src in ((m.relb[0:NE, :], i["rel_bias"]),
                             (m.rel64[0:NE], i["rel_bias"].unsqueeze(1).to_broadcast([NE, NS, NH])),
                             (m.rel64[NE:NE + 1], i["sinks"].unsqueeze(1).to_broadcast([1, NS, NH])),
                             (m.oh_line[:], i["oh_line"]), (m.oh_s[:], i["oh_s"]),
                             (m.sinks_bc[:], i["sinks"].to_broadcast([P, NH])),
                             (m.qn_bc[:], i["q_norm"].to_broadcast([P, HD])),
                             (m.kn_bc[:], i["k_norm"].to_broadcast([P, HD])),
                             (m.br_bc[:], i["b_router"].to_broadcast([P, NE])),
                             (m.rec[:].rearrange("p g c -> p (g c)"),
                              i["rec"].rearrange("g c -> (g c)").unsqueeze(0).to_broadcast([P, 4 * (BUF + 1)])),
                             (m.w_pool[:], i["w_pool"][0].rearrange("g k n -> k g n")),
                             (m.sp[:], i["state_pool"][0].rearrange("b t c -> (b t) c"))):
                gp.dma_start(dst, src).then_inc(s.small_in, 16)
            gp.dma_start(m.bb[:, 0:2 * D], i["b1"][0]).then_inc(s.bb_in, 16)
            gp.dma_start(m.bb[:, 2 * D:3 * D], i["b2"][0]).then_inc(s.bb_in, 16)
            gp.wait_ge(s.pad_ready, 2)
            gp.memset(m.U[:, :, 0:BUF], 0.0).then_inc(s.pad_ready, 1)
            gp.wait_ge(s.pad_ready, 3)
            gp.memset(m.zero[:], 0.0).then_inc(s.zeros_ready, 1)
            gp.wait_ge(s.zeros_ready, 1)
            gp.memset(m.tab[:, :, 0], OOB).then_inc(s.tab_init, 1)
            gp.wait_ge(s.tab_init, 1)
            gp.memset(m.tab[:, :, 1], 0).then_inc(s.tab_init, 1)
            gp.wait_ge(s.tab_init, 2)
            gp.dma_start(m.tabd, m.tab[:].rearrange("p c w -> p (c w)")).then_inc(s.tab_out, 16)
            gp.wait_ge(s.zeros_ready, 1)
            for t in range(TT):
                gp.dma_start(m.yd[tok(t), :], m.zero[0:ROWS[t], :]).then_inc(s.zero_out, 16)
            gp.dma_start(sk[:, 0:P - 1], ck[:, 1:P]).then_inc(s.new_out, 16)
            gp.dma_start(sv[:, 0:P - 1], cv[:, 1:P]).then_inc(s.new_out, 16)
            gp.dma_start(su[:, 0:BUF - 1], i["state_pool"][0, :, 1:BUF]).then_inc(s.new_out, 16)
            gp.wait_ge(s.line_ready, NH)
            gp.dma_start(m.skew.rearrange("h (p n) -> p h n", n=LINE), m.line[:]).then_inc(s.skew_out, 16)
            gp.dma_start(m.Kc[:], ck.rearrange("b j g d -> j b (g d)")).then_inc(s.kv_in, 16)
            gp.dma_start(m.Vc[:], cv.rearrange("b j g d -> j b (g d)")).then_inc(s.kv_in, 16)
            gp.wait_ge(s.skew_out, 16)
            gp.wait_ge(s.x_tr, 2 * TT)
            for h in range(NH):
                src = m.skew[h, P - 1:P - 1 + P * (LINE - 1)].rearrange("(p n) -> p n", n=LINE - 1)
                gp.dma_start(m.bias[:, h, :], src[:, 0:2 * P]).then_inc(s.bias_in, 16)
            gp.wait_ge(s.bb_lo_done, 1)
            gp.dma_start(m.bd[:, 0, :], m.bb_hi[:]).then_inc(s.bb_out, 16)
            gp.dma_start(m.bd[:, 1, :], m.bb_lo[:]).then_inc(s.bb_out, 16)
            gp.wait_ge(s.kv_in, 32)
            gp.wait_ge(s.qk_ready, TT)
            gp.wait_ge(s.vt_ready, TT)
            gp.dma_start(m.Kc[0:1, :, :], m.kn[0:NS, 1, :]).then_inc(s.newkv_in, 16)
            gp.dma_start(m.Vc[0:1, :, :], m.vt[0:NS, TP, :]).then_inc(s.newkv_in, 16)
            gp.dma_start(sk[:, P - 1].rearrange("b g d -> b (g d)"), m.kn[0:NS, 1, :]).then_inc(s.new_out, 16)
            gp.dma_start(sv[:, P - 1].rearrange("b g d -> b (g d)"), m.vt[0:NS, TP, :]).then_inc(s.new_out, 16)
            gp.dma_start(out_k.rearrange("t g d -> t (g d)"), m.kn[:, 0, :]).then_inc(s.new_out, 16)
            gp.dma_start(out_v.rearrange("t g d -> t (g d)"), m.vt[:, TP - 1, :]).then_inc(s.new_out, 16)
            gp.wait_ge(s.qk_tr, TT)
            gp.wait_ge(s.small_in, 12 * 16)
            n = 0
            for g, w in enumerate(WINDOWS):
                gp.wait_ge(s.U_ready, g + 1)
                src = m.U[:, g, :]
                step, k = 1, 0
                while step < w:
                    dst = (m.la, m.lb)[k % 2]
                    lo_ = 2 * step - 1
                    if n:
                        gp.wait_ge(s.pool_step, n)
                    if g:
                        gp.wait_ge(s.pooled, g)
                    gp.tensor_tensor(dst[:, lo_:], src[:, lo_:], src[:, lo_ - step:BUF + SEQ - step],
                                     ALU.add).then_inc(s.pool_step, 1)
                    n += 1
                    src, step, k = dst, 2 * step, k + 1
                gp.wait_ge(s.pool_step, n)
                gp.tensor_scalar(src[:, 2 * BUF + 1:], src[:, 2 * BUF + 1:], 1.0 / w, None,
                                 ALU.mult).then_inc(s.pool_step, 1)
                gp.wait_ge(s.pool_step, n + 1)
                gp.tensor_tensor(src[:, BUF:2 * BUF + 1], src[:, BUF:2 * BUF + 1], m.rec[:, g, :],
                                 ALU.mult).then_inc(s.pool_step, 1)
                n += 2
                gp.wait_ge(s.pool_step, n)
                if g:
                    gp.wait_ge(s.pm_ready, g)
                gp.tensor_tensor(m.dT[:], src[:, BUF:], m.U[:, g, BUF:], ALU.subtract).then_inc(s.pooled, 1)
            gp.wait_ge(s.pooled, 4)
            gp.wait_ge(s.ur_tr, 1)
            gp.wait_ge(s.new_out, 7 * 16)
            gp.memset(m.ones_b[:], 1.0).then_inc(s.r_init, 1)
            gp.wait_ge(s.r_init, 1)
            gp.memset(m.tri[:], 1.0).then_inc(s.r_init, 1)
            gp.wait_ge(s.r_init, 2)
            gp.affine_select(out=m.tri[:], in_=m.tri[:], compare_op=ALU.is_gt, fill=0.0, base=0,
                             pattern=[[1, P]], channel_multiplier=-1).then_inc(s.r_init, 1)
            gp.wait_ge(s.r_init, 3)
            gp.iota(m.iota_e[:], pattern=[[1, NE]], base=0, channel_multiplier=0,
                    allow_small_or_imprecise_dtypes=True).then_inc(s.r_init, 1)
            gp.wait_ge(s.r_init, 4)
            gp.iota(m.tok_no[:], pattern=[[P, TT]], base=0, channel_multiplier=1).then_inc(s.r_init, 1)
            gp.wait_ge(s.r_init, 5)
            gp.iota(m.iota_o[:], pattern=[[1, NOVER + 1]], base=0, channel_multiplier=0,
                    allow_small_or_imprecise_dtypes=True).then_inc(s.r_init, 1)
            gp.wait_ge(s.r_init, 6)
            gp.iota(m.eid[:], pattern=[[1, NCOL + 1]], base=-1, channel_multiplier=0).then_inc(s.r_init, 1)
            gp.wait_ge(s.r_init, 7)
            gp.memset(m.idx[:], 99.0).then_inc(s.r_init, 1)
            gp.wait_ge(s.r_init, 8)
            gp.memset(m.v8[:], 0.0).then_inc(s.r_init, 1)
            gp.wait_ge(s.r_init, 9)
            gp.memset(m.zero_e[:], 0.0).then_inc(s.r_init, 1)
            gp.wait_ge(s.mod_out, 4 * 16)
            gp.wait_ge(s.sc_used, 4 * TP)
            gp.wait_ge(s.pm_ready, 4)
            for v, dst in ((0, m.gm_s), (2, m.g2_s), (1, m.s2_s)):
                gp.dma_start(dst[:], m.modd[v, 0:NS, :]).then_inc(s.bcs_in, 16)
            gp.dma_start(m.w_router[:], i["w_router"][0].rearrange("(k p) n -> p k n", p=P)).then_inc(s.wr_in, 16)
            gp.wait_ge(s.tab_out, 16)
            gp.wait_ge(s.dest_ready, 1)
            gp.wait_ge(s.pay_no, 2)
            places = m.tabd.rearrange("p (c w) -> (p c) w", w=2)
            for k in range(TOPK):
                for t in range(TT):
                    gp.indirect_dma_start(places, bass.IndirectOffsetOnAxis(ap=m.dest[0:ROWS[t], k, t:t + 1], axis=0),
                                          m.pay[0:ROWS[t], t, k, :], None).then_inc(s.scattered, 16)
            gp.wait_ge(s.scattered, TT * TOPK * 16)
            gp.dma_start(m.tab[:].rearrange("p c w -> p (c w)"), m.tabd).then_inc(s.tab_in, 16)
            gp.wait_ge(s.tab_in, 16)
            gp.wait_ge(s.zero_out, TT * 16)
            gp.wait_ge(s.bb_out, 32)

        @block.scalar
        def _(act):
            act.dma_start(m.vrow[0:48, :], i["b_ada"][0].rearrange("(a b) -> a b", b=P)).then_inc(s.vecs_in, 16)
            for r, name, n in ((48, "norm_mix", 8), (56, "norm_ffn", 8), (64, "pool_scale", 4)):
                act.dma_start(m.vrow[r:r + n, :], i[name][0].rearrange("(a b) -> a b", b=P)).then_inc(s.vecs_in, 16)
            act.wait_ge(s.c_in, 32)
            nc.scalar.activation(m.crow[:], m.crow[:], ACT.Silu).then_inc(s.c_act, 1)

            def norm_x(t):
                R = ROWS[t]
                act.wait_ge(x_in[t], 16)
                if t >= 2:
                    act.wait_ge(s.x_tr, 2 * t - 2)
                if t:
                    act.wait_ge(s.xn_ready, t)
                nc.scalar.activation(m.xn[0:R, t % 2, :], m.xs[0:R, t, :], ACT.Square,
                                     accum_out=m.ssq[0:R, t:t + 1]).then_inc(s.ssq_ready, 1)
                act.wait_ge(s.ssq_ready, t + 1)
                act.wait_ge(s.eps_ready, 1)
                nc.scalar.activation(m.rstd[0:R, t:t + 1], m.ssq[0:R, t:t + 1], ACT.Sqrt, scale=1.0 / D,
                                     bias=m.eps[0:R, :]).then_inc(s.rms_ready, 1)
                act.wait_ge(s.rstd_ready, t + 1)
                nc.scalar.activation(m.xn[0:R, t % 2, :], m.xs[0:R, t, :], ACT.Copy,
                                     scale=m.rstd[0:R, t:t + 1]).then_inc(s.xn_ready, 1)

            def take_x(t):
                act.wait_ge(s.x_tr, 2 * t + 1)
                R = ROWS[t]
                nc.scalar.copy(m.hT[:, 0:4, tok(t)],
                               bank[0][:].rearrange("p (k n) -> p k n", k=4)[:, :, 0:R]).then_inc(s.xT_act, 1)

            for t in range(TT):
                norm_x(t)
                if t:
                    take_x(t - 1)
            take_x(TP)
            act.wait_ge(s.bb_in, 32)
            nc.scalar.copy(m.bb_hi[:], m.bb[:]).then_inc(s.bb_hi_done, 1)
            def take_qT(t):
                act.wait_ge(s.qk_tr, t + 1)
                if not t:
                    act.wait_ge(s.zero_out, TT * 16)
                nc.scalar.copy(m.qT[:, :, tok(t)],
                               bank[0][:].rearrange("p (k n) -> p k n", k=4)[:, :, 0:ROWS[t]]).then_inc(s.qT_ready, 1)

            for t in range(TT):
                R, zq, zk = ROWS[t], bank[4 + 2 * (t % 2)], bank[5 + 2 * (t % 2)]
                act.wait_ge(s.z_ready, t + 1)
                if t:
                    act.wait_ge(s.hss_ready, t)
                nc.scalar.activation(m.sq[0:R, 0:512], zq[0:R, :], ACT.Square).then_inc(s.sq_ready, 1)
                nc.scalar.activation(m.sq[0:R, 512:640], zk[0:R, 0:KVW], ACT.Square).then_inc(s.sq_ready, 1)
                nc.scalar.copy(m.vt[0:R, t, :], zk[0:R, KVW:2 * KVW]).then_inc(s.vt_ready, 1)
                act.wait_ge(s.hss_ready, t + 1)
                if t:
                    act.wait_ge(s.qk_ready, t)
                nc.scalar.activation(m.hrs[0:R, :], m.hss[0:R, :], ACT.Sqrt, scale=1.0 / HD,
                                     bias=m.eps[0:R, :]).then_inc(s.hrms_ready, 1)
                if t:
                    take_qT(t - 1)
            take_qT(TP)
            for g in range(4):
                act.wait_ge(s.u_ready, g + 1)
                if not g:
                    act.wait_ge(s.pad_ready, 3)
                nc.scalar.copy(m.U[:, g, BUF:], bank[4 + g][:]).then_inc(s.U_ready, 1)

            def exps(t):
                act.wait_ge(s.sm_ready, t + 1)
                if t:
                    act.wait_ge(s.o_ready, t)
                c0 = 0 if t else P
                for h in range(NH):
                    e = nc.scalar.activation(m.Pb[:, h, c0:], m.Pb[:, h, c0:], ACT.Exp, bias=m.negm[:, h:h + 1],
                                             accum_out=m.den[:, h:h + 1])
                    if h % 2:
                        e.then_inc(s.p_ready, 1)
                nc.scalar.activation(m.esink[:], m.esink[:], ACT.Exp).then_inc(s.e_ready, 1)

            def take_PT(t):
                for j in range(4):
                    act.wait_ge(s.pt_tr, 4 * t + j + 1)
                    if 4 * t + j >= 2:
                        act.wait_ge(s.pv_done, 4 * t + j - 1)
                    if t:
                        nc.scalar.copy(m.PT[:, j % 2, :], bank[j % 2][:]).then_inc(s.pt_ev, 1)
                    else:
                        nc.scalar.copy(m.PT[:, j % 2, :].rearrange("p (a b n) -> p a b n", a=2, b=2)[:, :, 1, :],
                                       bank[j % 2][:].rearrange("p (a b n) -> p a b n", a=2, b=2)[:, :, 1, :]
                                       ).then_inc(s.pt_ev, 1)

            def take_attn(t):
                act.wait_ge(s.at_tr, t + 1)
                nc.scalar.copy(m.mixT[:, 0:4, tok(t)],
                               bank[2][:].rearrange("p (k n) -> p k n", k=4)).then_inc(s.at_ev, 1)

            for t in range(TP):
                exps(t)
                if t:
                    take_attn(t - 1)
                take_PT(t)
            take_attn(TP - 1)
            act.wait_ge(s.s_step, 2)
            nc.scalar.activation(m.P64[:], m.P64[:], ACT.Exp, bias=m.s64[:, 1:2],
                                 accum_out=m.s64[:, 2:3]).then_inc(s.s_exp, 1)
            act.wait_ge(s.s_step, 3)
            nc.scalar.activation(m.s64[:, 3:4], m.s64[:, 3:4], ACT.Exp).then_inc(s.s_exp, 1)
            for g in range(4):
                act.wait_ge(s.pm_ready, g + 1)
                nc.scalar.activation(m.mixT[:, 4 + g, 0:SEQ], bank[3][:], ACT.Copy,
                                     scale=m.vecsT[:, 64 + g:65 + g]).then_inc(s.pm_done, 1)
            act.wait_ge(s.pms_ready, 1)
            for g in range(4):
                nc.scalar.activation(m.mixT[:, 4 + g, SEQ:TOK], bank[2][:, g * NS:(g + 1) * NS], ACT.Copy,
                                     scale=m.vecsT[:, 64 + g:65 + g]).then_inc(s.pms_done, 1)

            def squares(t):
                R = ROWS[t]
                act.wait_ge(s.x1_ready, t + 1)
                if t:
                    act.wait_ge(s.ss2_ready, t)
                nc.scalar.activation(m.junk[0:R, :], m.xs[0:R, t, :], ACT.Square,
                                     accum_out=m.ss2[0:R, t:t + 1]).then_inc(s.ss2_ready, 1)
                act.wait_ge(s.ss2_ready, t + 1)
                nc.scalar.activation(m.rs2[0:R, t:t + 1], m.ss2[0:R, t:t + 1], ACT.Sqrt, scale=1.0 / D,
                                     bias=m.eps[0:R, :]).then_inc(s.rms2_ready, 1)

            def take_h2T(t):
                for half in range(2):
                    act.wait_ge(s.h2_tr, 2 * t + half + 1)
                    if t and not half:
                        act.wait_ge(s.rt_ready, t)
                    nc.scalar.copy(m.h2T[:, 4 * half:4 * half + 4, 0:ROWS[t]],
                                   bank[half][:].rearrange("p (k n) -> p k n", k=4)[:, :, 0:ROWS[t]]
                                   ).then_inc(s.h2T_ready, 1)

            for t in range(TT):
                squares(t)
                if t:
                    take_h2T(t - 1)
            take_h2T(TP)
            act.wait_ge(s.gate_in, 1)
            nc.scalar.activation(m.gates[:], m.gates[:], ACT.Exp).then_inc(s.gate_exp, 1)

        @block.vector
        def _(v):
            v.memset(m.eps[:], EPS).then_inc(s.eps_ready, 1)
            v.wait_ge(s.vecs_tr, 1)
            v.tensor_copy(m.vecsT[:], bank[7][:, 0:68]).then_inc(s.vecs_ready, 1)
            v.wait_ge(s.c_tr, 1)
            v.tensor_copy(m.cT[:].rearrange("p k n -> p (k n)"), bank[6][:, 0:72]).then_inc(s.cT_ready, 1)
            for t in range(TT):
                R = ROWS[t]
                v.wait_ge(s.rms_ready, t + 1)
                v.reciprocal(m.rstd[0:R, t:t + 1], m.rstd[0:R, t:t + 1]).then_inc(s.rstd_ready, 1)
                if t:
                    v.wait_ge(s.x_tr, 2 * t)
                    v.tensor_copy(m.hT[:, 4:8, tok(t - 1)],
                                  bank[1][:].rearrange("p (k n) -> p k n", k=4)).then_inc(s.xT_dve, 1)
            v.wait_ge(s.x_tr, 2 * TT)
            v.tensor_copy(m.hT[:, 4:8, tok(TP)],
                          bank[1][:].rearrange("p (k n) -> p k n", k=4)[:, :, 0:NS]).then_inc(s.xT_dve, 1)
            v.wait_ge(s.small_in, 12 * 16)
            v.wait_ge(s.pad_ready, 2)
            v.tensor_copy(m.relrep[:], m.relb[:].unsqueeze(2).to_broadcast([NE + 1, NH, P])).then_inc(s.rel_ready, 1)
            for h in range(NH):
                v.wait_ge(s.line_tr, h + 1)
                if not h:
                    v.wait_ge(s.c_tr, 1)
                v.tensor_copy(m.line[:, h, :], bank[4 + h % 2][:, 0:LINE]).then_inc(s.line_ready, 1)
            v.wait_ge(s.bias64_tr, 1)
            v.tensor_copy(m.bias64[:], bank[6][0:64, 0:P + 1]).then_inc(s.bias64_ready, 1)
            def take_mod(ph):
                v.wait_ge(s.ada_used, KC * (ph + 1))
                v.tensor_tensor(m.modT[:, 16 * ph:16 * ph + 16, :],
                                bank[2 + ph % 2][:, 0:144].rearrange("p (c n) -> p c n", n=9),
                                m.vecsT[:, 16 * ph:16 * ph + 16].unsqueeze(2).to_broadcast([P, 16, 9]),
                                ALU.add).then_inc(s.mod_ready, 1)

            v.wait_ge(s.vecs_ready, 1)
            take_mod(0)
            v.wait_ge(s.mod_ready, 1)
            v.scalar_tensor_tensor(m.g1T[:], m.modT[:, 8:16, :], 1.0,
                                   m.vecsT[:, 48:56].unsqueeze(2).to_broadcast([P, 8, 9]),
                                   ALU.add, ALU.mult).then_inc(s.g1_ready, 1)
            v.wait_ge(s.g1_ready, 1)
            v.wait_ge(s.xT_act, TT)
            v.wait_ge(s.xT_dve, TT)
            v.tensor_tensor(m.hT[:, :, SEQ:TOK], m.hT[:, :, SEQ:TOK], m.g1T[:, :, 0:NS],
                            ALU.mult).then_inc(s.hT_half, 1)
            for k in range(KC):
                v.tensor_scalar(m.hT[:, k, 0:SEQ], m.hT[:, k, 0:SEQ], m.g1T[:, k, 8:9], m.modT[:, k, 8:9],
                                ALU.mult, ALU.add).then_inc(s.h_ready, 1)
            v.wait_ge(s.hT_half, 1)
            v.tensor_tensor(m.hT[:, :, SEQ:TOK], m.hT[:, :, SEQ:TOK], m.modT[:, 0:8, 0:NS],
                            ALU.add).then_inc(s.h_ready, 1)
            v.wait_ge(s.bb_hi_done, 1)
            v.tensor_tensor(m.bb_lo[:], m.bb[:], m.bb_hi[:].bitcast(F32), ALU.subtract).then_inc(s.bb_lo_done, 1)
            take_mod(1)

            def take_kT(t):
                v.wait_ge(s.qk_tr, t + 1)
                v.tensor_copy(m.kT[:, :, tok(t)], bank[1][:, 0:2 * P].rearrange("p (k n) -> p k n", k=2)
                              [:, :, 0:ROWS[t]]).then_inc(s.kT_ready, 1)

            for t in range(TT):
                R, zq, zk = ROWS[t], bank[4 + 2 * (t % 2)], bank[5 + 2 * (t % 2)]
                v.wait_ge(s.sq_ready, 2 * t + 2)
                if t:
                    v.wait_ge(s.hrs_ready, t)
                v.tensor_reduce(m.hss[0:R, :], m.sq[0:R, :].rearrange("p (h d) -> p h d", d=HD), AX_X,
                                ALU.add).then_inc(s.hss_ready, 1)
                v.wait_ge(s.hrms_ready, t + 1)
                v.reciprocal(m.hrs[0:R, :], m.hrs[0:R, :]).then_inc(s.hrs_ready, 1)
                v.wait_ge(s.hrs_ready, t + 1)
                if t:
                    v.wait_ge(s.qk_tr, t)
                v.tensor_tensor(m.qn[0:R, :].rearrange("p (h d) -> p h d", d=HD),
                                zq[0:R, :].rearrange("p (h d) -> p h d", d=HD),
                                m.hrs[0:R, 0:NH].unsqueeze(2).to_broadcast([R, NH, HD]), ALU.mult).then_inc(s.qn_raw, 1)
                keys = m.kn[0:R, t // TP, :].rearrange("p (g d) -> p g d", d=HD)
                v.tensor_tensor(keys, zk[0:R, 0:KVW].rearrange("p (g d) -> p g d", d=HD),
                                m.hrs[0:R, NH:].unsqueeze(2).to_broadcast([R, NKV, HD]), ALU.mult).then_inc(s.kn_raw, 1)
                v.wait_ge(s.qn_raw, t + 1)
                v.tensor_tensor(m.qn[0:R, :].rearrange("p (h d) -> p h d", d=HD),
                                m.qn[0:R, :].rearrange("p (h d) -> p h d", d=HD),
                                m.qn_bc[0:R, :].unsqueeze(1).to_broadcast([R, NH, HD]), ALU.mult)
                v.wait_ge(s.kn_raw, 2 * t + 1)
                v.tensor_tensor(keys, keys, m.kn_bc[0:R, :].unsqueeze(1).to_broadcast([R, NKV, HD]),
                                ALU.mult).then_inc(s.kn_raw, 1)
                v.wait_ge(s.kn_raw, 2 * t + 2)
                v.tensor_copy(m.kd[0:R, :, 0, :], keys)
                v.tensor_copy(m.kd[0:R, :, 1, :], keys).then_inc(s.qk_ready, 1)
                if t:
                    take_kT(t - 1)
            take_kT(TP)
            v.wait_ge(s.u_ready, 5)
            v.tensor_copy(m.Us[:].rearrange("p g n -> p (g n)"), bank[3][:, 0:4 * NS]).then_inc(s.Us_ready, 1)
            v.wait_ge(s.sp_tr, 1)
            v.tensor_copy(m.spT[:].rearrange("p g b t -> p g (b t)"),
                          bank[0][:, 0:480].rearrange("p (g n) -> p g n", g=4)).then_inc(s.spT_ready, 1)
            v.wait_ge(s.spT_ready, 1)
            for g, w in enumerate(WINDOWS):
                v.tensor_reduce(m.dTs[:, g, :], m.spT[:, g, :, BUF + 1 - w:], AX_X, ALU.add).then_inc(s.spool_step, 1)
            v.wait_ge(s.spool_step, 4)
            v.wait_ge(s.Us_ready, 1)
            v.tensor_tensor(m.dTs[:], m.dTs[:], m.Us[:], ALU.add).then_inc(s.spool_step, 1)
            v.wait_ge(s.spool_step, 5)
            for g, w in enumerate(WINDOWS):
                v.scalar_tensor_tensor(m.dTs[:, g, :], m.dTs[:, g, :], 1.0 / w, m.Us[:, g, :], ALU.mult,
                                       ALU.subtract).then_inc(s.dTs_ready, 1)
            take_mod(2)
            v.wait_ge(s.mod_ready, 3)
            v.scalar_tensor_tensor(m.modT[:, 32:40, :], m.modT[:, 32:40, :], 1.0,
                                   m.vecsT[:, 56:64].unsqueeze(2).to_broadcast([P, 8, 9]),
                                   ALU.add, ALU.mult).then_inc(s.g2_col, 1)

            def scores(t):
                c0 = 0 if t else P
                if not t:
                    v.wait_ge(s.bias_in, NH * 16)
                    v.wait_ge(s.bb_out, 32)
                for j in range(4):
                    v.wait_ge(s.sc_ready, 4 * t + j + 1)
                    g, odd = j // 2, j % 2
                    heads = slice(4 * g + odd, 4 * g + odd + 3, 2)
                    if t:
                        v.wait_ge(s.pt_tr, 4 * (t - 1) + 2 * g + 2)
                    v.scalar_tensor_tensor(m.Pb[:, heads, c0:],
                                           bank[4 + j][:].rearrange("p (a n) -> p a n", a=2)[:, :, c0:],
                                           HD ** -0.5, m.bias[:, heads, c0:], ALU.mult,
                                           ALU.add).then_inc(s.sc_used, 1)

            def maxima(t):
                c0 = 0 if t else P
                v.wait_ge(s.sc_used, 4 * t + 4)
                v.tensor_reduce(m.m8[:], m.Pb[:, :, c0:], AX_X, ALU.max).then_inc(s.mx_step, 1)
                v.wait_ge(s.mx_step, 2 * t + 1)
                v.tensor_tensor(m.m8[:], m.m8[:], m.sinks_bc[:], ALU.max).then_inc(s.mx_step, 1)
                v.wait_ge(s.mx_step, 2 * t + 2)
                v.tensor_scalar(m.negm[:], m.m8[:], -1.0, None, ALU.mult)
                v.tensor_tensor(m.esink[:], m.sinks_bc[:], m.m8[:], ALU.subtract).then_inc(s.sm_ready, 1)

            rd = [0]

            def normed(t):
                v.wait_ge(s.e_ready, t + 1)
                v.tensor_tensor(m.den[:], m.den[:], m.esink[:], ALU.add).then_inc(s.den_sum, 1)
                v.wait_ge(s.den_sum, t + 1)
                if t:
                    v.wait_ge(s.attn_ready, t)
                v.reciprocal(m.rden[:], m.den[:]).then_inc(s.o_ready, 1)
                v.wait_ge(s.o_ready, t + 1)
                v.wait_ge(s.pv_done, 4 * t + 4)
                if t:
                    v.wait_ge(s.at_tr, t)
                v.tensor_tensor(m.attn[:].rearrange("p (h d) -> p h d", d=HD),
                                bank[3][:].rearrange("p (h d) -> p h d", d=HD),
                                m.rden[:].unsqueeze(2).to_broadcast([P, NH, HD]), ALU.mult).then_inc(s.attn_ready, 1)

            scores(0)
            maxima(0)
            for t in range(1, TP):
                scores(t)
                normed(t - 1)
                maxima(t)
            normed(TP - 1)
            for k in range(4):
                for half in range(2):
                    v.wait_ge(s.mr_tr, 2 * k + half + 1)
                    if k and not half:
                        v.wait_ge(s.mod_out, 16 * k)
                    v.tensor_copy(m.mrow[:, half * 512:half * 512 + 512], bank[half][0:9, :]).then_inc(s.mr_ready, 1)
            for half in range(2):
                v.wait_ge(s.kc_tr, half + 1)
                v.tensor_copy(m.KcT[:, 4 * half:4 * half + 4, :].rearrange("p k n -> p (k n)"),
                              bank[4 + half][:]).then_inc(s.kcT_ready, 1)
            v.wait_ge(s.qT_ready, TT)
            for g in range(NKV):
                for q in range(GROUP):
                    src = 64 * (q % 2)
                    v.tensor_copy(m.qsT[64 * g:64 * g + 64, g, :, q],
                                  m.qT[src:src + 64, 2 * g + q // 2, SEQ:TOK]).then_inc(s.qs_ready, 1)
            v.wait_ge(s.s_sc, 1)
            for g in range(NKV):
                v.tensor_copy(m.sT[:].rearrange("p (b g q) -> p g b q", g=NKV, q=GROUP)[:, g],
                              bank[6 + g][:, 0:64].rearrange("p (b g q) -> p g b q", g=NKV, q=GROUP)[:, g]
                              ).then_inc(s.s_scT, 1)
            v.wait_ge(s.s_tr, 1)
            v.wait_ge(s.bias64_ready, 1)
            v.scalar_tensor_tensor(m.P64[:], bank[7][0:64, 0:P], HD ** -0.5, m.bias64[:, 0:P], ALU.mult,
                                   ALU.add).then_inc(s.s_soft, 1)
            v.wait_ge(s.s_soft, 1)
            v.tensor_reduce(m.s64[:, 0:1], m.P64[:], AX_X, ALU.max).then_inc(s.s_soft, 1)
            v.wait_ge(s.s_soft, 2)
            v.tensor_tensor(m.s64[:, 0:1], m.s64[:, 0:1], m.bias64[:, P:P + 1], ALU.max).then_inc(s.s_step, 1)
            v.wait_ge(s.s_step, 1)
            v.tensor_scalar(m.s64[:, 1:2], m.s64[:, 0:1], -1.0, None, ALU.mult).then_inc(s.s_step, 1)
            v.tensor_tensor(m.s64[:, 3:4], m.bias64[:, P:P + 1], m.s64[:, 0:1], ALU.subtract).then_inc(s.s_step, 1)
            v.wait_ge(s.s_exp, 2)
            v.tensor_tensor(m.s64[:, 2:3], m.s64[:, 2:3], m.s64[:, 3:4], ALU.add).then_inc(s.s_soft, 1)
            v.wait_ge(s.s_soft, 3)
            v.reciprocal(m.s64[:, 4:5], m.s64[:, 2:3]).then_inc(s.s_soft, 1)
            v.wait_ge(s.s_soft, 4)
            v.tensor_scalar(m.P64[:], m.P64[:], m.s64[:, 4:5], None, ALU.mult).then_inc(s.s_norm, 1)
            v.wait_ge(s.s_ptr, 1)
            v.tensor_copy(m.PTs[:], bank[6][:, 0:64]).then_inc(s.s_pts, 1)
            v.wait_ge(s.s_pv, 1)
            for half in range(2):
                v.tensor_copy(m.mixT[64 * half:64 * half + 64, 0:4, SEQ:TOK],
                              bank[7][0:64, 0:64].rearrange("p (b c a) -> p c b a", b=NS, a=2)[:, :, :, half]
                              ).then_inc(s.s_mix, 1)
            v.wait_ge(s.ur_tr, 1)
            v.wait_ge(s.mod_out, 64)
            v.tensor_copy(m.ulast[:], bank[0][0:BUF, :])
            v.tensor_copy(m.uslast[:], bank[1][0:NS, :]).then_inc(s.ur_ready, 1)
            sx = [0]

            def step(ins):
                ins.then_inc(s.x1_step, 1)
                sx[0] += 1
                v.wait_ge(s.x1_step, sx[0])

            def route(t):
                R = ROWS[t]
                v.wait_ge(s.rt_ready, t + 1)
                v.tensor_tensor(m.logits[0:R, t, :], bank[2][0:R, 0:NE], m.br_bc[0:R, :],
                                ALU.add).then_inc(s.logit_ready, 1)
                v.wait_ge(s.logit_ready, t + 1)
                step(v.max(m.v8[0:R, t, :], m.logits[0:R, t, :]))
                step(v.max_index(m.i8[0:R, t, :], m.v8[0:R, t, :], m.logits[0:R, t, :]))
                v.tensor_copy(m.idx[0:R, t, :], m.i8[0:R, t, 0:TOPK]).then_inc(s.top_ready, 1)

            for t in range(TT):
                R = ROWS[t]
                gm, g2, s2 = (m.gm_bc, m.g2_bc, m.s2_bc) if t < TP else (m.gm_s, m.g2_s, m.s2_s)
                v.wait_ge(s.xo_ready, t + 1)
                if t in (0, TP):
                    v.wait_ge(s.bc_in if not t else s.bcs_in, 3 * 16)
                if t >= 2:
                    v.wait_ge(s.h2_tr, 2 * (t - 1))
                    v.wait_ge(h2_free[t % 2], 16 * (t // 2))
                if not t:
                    v.wait_ge(s.r_init, 10)
                for half in range(2):
                    cs = slice(512 * half, 512 * half + 512)
                    step(v.tensor_tensor(m.h2[0:R, t % 2, cs], bank[4 + 2 * (t % 2) + half][0:R, :], gm[0:R, cs],
                                         ALU.mult))
                v.tensor_tensor(m.xs[0:R, t, :], m.xs[0:R, t, :], m.h2[0:R, t % 2, :], ALU.add).then_inc(s.x1_ready, 1)
                v.wait_ge(s.rms2_ready, t + 1)
                v.reciprocal(m.rs2[0:R, t:t + 1], m.rs2[0:R, t:t + 1]).then_inc(s.rs2_ready, 1)
                v.wait_ge(s.rs2_ready, t + 1)
                step(v.scalar_tensor_tensor(m.h2[0:R, t % 2, :], m.xs[0:R, t, :], m.rs2[0:R, t:t + 1], g2[0:R, :],
                                            ALU.mult, ALU.mult))
                v.tensor_tensor(m.h2[0:R, t % 2, :], m.h2[0:R, t % 2, :], s2[0:R, :], ALU.add).then_inc(s.h2_ready, 1)
                if t:
                    route(t - 1)
            route(TP)
            v.wait_ge(s.top_ready, TT)
            ids = m.iota_e[:].unsqueeze(1).to_broadcast([P, TT, NE])
            for k in range(TOPK):
                step(v.tensor_tensor(m.ohk[:, k, :].rearrange("p (t e) -> p t e", t=TT), ids,
                                     m.idx[:, :, k:k + 1].to_broadcast([P, TT, NE]), ALU.is_equal))
            step(v.tensor_tensor(m.rtmp[:], m.ohk[:, 0, :], m.ohk[:, 1, :], ALU.add))
            step(v.tensor_tensor(m.rtmp[:], m.rtmp[:], m.ohk[:, 2, :], ALU.add))
            v.tensor_tensor(m.mask[:], m.rtmp[:], m.ohk[:, 3, :], ALU.add).then_inc(s.mask_ready, 1)
            v.tensor_tensor(m.gates[:], m.v8[:, :, 0:TOPK], m.v8[:, :, 0:1].to_broadcast([P, TT, TOPK]),
                            ALU.subtract).then_inc(s.gate_in, 1)
            v.wait_ge(s.cnt_ready, 1)
            step(v.tensor_copy(m.cnt[:], bank[7][:, 0:NE]))
            step(v.tensor_scalar(m.nov[:], m.cnt[:], float(SL), None, ALU.is_gt))
            for j in range(2, -(-TOK // SL)):
                step(v.scalar_tensor_tensor(m.nov[:], m.cnt[:], float(j * SL), m.nov[:], ALU.is_gt, ALU.add))
            step(v.tensor_tensor_scan(m.ends[:], m.nov[:], m.zero_e[:], 0.0, ALU.add, ALU.add))
            step(v.tensor_tensor(m.adj[:], m.ends[:], m.nov[:], ALU.subtract))
            step(v.scalar_tensor_tensor(m.adj[:], m.adj[:], float(NE - 1), m.iota_e[:], ALU.add, ALU.subtract))
            v.wait_ge(s.pos_ready, 1)
            step(v.tensor_copy(m.pos[:], bank[6][:, 0:TT * NE]))
            step(v.tensor_scalar(m.blk[:], m.pos[:], float(SL), None, ALU.is_ge))
            for j in range(2, -(-TOK // SL)):
                step(v.scalar_tensor_tensor(m.blk[:], m.pos[:], float(j * SL), m.blk[:], ALU.is_ge, ALU.add))
            step(v.scalar_tensor_tensor(m.flat[:], m.blk[:], -float(SL), m.pos[:], ALU.mult, ALU.add))
            step(v.scalar_tensor_tensor(m.flat[:], m.flat[:], float(NCOL), m.blk[:], ALU.mult, ALU.add))
            step(v.tensor_scalar(m.rtmp[:], m.blk[:], 1.0, None, ALU.min))
            step(v.tensor_tensor(m.rtmp[:].rearrange("p (t e) -> p t e", t=TT),
                                 m.rtmp[:].rearrange("p (t e) -> p t e", t=TT),
                                 m.adj[:].unsqueeze(1).to_broadcast([P, TT, NE]), ALU.mult))
            step(v.scalar_tensor_tensor(m.flat[:], m.flat[:], 1.0, m.rtmp[:], ALU.add, ALU.add))
            step(v.tensor_tensor(m.flat[:].rearrange("p (t e) -> p t e", t=TT),
                                 m.flat[:].rearrange("p (t e) -> p t e", t=TT), ids, ALU.add))
            for k in range(TOPK):
                step(v.tensor_tensor(m.rtmp[:], m.flat[:], m.ohk[:, k, :], ALU.mult))
                step(v.tensor_reduce(m.dest_f[:, k, :], m.rtmp[:].rearrange("p (t e) -> p t e", t=TT), AX_X, ALU.add))
            v.tensor_copy(m.dest[:], m.dest_f[:]).then_inc(s.dest_ready, 1)
            v.wait_ge(s.gate_exp, 1)
            step(v.tensor_reduce(m.gsum[:], m.gates[:], AX_X, ALU.add))
            step(v.reciprocal(m.gsum[:], m.gsum[:]))
            v.tensor_tensor(m.pay[:].bitcast(F32)[:, :, :, 1], m.gates[:],
                            m.gsum[:].unsqueeze(2).to_broadcast([P, TT, TOPK]), ALU.mult).then_inc(s.pay_no, 1)
            v.tensor_copy(m.pay[:, :, :, 0], m.tok_no[:].unsqueeze(2).to_broadcast([P, TT, TOPK])
                          ).then_inc(s.pay_no, 1)
            step(v.tensor_tensor(m.ovc[:], m.iota_o[:].unsqueeze(2).to_broadcast([1, NOVER + 1, NE]),
                                 m.ends[0:1, :].unsqueeze(1).to_broadcast([1, NOVER + 1, NE]), ALU.is_ge))
            step(v.tensor_reduce(m.ovf[:], m.ovc[:], AX_X, ALU.add))
            v.tensor_scalar(m.eid[:, NE + 1:NE + 1 + NOVER + 1], m.ovf[:], float(NE - 1), None, ALU.min)
            v.tensor_copy(m.eid[:, NCOL:NCOL + 1], m.ends[0:1, NE - 1:NE]).then_inc(m.eid_ready, 1)

        @block.tensor
        def _(pe):
            mm, tr = nc.tensor.matmul, nc.tensor.transpose
            pe.wait_ge(s.ident_ready, 1)
            pe.wait_ge(s.vecs_in, 4 * 16)
            tr(bank[7][:, 0:68], m.vrow[0:68, :], m.ident[0:68, 0:68]).then_inc(s.vecs_tr, 1)
            pe.wait_ge(s.c_act, 1)
            for k in range(KC):
                last = tr(bank[6][:, 9 * k:9 * k + 9], m.crow[:, k * P:(k + 1) * P], m.ident[0:9, 0:9])
            last.then_inc(s.c_tr, 1)
            for t in range(TT):
                R = ROWS[t]
                pe.wait_ge(s.xn_ready, t + 1)
                for half in range(2):
                    if t:
                        pe.wait_ge((s.xT_act, s.xT_dve)[half], t)
                    for k in range(4):
                        c = 4 * half + k
                        last = tr(bank[half][:, k * P:k * P + R], m.xn[0:R, t % 2, c * P:(c + 1) * P],
                                  m.ident[0:R, 0:R])
                    last.then_inc(s.x_tr, 1)
            pe.wait_ge(s.rel_ready, 1)
            for h in range(NH):
                if h >= 2:
                    pe.wait_ge(s.line_ready, h - 1)
                mm(bank[4 + h % 2][:, 0:LINE], m.relrep[:, h, :], m.oh_line[:, 0:LINE], start=True,
                   stop=True).then_inc(s.line_tr, 1)
            pe.wait_ge(s.cT_ready, 1)
            mm(bank[6][0:64, 0:P + 1], m.rel64[:].rearrange("p b h -> p (b h)"), m.oh_s[:], start=True,
               stop=True).then_inc(s.bias64_tr, 1)

            def ada(n):
                ph, k = n // KC, n % KC
                pe.wait_ge(ada_in[n % ADA_SLOTS], 16 * (n // ADA_SLOTS + 1))
                for c in range(16):
                    last = mm(bank[2 + ph % 2][:, 9 * c:9 * c + 9], m.raw[:, n % ADA_SLOTS, c * P:(c + 1) * P],
                              m.cT[:, k, :], start=(k == 0 and c == 0), stop=(k == KC - 1), skip_group_check=True)
                last.then_inc(s.ada_used, 1)

            for n in range(2 * KC):
                ada(n)
            def turn_qk(t):
                R = ROWS[t]
                pe.wait_ge(s.qk_ready, t + 1)
                if t:
                    pe.wait_ge(s.qT_ready, t)
                    pe.wait_ge(s.kT_ready, t)
                else:
                    pe.wait_ge(s.xT_act, TT)
                    pe.wait_ge(s.xT_dve, TT)
                for c in range(4):
                    tr(bank[0][:, c * P:c * P + R], m.qn[0:R, c * P:(c + 1) * P], m.ident[0:R, 0:R])
                for g in range(NKV):
                    last = tr(bank[1][:, g * P:g * P + R], m.kd[0:R, g, :, :].rearrange("p a d -> p (a d)"),
                              m.ident[0:R, 0:R])
                last.then_inc(s.qk_tr, 1)

            pe.wait_ge(s.win_in, 16)
            pe.wait_ge(s.h_ready, KC + 1)
            pe.wait_ge(s.bias64_ready, 1)
            for t in range(TT):
                R, b = ROWS[t], 4 + 2 * (t % 2)
                if t >= 2:
                    pe.wait_ge(s.qk_ready, t - 1)
                    pe.wait_ge(s.vt_ready, t - 1)
                for k in range(KC):
                    mm(bank[b][0:R, :], m.hT[:, k, tok(t)], m.w_in[:, k, 0:512], start=(k == 0), stop=(k == KC - 1))
                    last = mm(bank[b + 1][0:R, 0:256], m.hT[:, k, tok(t)], m.w_in[:, k, 512:768], start=(k == 0),
                              stop=(k == KC - 1))
                last.then_inc(s.z_ready, 1)
                if t:
                    turn_qk(t - 1)
            pe.wait_ge(s.mod_ready, 2)
            pe.wait_ge(s.vt_ready, TT)
            for g in range(4):
                if not g:
                    pe.wait_ge(s.qk_ready, TT)
                for k in range(KC):
                    last = mm(bank[4 + g][:], m.w_in[:, k, 768 + g * P:768 + (g + 1) * P], m.hT[:, k, 0:SEQ],
                              start=(k == 0), stop=(k == KC - 1))
                last.then_inc(s.u_ready, 1)
            turn_qk(TP)
            for g in range(4):
                for k in range(KC):
                    last = mm(bank[3][:, g * NS:(g + 1) * NS], m.w_in[:, k, 768 + g * P:768 + (g + 1) * P],
                              m.hT[:, k, SEQ:TOK], start=(k == 0), stop=(k == KC - 1))
            last.then_inc(s.u_ready, 1)
            pe.wait_ge(s.qT_ready, TT)
            for g in range(4):
                last = tr(bank[0][:, g * 120:(g + 1) * 120], m.sp[:, g * P:(g + 1) * P], m.ident[0:120, 0:120])
            last.then_inc(s.sp_tr, 1)
            for n in range(2 * KC, ADA):
                ada(n)

            def score(t):
                c0 = 0 if t else P
                pe.wait_ge(s.qT_ready, t + 1)
                pe.wait_ge(s.kT_ready, t + 1)
                for j in range(4):
                    if t:
                        pe.wait_ge(s.sc_used, 4 * (t - 1) + j + 1)
                    else:
                        pe.wait_ge(s.U_ready, j + 1)
                    g, odd = j // 2, j % 2
                    half = slice(64 * odd, 64 * odd + 64)
                    for a in range(2):
                        last = mm(bank[4 + j][:, a * 256 + c0:a * 256 + 256], m.qT[half, 2 * g + a, tok(t)],
                                  m.kT[half, g, t * P - P + c0:t * P + P], start=True, stop=True)
                    last.then_inc(s.sc_ready, 1)

            def turn_P(t, j):
                pe.wait_ge(s.p_ready, 4 * t + j + 1)
                if 4 * t + j >= 2:
                    pe.wait_ge(s.pt_ev, 4 * t + j - 1)
                else:
                    pe.wait_ge(s.spT_ready, 1)
                    pe.wait_ge(s.kT_ready, TT)
                for a in range(2):
                    for kb in range(0 if t else 1, 2):
                        last = tr(bank[j % 2][:, (2 * a + kb) * P:(2 * a + kb + 1) * P],
                                  m.Pb[:, 2 * j + a, kb * P:(kb + 1) * P], m.ident[:])
                last.then_inc(s.pt_tr, 1)

            def values(t, j):
                pe.wait_ge(s.pt_ev, 4 * t + j + 1)
                if not j:
                    if t:
                        pe.wait_ge(s.attn_ready, t)
                    else:
                        pe.wait_ge(s.Us_ready, 1)
                for a in range(2):
                    h = 2 * j + a
                    g = h // GROUP
                    for kb in range(0 if t else 1, 2):
                        last = mm(bank[3][:, h * HD:(h + 1) * HD], m.PT[:, j % 2, (2 * a + kb) * P:(2 * a + kb + 1) * P],
                                  m.vt[:, t - 1 + kb, g * HD:(g + 1) * HD], start=(kb == (0 if t else 1)),
                                  stop=(kb == 1))
                last.then_inc(s.pv_done, 1)

            def turn_attn(t):
                pe.wait_ge(s.attn_ready, t + 1)
                if t:
                    pe.wait_ge(s.at_ev, t)
                else:
                    pe.wait_ge(s.mod_ready, 3)
                for c in range(4):
                    last = tr(bank[2][:, c * P:(c + 1) * P], m.attn[:, c * P:(c + 1) * P], m.ident[:])
                last.then_inc(s.at_tr, 1)

            score(0)
            for t in range(TP):
                if t + 1 < TP:
                    score(t + 1)
                turn_P(t, 0)
                if t:
                    turn_attn(t - 1)
                turn_P(t, 1)
                values(t, 0)
                turn_P(t, 2)
                values(t, 1)
                turn_P(t, 3)
                values(t, 2)
                values(t, 3)
            turn_attn(TP - 1)
            pe.wait_ge(s.g2_col, 1)
            pe.wait_ge(s.pt_ev, 4 * TP)
            for k in range(4):
                for half in range(2):
                    if k:
                        pe.wait_ge(s.mr_ready, 2 * (k - 1) + half + 1)
                    for c in range(4):
                        last = tr(bank[half][0:9, c * P:(c + 1) * P], m.modT[:, 16 + 8 * k + 4 * half + c, :], m.ident[:])
                    last.then_inc(s.mr_tr, 1)
            pe.wait_ge(s.newkv_in, 32)
            pe.wait_ge(s.sc_used, 4 * TP)
            for half in range(2):
                for b in range(4):
                    last = tr(bank[4 + half][:, b * P:(b + 1) * P], m.Kc[:, 4 * half + b, :], m.ident[:])
                last.then_inc(s.kc_tr, 1)
            pe.wait_ge(s.kcT_ready, 2)
            pe.wait_ge(s.qs_ready, NH)
            for b in range(NS):
                for g in range(NKV):
                    c = (b * NKV + g) * GROUP
                    last = mm(bank[6 + g][:, c:c + GROUP], m.KcT[64 * g:64 * g + 64, b, :], m.qsT[64 * g:64 * g + 64, g, b, :],
                              start=True, stop=True)
            last.then_inc(s.s_sc, 1)
            pe.wait_ge(s.s_scT, NKV)
            tr(bank[7][0:64, 0:P], m.sT[:], m.ident[:]).then_inc(s.s_tr, 1)
            pe.wait_ge(s.s_norm, 1)
            tr(bank[6][:, 0:64], m.P64[:], m.ident[0:64, 0:64]).then_inc(s.s_ptr, 1)
            pe.wait_ge(s.s_pts, 1)
            for b in range(NS):
                for g in range(NKV):
                    c = (b * NKV + g) * GROUP
                    last = mm(bank[7][0:64, c:c + GROUP], m.Vc[:, b, g * HD:(g + 1) * HD], m.PTs[:, c:c + GROUP],
                              start=True, stop=True)
            last.then_inc(s.s_pv, 1)
            for g in range(4):
                pe.wait_ge(s.pooled, g + 1)
                if g:
                    pe.wait_ge(s.pm_done, g)
                else:
                    pe.wait_ge(s.attn_ready, TP)
                mm(bank[3][:], m.w_pool[:, g, :], m.dT[:], start=True, stop=True).then_inc(s.pm_ready, 1)
            pe.wait_ge(s.dTs_ready, 4)
            pe.wait_ge(s.at_ev, TP)
            for g in range(4):
                last = mm(bank[2][:, g * NS:(g + 1) * NS], m.w_pool[:, g, :], m.dTs[:, g, :], start=True, stop=True)
            last.then_inc(s.pms_ready, 1)
            pe.wait_ge(s.mr_ready, 8)
            for g in range(4):
                tr(bank[0][0:BUF, g * P:(g + 1) * P], m.U[:, g, SEQ:SEQ + BUF], m.ident[:])
                last = tr(bank[1][0:NS, g * P:(g + 1) * P], m.Us[:, g, :], m.ident[:])
            last.then_inc(s.ur_tr, 1)
            pe.wait_ge(s.wout_in, 16)
            pe.wait_ge(s.pm_done, 4)
            pe.wait_ge(s.pms_done, 4)
            pe.wait_ge(s.s_mix, 2)

            def mix_out(t):
                R, b = ROWS[t], 4 + 2 * (t % 2)
                if t >= 2:
                    pe.wait_ge(s.x1_ready, t - 1)
                for k in range(KC):
                    for half in range(2):
                        last = mm(bank[b + half][0:R, :], m.mixT[:, k, tok(t)], m.w_out[:, k, 512 * half:512 * half + 512],
                                  start=(k == 0), stop=(k == KC - 1))
                last.then_inc(s.xo_ready, 1)

            def turn_h2(t):
                R = ROWS[t]
                pe.wait_ge(s.h2_ready, t + 1)
                if t:
                    pe.wait_ge(s.h2T_ready, 2 * t)
                else:
                    pe.wait_ge(s.ur_ready, 1)
                for half in range(2):
                    for k in range(4):
                        c = 4 * half + k
                        last = tr(bank[half][:, k * P:k * P + R], m.h2[0:R, t % 2, c * P:(c + 1) * P], m.ident[0:R, 0:R])
                    last.then_inc(s.h2_tr, 1)

            def router(t):
                R = ROWS[t]
                pe.wait_ge(s.h2T_ready, 2 * t + 2)
                pe.wait_ge(s.wr_in, 16)
                if t:
                    pe.wait_ge(s.logit_ready, t)
                for k in range(KC):
                    last = mm(bank[2][0:R, 0:NE], m.h2T[:, k, 0:R], m.w_router[:, k, :], start=(k == 0), stop=(k == KC - 1))
                last.then_inc(s.rt_ready, 1)

            mix_out(0)
            mix_out(1)
            for t in range(TT):
                turn_h2(t)
                router(t)
                if t + 2 < TT:
                    mix_out(t + 2)
            pe.wait_ge(s.mask_ready, 1)
            pe.wait_ge(s.x1_ready, TT)
            mk = m.mask[:].rearrange("p (t e) -> p t e", t=TT)
            for t in range(TT):
                last = mm(bank[7][:, 0:NE], m.ones_b[:], mk[:, t, :], start=(t == 0), stop=(t == TP))
            last.then_inc(s.cnt_ready, 1)
            for t in range(TT):
                for b in range(t + 1):
                    last = mm(bank[6][:, t * NE:(t + 1) * NE], (m.ones_b if b < t else m.tri)[:], mk[:, b, :],
                              start=(b == 0), stop=(b == t))
            last.then_inc(s.pos_ready, 1)

    return sems


def experts(nc, m):
    bank, i, o = m.bank, m.i, m.o
    sem = m.sem
    hi_done, lo_done, unit_used = sem("hi_done"), sem("lo_done"), sem("unit_used")
    gu_used, gmin_ready = sem("gu_used"), sem("gmin_ready")
    tables_in = sem("tables_in")
    silu_ready, act_ready, ta_tr = sem("silu_ready"), sem("act_ready"), sem("ta_tr")
    ah_done, al_done = sem("ah_done"), sem("al_done")
    tx_tr, xh_done, xl_done = sem("tx_tr"), sem("xh_done"), sem("xl_done")
    xg_in, idx_ready, col_ready = sem("xg_in"), sem("idx_ready"), sem("col_ready")
    bhl_in, b2_used, out_zero, out_ev = sem("bhl_in"), sem("b2_used"), sem("out_zero"), sem("out_ev")
    gathers, stores = sem("gathers"), sem("stores")
    scat_done, summed, ones_ready, xg_init = sem("scat_done"), sem("summed"), sem("ones_ready"), sem("xg_init")
    gf_in, f_scaled, f_ready, f_out = sem("gf_in"), sem("f_scaled"), sem("f_ready"), sem("f_out")
    x1_in = [sem(f"x1_in{t}") for t in range(TT)]
    y_in = [sem(f"y_in{t}") for t in range(TT)]
    gate_up = ((bank[0], bank[1]), (bank[2], bank[3]))
    outb, bank_a, bank_x = (bank[4], bank[5]), bank[6], bank[7]
    halves = (slice(0, 512), slice(512, 1024))

    def tok(t):
        return slice(t * P, t * P + ROWS[t])

    def passes(eng, body, first=0):
        with eng.Fori(first, NE) as p:
            body(p, p)
        extra = eng.value_load(m.eid[0:1, NCOL:NCOL + 1], min_val=0, max_val=NOVER)
        with eng.Fori(0, NOVER) as q:
            with eng.If(q < extra):
                body(q + NE, None)
        return extra + NE

    with nc.Block() as block:

        @block.sync
        def _(sp):
            def load(p, e):
                if e is None:
                    e = sp.value_load(m.eid[0:1, ds(p + 1)], min_val=0, max_val=NE - 1)
                for u in range(UNITS):
                    sp.wait_ge(lo_done, p * UNITS + (u + 1 - UNITS))
                    m.load_unit(sp, e, u)

            n = passes(sp, load, 1)
            sp.wait_ge(lo_done, n * UNITS)
            for t in range(TT):
                sp.dma_start(m.xf[0:ROWS[t], t, :], m.x1d[tok(t), :]).then_inc(x1_in[t], 16)
            sp.dma_start(m.gf[:, 0, :], m.modd[3, NS:NS + 1, :].to_broadcast([P, D])).then_inc(gf_in, 16)
            sp.dma_start(m.gf[0:NS, 1, :], m.modd[3, 0:NS, :]).then_inc(gf_in, 16)
            sp.wait_ge(summed, 1)
            for t in range(TT):
                sp.dma_start(m.yf[0:ROWS[t], t, :], m.yd[tok(t), :]).then_inc(y_in[t], 16)
            for t in range(TT):
                dst = o["y_prompt"][0, tok(t), :] if t < TP else o["y_sample"].rearrange("b t d -> (b t) d")
                sp.wait_ge(f_ready, t + 1)
                sp.dma_start(dst, m.yf[0:ROWS[t], t, :]).then_inc(f_out, 16)
            sp.wait_ge(f_out, TT * 16)

        @block.gpsimd
        def _(gp):
            limit = gp.to_reg(TOK - 1)
            gp.memset(m.ones2[:].bitcast(F32), 1.0).then_inc(ones_ready, 1)
            gp.wait_ge(ones_ready, 1)
            gp.memset(m.xg[:], 0.0).then_inc(xg_init, 1)

            gp.wait_ge(xg_init, 1)
            gp.tensor_copy(m.idx_g[:], m.tab[:, 1:2, 0]).then_inc(idx_ready, 1)
            gp.wait_ge(idx_ready, 1)
            gp.indirect_dma_start(m.xg[:], None, m.h2d, bass.IndirectOffsetOnAxis(ap=m.idx_g[:], axis=0),
                                  bounds_check=limit, oob_is_err=False).then_inc(xg_in, 16)
            gp.dma_start(m.bhl[:], m.bd[0]).then_inc(bhl_in, 16)

            def store(p):
                gp.wait_ge(out_ev, p + 1)
                gp.sem_inc(stores, 1)
                gp.indirect_dma_start(m.yd, bass.IndirectOffsetOnAxis(ap=m.col_s[:, 0:1], axis=0), m.ost[:], None,
                                      bounds_check=limit, oob_is_err=False,
                                      compute_op=ALU.add).then_inc(scat_done, 16)
                gp.wait_ge(scat_done, p * 16 + 16)

            def one(p, e):
                nxt = gp.value_load(m.eid[0:1, ds(p + 2)], min_val=0, max_val=NE - 1)
                gp.tensor_copy(m.col_s[:], m.tab[:, ds(p), :].rearrange("p c w -> p (c w)")).then_inc(col_ready, 1)
                gp.wait_ge(col_ready, p + 1)
                gp.wait_ge(xg_in, p * 16 + 16)
                gp.tensor_copy(m.idx_g[:], m.tab[:, ds(p + 2), 0]).then_inc(idx_ready, 1)
                gp.wait_ge(idx_ready, p + 2)
                gp.wait_ge(tx_tr, p * 2 + 2)
                gp.sem_inc(gathers, 1)
                gp.indirect_dma_start(m.xg[:], None, m.h2d, bass.IndirectOffsetOnAxis(ap=m.idx_g[:], axis=0),
                                      bounds_check=limit, oob_is_err=False).then_inc(xg_in, 16)
                store(p)
                gp.wait_ge(b2_used, p + 1)
                gp.dma_start(m.bhl[:], m.bd[ds(nxt), :, :].rearrange("e a n -> (e a) n")).then_inc(bhl_in, 16)

            n = passes(gp, one)
            gp.tensor_copy(m.col_s[:], m.tab[:, ds(n), :].rearrange("p c w -> p (c w)")).then_inc(col_ready, 1)
            store(n)
            gp.sem_inc(summed, 1)

        @block.scalar
        def _(act):
            def high(p, u):
                act.wait_ge(m.raw_in[u], (p + 1) * (32 if u < W1_UNITS else 16))
                act.wait_ge(unit_used, p * UNITS + (u + 1))
                nc.scalar.copy(m.hi[:, u % HL, :], m.raw[:, u, :]).then_inc(hi_done, 1)

            def high_x(p, half):
                act.wait_ge(tx_tr, p * 2 + (half + 1))
                nc.scalar.copy(m.xTh[:, 4 * half:4 * half + 4, :].rearrange("p k n -> p (k n)"),
                               bank_x[:]).then_inc(xh_done, 1)

            def gated(p):
                act.wait_ge(col_ready, p + 1)
                act.wait_ge(unit_used, p * UNITS + HL)
                for half in range(2):
                    ins = nc.scalar.activation(m.ost[:, halves[half]], outb[half][:], ACT.Copy,
                                               scale=m.col_s[:, 1:2].bitcast(F32))
                ins.then_inc(out_ev, 1)

            def swish(p, j):
                act.wait_ge(gmin_ready, p * 2 + (j + 1))
                nc.scalar.activation(m.gate[:], m.gate[:], ACT.Silu, scale=ALPHA).then_inc(silu_ready, 1)

            def high_a(p, j):
                act.wait_ge(ta_tr, p * 2 + (j + 2))
                nc.scalar.activation(m.aTh[:, 4 * j:4 * j + 4, :].rearrange("p k n -> p (k n)"), bank_a[:], ACT.Copy,
                                     scale=1.0 / ALPHA).then_inc(ah_done, 1)

            def one(p, e):
                for u in range(3):
                    high(p, u)
                gated(p)
                for u in range(3, 8):
                    high(p, u)
                swish(p, 0)
                high(p, 8)
                high(p, 9)
                high_a(p, 0)
                high(p, 10)
                swish(p, 1)
                high(p, 11)
                high_x(p + 1, 0)
                high_a(p, 1)
                high_x(p + 1, 1)

            act.wait_ge(ones_ready, 1)
            nc.scalar.activation(m.ost[0:2, 0:P], m.ones2[:].bitcast(F32), ACT.Silu).then_inc(tables_in, 1)
            act.wait_ge(tables_in, 1)
            high_x(0, 0)
            high_x(0, 1)
            act.wait_ge(out_zero, 1)
            n = passes(act, one)
            gated(n)

        @block.vector
        def _(v):
            def low(p, u):
                v.wait_ge(hi_done, p * UNITS + (u + 1))
                v.tensor_tensor(m.lo[:, u % HL, :], m.raw[:, u, :], m.hi[:, u % HL, :].bitcast(F32),
                                ALU.subtract).then_inc(lo_done, 1)

            def low_x(p, half):
                v.wait_ge(xh_done, p * 2 + (half + 1))
                ks = slice(4 * half, 4 * half + 4)
                v.tensor_tensor(m.xTl[:, ks, :].rearrange("p k n -> p (k n)"), bank_x[:],
                                m.xTh[:, ks, :].bitcast(F32).rearrange("p k n -> p (k n)"),
                                ALU.subtract).then_inc(xl_done, 1)

            def limit(p, j):
                gate, upb = gate_up[j]
                v.wait_ge(unit_used, p * UNITS + (4 * (j + 1) + HL))
                v.wait_ge(act_ready, p * 2 + (j + 1))
                v.tensor_scalar(m.gate[:], gate[:], LIMIT, None, ALU.min).then_inc(gmin_ready, 1)
                v.wait_ge(ta_tr, p * 2 + (j + 1))
                v.tensor_scalar(m.up[:], upb[:], LIMIT, -LIMIT, ALU.min, ALU.max).then_inc(gu_used, 1)

            def glu(p, j):
                v.wait_ge(gu_used, p * 2 + (j + 3))
                v.wait_ge(silu_ready, p * 2 + (j + 1))
                v.scalar_tensor_tensor(m.up[:], m.up[:], 1.0, m.gate[:], ALU.add, ALU.mult).then_inc(act_ready, 1)

            def low_a(p, j):
                v.wait_ge(ah_done, p * 2 + (j + 1))
                ks = slice(4 * j, 4 * j + 4)
                v.scalar_tensor_tensor(m.aTl[:, ks, :].rearrange("p k n -> p (k n)"), bank_a[:], 1.0 / ALPHA,
                                       m.aTh[:, ks, :].bitcast(F32).rearrange("p k n -> p (k n)"), ALU.mult,
                                       ALU.subtract).then_inc(al_done, 1)

            def one(p, e):
                for u in range(7):
                    low(p, u)
                limit(p, 0)
                low(p, 7)
                glu(p, 0)
                low(p, 8)
                low(p, 9)
                low_a(p, 0)
                limit(p, 1)
                low(p, 10)
                glu(p, 1)
                low_x(p + 1, 0)
                low(p, 11)
                low_a(p, 1)
                low_x(p + 1, 1)

            v.memset(outb[0][:], 0.0)
            v.memset(outb[1][:], 0.0).then_inc(out_zero, 1)
            low_x(0, 0)
            low_x(0, 1)
            passes(v, one)
            v.wait_ge(gf_in, 32)
            for t in range(TT):
                R = ROWS[t]
                v.wait_ge(y_in[t], 16)
                v.wait_ge(x1_in[t], 16)
                v.tensor_tensor(m.yf[0:R, t, :], m.yf[0:R, t, :], m.gf[0:R, t // TP, :], ALU.mult).then_inc(f_scaled, 1)
                v.wait_ge(f_scaled, t + 1)
                v.tensor_tensor(m.yf[0:R, t, :], m.yf[0:R, t, :], m.xf[0:R, t, :], ALU.add).then_inc(f_ready, 1)

        @block.tensor
        def _(pe):
            mm, tr = nc.tensor.matmul, nc.tensor.transpose

            def turn_x(p, half):
                if not half:
                    pe.wait_ge(xg_in, p * 16 + 16)
                pe.wait_ge(xl_done, p * 2 + half)
                for k in range(4):
                    c = 4 * half + k
                    last = tr(bank_x[:, k * P:(k + 1) * P], m.xg[:, c * P:(c + 1) * P], m.ident[:])
                last.then_inc(tx_tr, 1)

            def turn_a(p, j):
                pe.wait_ge(act_ready, p * 2 + (j + 2))
                pe.wait_ge(al_done, p * 2 + (j + 1))
                for k in range(4):
                    last = tr(bank_a[:, k * P:(k + 1) * P], m.up[:, k * P:(k + 1) * P], m.ident[:])
                last.then_inc(ta_tr, 1)

            def products(banks, h, l, w, c, last_one):
                for b in range(2):
                    mm(banks[b][:], h, m.hi[:, w, c + 512 * b:c + 512 * b + 512], start=False, stop=False)
                for b in range(2):
                    mm(banks[b][:], h, m.lo[:, w, c + 512 * b:c + 512 * b + 512], start=False, stop=False)
                for b in range(2):
                    ins = mm(banks[b][:], l, m.hi[:, w, c + 512 * b:c + 512 * b + 512], start=False, stop=last_one)
                return ins

            def up_unit(p, u):
                j = u // 4
                pe.wait_ge(lo_done, p * UNITS + (u + 1))
                for kk in range(2):
                    k = 2 * (u % 4) + kk
                    last = products(gate_up[j], m.xTh[:, k, :], m.xTl[:, k, :], u % HL, kk * D, k == KC - 1)
                last.then_inc(unit_used, 1)

            def down_half(p, u, kk):
                k = 2 * (u - W1_UNITS) + kk
                if not kk:
                    pe.wait_ge(lo_done, p * UNITS + (u + 1))
                    pe.wait_ge(al_done, p * 2 + (2 if u < 10 else 3))
                return products(outb, m.aTh[:, k, :], m.aTl[:, k, :], u % HL, kk * D, k == KC - 1)

            def bias(banks, c0, c1):
                mm(banks[0][:], m.ones2[:], m.bhl[:, c0:c0 + 512], start=True, stop=False)
                return mm(banks[1][:], m.ones2[:], m.bhl[:, c1:c1 + 512], start=True, stop=False)

            def one(p, e):
                pe.wait_ge(xl_done, p * 2 + 2)
                pe.wait_ge(bhl_in, p * 16 + 16)
                for j in range(2):
                    pe.wait_ge(gu_used, p * 2 + (j + 1))
                    bias(gate_up[j], 512 * j, D + 512 * j)
                    for u in range(4 * j, 4 * j + 4):
                        if u == 7:
                            turn_a(p, 0)
                        up_unit(p, u)
                pe.wait_ge(out_ev, p + 1)
                bias(outb, 2 * D, 2 * D + 512).then_inc(b2_used, 1)
                down_half(p, 8, 0)
                down_half(p, 8, 1).then_inc(unit_used, 1)
                turn_x(p + 1, 0)
                down_half(p, 9, 0)
                down_half(p, 9, 1).then_inc(unit_used, 1)
                turn_a(p, 1)
                turn_x(p + 1, 1)
                down_half(p, 10, 0)
                down_half(p, 10, 1).then_inc(unit_used, 1)
                down_half(p, 11, 0)
                down_half(p, 11, 1).then_inc(unit_used, 1)

            pe.sem_inc(unit_used, HL)
            pe.sem_inc(gu_used, 2)
            pe.sem_inc(act_ready, 1)
            pe.sem_inc(ta_tr, 1)
            pe.sem_inc(al_done, 1)
            pe.wait_ge(ones_ready, 1)
            pe.wait_ge(xg_in, 16)
            for half in range(2):
                if half:
                    pe.wait_ge(xl_done, 1)
                for k in range(4):
                    c = 4 * half + k
                    last = tr(bank_x[:, k * P:(k + 1) * P], m.xg[:, c * P:(c + 1) * P], m.ident[:])
                last.then_inc(tx_tr, 1)
            passes(pe, one)


OUTS = [("y_prompt", (1, SEQ, D)), ("y_sample", (NS, 1, D)), ("new_k_prompt", (1, 1, P, NKV, HD)),
        ("new_v_prompt", (1, 1, P, NKV, HD)), ("new_pool_prompt", (1, 1, BUF, PW)),
        ("new_k_sample", (1, NS, P, NKV, HD)), ("new_v_sample", (1, NS, P, NKV, HD)),
        ("new_pool_sample", (1, NS, BUF, PW))]


def distance_bucket():
    n = np.arange(P)
    far = np.log(np.maximum(n, 1).astype(np.float32) / np.float32(16)) / np.float32(np.log(128 / 16)) * np.float32(16)
    return np.where(n < 16, n, np.minimum(16 + far.astype(np.int32), NE - 1))


def constants():
    bucket = distance_bucket()
    line = np.zeros((NE + 1, 3 * P), np.float32)
    line[NE, :] = NEG
    for d in range(P):
        line[:, 2 * P - 1 - d] = 0.0
        line[bucket[d], 2 * P - 1 - d] = 1.0
    samples = np.zeros((NE + 1, P + 1), np.float32)
    for c in range(P):
        samples[bucket[(P - c) % P], c] = 1.0
    samples[NE, P] = 1.0
    rec = np.array([[1.0 / min(c + 1, w) for c in range(BUF + 1)] for w in WINDOWS], np.float32)
    return {"oh_line": line, "oh_s": samples, "rec": rec}


def kernel(**inputs):
    import concourse.bacc as bacc
    from concourse.bass_utils import run_bass_kernel_spmd

    nc = bacc.Bacc("TRN2", target_bir_lowering=False, num_devices=1)
    arrays, ins, outs = {}, {}, {}
    for name, a in {**inputs, **constants()}.items():
        a = np.ascontiguousarray(a)
        arrays[f"in_{name}"] = a
        ins[name] = nc.dram_tensor(f"in_{name}", a.shape, mybir.dt.from_np(a.dtype), kind="ExternalInput").ap()
    for name, shape in OUTS:
        outs[name] = nc.dram_tensor(f"out_{name}", shape, F32, kind="ExternalOutput").ap()
    build(nc, ins, outs)
    r = run_bass_kernel_spmd(nc, [arrays], core_ids=[0])
    return tuple(r.results[0][f"out_{name}"] for name, _ in OUTS)
```

```python
from contextlib import ExitStack

import numpy as np
import concourse.bass as bass
from concourse import mybir
from concourse.alu_op_type import AluOpType as ALU

ACT = mybir.ActivationFunctionType
AX_X = mybir.AxisListType.X
F32, F32R, BF16, I32, U32 = (mybir.dt.float32, mybir.dt.float32r, mybir.dt.bfloat16, mybir.dt.int32,
                             mybir.dt.uint32)

P = 128
D = 1024
SEQ, NS = 512, 8
TOK = SEQ + NS
HD, NH, NKV, GROUP = 64, 8, 2, 4
AW, KVW, PW = 512, 128, 512
IN_W = AW + 2 * KVW + PW
WINDOWS = (2, 4, 8, 16)
BUF = 15
NE, TOPK, DFF = 32, 4, 1024
LIMIT, ALPHA, EPS, NEG = 7.0, 1.702, 1e-6, -1e30
TP = SEQ // P
TT = TP + 1
ROWS = [P] * TP + [NS]
KC = D // P
SL = P
NOVER = (TOK * TOPK) // (SL + 1)
NPASS = NE + NOVER
NCOL = NPASS + 2
assert NOVER % 4 == 0
BLOCKS = -(-TOK // SL)
TCOL = BLOCKS * NE + 1
OOB = 1 << 20
LINE = 3 * P - 1
UNITS, W1_UNITS = 12, 8
HL = 4
ADA_SLOTS = 3


def ds(i, n=1):
    return bass.ds(i, n)


def y_rows(o, t):
    return o["y_prompt"][0, t * P:(t + 1) * P, :] if t < TP else o["y_sample"].rearrange("b t d -> (b t) d")


class Record:
    pass


def build(nc, i, o):
    m = Record()
    m.i, m.o = i, o
    with ExitStack() as ctx:
        def sem(name):
            return ctx.enter_context(nc.semaphore(name))

        m.sem = sem

        def dram(name, shape, dt):
            return nc.dram_tensor(name, shape, dt).ap()

        base = (nc.sbuf_base + 63) // 64 * 64
        size = {F32: 4, F32R: 4, BF16: 2, I32: 4, U32: 4}

        def at(name, shape, dt, offset):
            return nc.alloc_sbuf_tensor_at(name, shape, dt, offset=offset)

        kept = [base]

        def small(name, shape, dt=F32):
            t = at(name, shape, dt, kept[0])
            kept[0] += (int(np.prod(shape[1:])) * size[dt] + 31) // 32 * 32
            return t

        m.bank = [ctx.enter_context(nc.psum_tensor(f"bank{b}", [P, 512], F32)) for b in range(8)]

        m.ident = small("ident", [P, P])
        m.vecsT = small("vecsT", [P, 12])
        m.modT = small("modT", [P, 16, 9])
        m.g1T = small("g1T", [P, KC, 9])
        m.cT = small("cT", [P, KC, 9])
        m.eps = small("eps", [P, 1])
        m.ssq = small("ssq", [P, TT])
        m.rstd = small("rstd", [P, TT])
        m.hss = small("hss", [P, 10])
        m.hrs = small("hrs", [P, 10])
        m.m8 = small("m8", [P, NH])
        m.negm = small("negm", [P, NH])
        m.esink = small("esink", [P, NH])
        m.den = small("den", [P, NH])
        m.rden = small("rden", [P, NH])
        m.sinks_bc = small("sinks_bc", [P, NH])
        m.s64 = small("s64", [64, 8])
        m.qn_bc = small("qn_bc", [P, HD])
        m.kn_bc = small("kn_bc", [P, HD])
        m.ss2 = small("ss2", [P, TT])
        m.rs2 = small("rs2", [P, TT])
        m.logits = small("logits", [P, TT, NE])
        m.br_bc = small("br_bc", [P, NE])
        m.tab = small("tab", [P, TCOL, 2], I32)
        m.eid = small("eid", [1, NCOL + 1], I32)
        m.cols = small("cols", [1, NCOL], I32)
        m.qsT = small("qsT", [P, NKV, NS, GROUP])
        m.bias64 = small("bias64", [64, P + 1])
        m.rec = small("rec_sb", [P, 4, BUF + 1])
        m.dTs = small("dTs", [P, 4, NS])
        kept_end = kept[0]

        raw0 = (kept_end + 63) // 64 * 64
        SLOT = 2048 * 4
        m.raw = at("raw", [P, UNITS, 2048], F32, raw0)
        wproj0 = raw0 + 7 * SLOT
        m.w_in = at("w_in_sb", [P, KC, IN_W], F32, wproj0)
        m.w_out = at("w_out_sb", [P, KC, D], F32, wproj0)
        m.Kc = at("Kc", [P, NS, P], F32, raw0 + 6 * SLOT)
        m.relrep = at("relrep", [NE + 1, NH, P], F32, raw0 + 6 * SLOT)
        m.Vc = at("Vc", [P, NS, P], F32, raw0 + 6 * SLOT + 4096)
        H0 = raw0 + UNITS * SLOT

        s3 = raw0 + 3 * SLOT
        m.w_pool = at("w_pool_sb", [P, 4, P], F32, s3)
        m.sp = at("sp", [NS * BUF, PW], F32, s3 + 2048)
        m.spT = at("spT", [P, 4, NS, BUF], F32, s3 + 4096)
        m.oh_line = at("oh_line_sb", [NE + 1, 3 * P], F32, s3 + 6144)
        m.vrow = at("vrow", [12, P], F32, s3 + 7680)
        m.line = at("line", [P, NH, LINE], F32, raw0 + 4 * SLOT)
        m.wlo = at("wlo", [P, ADA_SLOTS, 2048], F32R, raw0)
        m.whi = at("whi", [P, 2, 2048], F32R, s3 + 2048)
        m.bada = at("bada", [9, D], F32, raw0 + 4 * SLOT + 12288)
        m.crow = at("crow", [9, D], F32, raw0 + 4 * SLOT + 12288)
        m.xs = at("xs", [P, TT, D], F32, H0)
        m.hT = at("hT", [P, KC, TOK], F32, H0 + 20480)
        m.mixT = at("mixT", [P, KC, TOK], F32, H0 + 20480)
        m.zero = at("zero", [P, D], F32, H0 + 37120)
        m.qT = at("qT", [P, 4, TOK], F32, H0 + 37120)
        m.kT = at("kT", [P, NKV, TOK], F32, H0 + 45440)
        m.vt = at("vt", [P, TT, KVW], F32, H0 + 49600)
        m.U = at("U", [P, 4, BUF + SEQ], F32, H0 + 52160)
        m.Us = at("Us", [P, 4, NS], F32, H0 + 60608)
        m.xn = at("xn", [P, 2, D], F32, H0 + 60736)
        m.bias = at("bias", [P, NH, 2 * P], F32, H0 + 60736)
        m.gm_s = at("gm_s", [NS, D], F32, H0 + 60736)
        m.g2_s = at("g2_s", [NS, D], F32, H0 + 64832)
        m.bb = at("bb", [NE, 3 * D], F32, H0 + 68928)
        m.bb_lo = at("bb_lo", [NE, 3 * D], F32R, H0 + 68928)
        m.Pb = at("Pb", [P, NH, 2 * P], F32, H0 + 68928)
        m.KcT = at("KcT", [P, NS, P], F32, H0 + 68928)
        m.h2 = at("h2", [P, 2, D], F32, H0 + 68928)
        m.PT = at("PT", [P, 2, 512], F32, H0 + 77120)
        m.sT = at("sT", [P, 64], F32, H0 + 77120)
        m.P64 = at("P64", [64, P], F32, H0 + 77376)
        m.PTs = at("PTs", [P, 64], F32, H0 + 77888)
        m.attn = at("attn", [P, NH * HD], F32, H0 + 81216)
        m.sq = at("sq", [P, 640], F32, H0 + 83264)
        m.qn = at("qn", [P, 512], F32, H0 + 85824)
        m.kd = at("kd", [P, NKV, 2, HD], F32, H0 + 87872)
        m.la = at("la", [P, BUF + SEQ], F32, H0 + 83264)
        m.lb = at("lb", [P, BUF + SEQ], F32, H0 + 85376)
        m.dT = at("dT", [P, SEQ], F32, H0 + 87488)
        m.s2_s = at("s2_s", [NS, D], F32, H0 + 83264)
        m.bb_hi = at("bb_hi", [NE, 3 * D], F32R, H0 + 89600)
        m.c2 = at("c2", [P, KC, P], F32R, H0 + 89600)
        m.gm_bc = at("gm_bc", [P, D], F32, H0 + 89600)
        m.g2_bc = at("g2_bc", [P, D], F32, H0 + 93696)
        m.s2_bc = at("s2_bc", [P, D], F32, H0 + 97792)
        m.nf = at("nf", [9, D], F32, H0 + 97792)
        m.mrow = at("mrow", [9, 2, 512], F32, H0 + 101888)
        m.ulast = at("ulast", [BUF, PW], F32, H0 + 101888)
        m.uslast = at("uslast", [NS, PW], F32, H0 + 81216)
        m.w_router = at("w_router_sb", [P, KC, NE], F32, H0 + 87488)
        m.oh_s = at("oh_s_sb", [NE + 1, P + 1], F32, H0 + 105984)
        m.relb = at("relb", [NE + 1, NH], F32, H0 + 106528)
        m.rel64 = at("rel64", [NE + 1, NS, NH], F32, H0 + 106560)
        m.kn = at("kn", [P, 2, KVW], F32, H0 + 105984)
        m.h2T = at("h2T", [P, KC, P], F32, H0 + 37120)
        m.junk = at("junk", [P, D], F32, H0 + 41216)
        r_at = [H0 + 45440]

        def rt(name, shape, dt=F32):
            t = at(name, shape, dt, r_at[0])
            r_at[0] += (int(np.prod(shape[1:])) * size[dt] + 31) // 32 * 32
            return t

        m.ones_b = rt("ones_b", [P, P], BF16)
        m.tri = rt("tri", [P, P], BF16)
        m.iota_e = rt("iota_e", [P, NE])
        m.tok_no = rt("tok_no", [P, TT], I32)
        m.v8 = rt("v8", [P, TT, 8])
        m.i8 = rt("i8", [P, TT, 8], U32)
        m.idx = rt("idx", [P, TT, TOPK])
        m.ohk = rt("ohk", [P, TT, TOPK, NE])
        m.mask = rt("mask", [P, TT, NE], BF16)
        m.blk = rt("blk", [P, TT, NE])
        m.flat = rt("flat", [P, TT, NE])
        m.picked = rt("picked", [P, TT, TOPK, NE])
        m.gates = rt("gates", [P, TT, TOPK])
        m.gsum = rt("gsum", [P, TT])
        m.dest_f = rt("dest_f", [P, TT, TOPK])
        m.dest = rt("dest", [P, TT, TOPK], I32)
        m.pay = rt("pay", [P, TT, TOPK, 2], I32)
        m.cnt = rt("cnt", [1, NE])
        m.nov = rt("nov", [1, NE])
        m.ends = rt("ends", [1, NE])
        m.starts = rt("starts", [1, NE])
        m.zero_e = rt("zero_e", [1, NE])
        m.behind = rt("behind", [1, NOVER + 1, NE])
        m.begun = rt("begun", [1, NOVER + 1, NE])
        m.ovf = rt("ovf", [1, 3, NOVER + 1])
        m.iota_o = rt("iota_o", [1, NOVER + 1])
        m.iota_c = rt("iota_c", [1, NOVER + 1])
        assert r_at[0] <= H0 + 60736, r_at[0] - H0

        m.hi = at("hi", [P, HL, 2048], F32R, H0)
        m.lo = at("lo", [P, HL, 2048], F32R, H0 + 4 * SLOT)
        m.xg = at("xg", [P, D], F32, H0 + 65536)
        m.xTh = at("xTh", [P, KC, P], F32R, H0 + 69632)
        m.xTl = at("xTl", [P, KC, P], F32R, H0 + 73728)
        m.aTh = at("aTh", [P, KC, P], F32R, H0 + 77824)
        m.aTl = at("aTl", [P, KC, P], F32R, H0 + 81920)
        m.gate = at("gate", [P, 512], F32, H0 + 86016)
        m.up = at("up", [P, 512], F32, H0 + 88064)
        m.ost = at("ost", [P, D], F32, H0 + 90112)
        m.bhl = at("bhl", [2, 3 * D], F32R, H0 + 94208)
        m.ones2 = at("ones2", [2, P], F32R, H0 + 106496)
        m.col_s = at("col_s", [P, 2], I32, H0 + 107008)
        m.idx_g = at("idx_g", [P, 1], I32, H0 + 107040)
        m.yf = at("yf", [P, TT, D], F32, raw0)
        m.gf = at("gf", [P, 2, D], F32, raw0 + 40960)
        assert H0 + 107072 <= nc.sbuf_usable_end

        m.h2d = dram("h2d", [TOK, D], F32)
        m.yd = dram("yd", [TOK, D], F32)
        m.tabd = dram("tabd", [P, TCOL * 2], I32)
        m.skew = dram("skew", [NH, P * LINE], F32)
        m.modd = dram("modd", [4, 9, D], F32)
        m.bd = dram("bd", [NE, 2, 3 * D], F32R)
        m.raw_in = [sem(f"raw_in{u}") for u in range(UNITS)]
        m.eid_ready = sem("eid_ready")
        head_sems = head(nc, m)
        nc.clear_and_free_semaphores(head_sems)
        nc.all_engine_barrier()
        experts(nc, m)


def head(nc, m):
    i, o, bank, sem = m.i, m.o, m.bank, m.sem
    sems = []

    def signal(name):
        sems.append(nc.alloc_semaphore(name=name))
        return sems[-1]

    s = Record()
    s.bada_in = signal("bada_in")
    s.nf_in = signal("nf_in")
    s.mt_tr = signal("mt_tr")
    s.modT_ready = signal("modT_ready")
    s.us_rows = signal("us_rows")
    s.us_tr = signal("us_tr")
    s.gate_in = signal("gate_in")
    s.pay_ready = signal("pay_ready")
    s.ada_hi = signal("ada_hi")
    s.ada_lo = signal("ada_lo")
    s.c2_ready = signal("c2_ready")
    s.vecs_in = signal("vecs_in")
    s.c_in = signal("c_in")
    s.small_in = signal("small_in")
    s.bb_in = signal("bb_in")
    s.win_in = signal("win_in")
    s.wout_in = signal("wout_in")
    s.kv_in = signal("kv_in")
    s.newkv_in = signal("newkv_in")
    s.ident_ready = signal("ident_ready")
    s.zeros_ready = signal("zeros_ready")
    s.zero_out = signal("zero_out")
    s.vecs_tr = signal("vecs_tr")
    s.vecs_ready = signal("vecs_ready")
    s.c_act = signal("c_act")
    s.c_tr = signal("c_tr")
    s.cT_ready = signal("cT_ready")
    s.ssq_ready = signal("ssq_ready")
    s.rms_ready = signal("rms_ready")
    s.rstd_ready = signal("rstd_ready")
    s.xn_ready = signal("xn_ready")
    s.x_tr = signal("x_tr")
    s.xT_act = signal("xT_act")
    s.xT_dve = signal("xT_dve")
    s.ada_used = signal("ada_used")
    s.g1_ready = signal("g1_ready")
    s.hT_half = signal("hT_half")
    s.h_ready = signal("h_ready")
    s.rel_ready = signal("rel_ready")
    s.line_tr = signal("line_tr")
    s.line_ready = signal("line_ready")
    s.skew_out = signal("skew_out")
    s.bias_in = signal("bias_in")
    s.bias64_tr = signal("bias64_tr")
    s.bias64_ready = signal("bias64_ready")
    s.bb_hi_done = signal("bb_hi_done")
    s.bb_lo_done = signal("bb_lo_done")
    s.bb_out = signal("bb_out")
    s.z_ready = signal("z_ready")
    s.sq_ready = signal("sq_ready")
    s.vt_ready = signal("vt_ready")
    s.hss_ready = signal("hss_ready")
    s.hrms_ready = signal("hrms_ready")
    s.hrs_ready = signal("hrs_ready")
    s.qn_raw = signal("qn_raw")
    s.kn_raw = signal("kn_raw")
    s.qk_ready = signal("qk_ready")
    s.qk_tr = signal("qk_tr")
    s.qT_ready = signal("qT_ready")
    s.kT_ready = signal("kT_ready")
    s.u_ready = signal("u_ready")
    s.U_ready = signal("U_ready")
    s.Us_ready = signal("Us_ready")
    s.pad_ready = signal("pad_ready")
    s.pool_step = signal("pool_step")
    s.pooled = signal("pooled")
    s.sp_tr = signal("sp_tr")
    s.spT_ready = signal("spT_ready")
    s.spool_step = signal("spool_step")
    s.dTs_ready = signal("dTs_ready")
    s.pm_ready = signal("pm_ready")
    s.pm_done = signal("pm_done")
    s.pms_ready = signal("pms_ready")
    s.pms_done = signal("pms_done")
    s.sc_ready = signal("sc_ready")
    s.sc_used = signal("sc_used")
    s.sm_ready = signal("sm_ready")
    s.p_ready = signal("p_ready")
    s.e_ready = signal("e_ready")
    s.pt_tr = signal("pt_tr")
    s.pt_ev = signal("pt_ev")
    s.pv_done = signal("pv_done")
    s.o_ready = signal("o_ready")
    s.eps_ready = signal("eps_ready")
    s.attn_ready = signal("attn_ready")
    s.at_tr = signal("at_tr")
    s.at_ev = signal("at_ev")
    s.kc_tr = signal("kc_tr")
    s.kcT_ready = signal("kcT_ready")
    s.qs_ready = signal("qs_ready")
    s.s_sc = signal("s_sc")
    s.s_scT = signal("s_scT")
    s.s_tr = signal("s_tr")
    s.s_soft = signal("s_soft")
    s.s_step = signal("s_step")
    s.s_exp = signal("s_exp")
    s.s_norm = signal("s_norm")
    s.s_ptr = signal("s_ptr")
    s.s_pts = signal("s_pts")
    s.s_pv = signal("s_pv")
    s.s_mix = signal("s_mix")
    s.mr_ready = signal("mr_ready")
    s.mod_out = signal("mod_out")
    s.bc_in = signal("bc_in")
    s.bcs_in = signal("bcs_in")
    s.wr_in = signal("wr_in")
    s.xo_ready = signal("xo_ready")
    s.vector_step = signal("vector_step")
    s.x1_ready = signal("x1_ready")
    s.ss2_ready = signal("ss2_ready")
    s.rms2_ready = signal("rms2_ready")
    s.rs2_ready = signal("rs2_ready")
    s.h2_ready = signal("h2_ready")
    s.x1_out = signal("x1_out")
    s.h2_tr = signal("h2_tr")
    s.h2T_ready = signal("h2T_ready")
    s.rt_ready = signal("rt_ready")
    s.logit_ready = signal("logit_ready")
    s.r_init = signal("r_init")
    s.mask_ready = signal("mask_ready")
    s.cnt_ready = signal("cnt_ready")
    s.pos_ready = signal("pos_ready")
    s.gate_exp = signal("gate_exp")
    s.tab_init = signal("tab_init")
    s.tab_out = signal("tab_out")
    s.dest_ready = signal("dest_ready")
    s.scattered = signal("scattered")
    s.tab_in = signal("tab_in")
    s.new_out = signal("new_out")
    s.ur_tr = signal("ur_tr")
    s.ur_ready = signal("ur_ready")
    s.ulast_out = signal("ulast_out")
    x_in = [signal(f"x_in{t}") for t in range(TT)]
    ada_in = [signal(f"ada_in{n}") for n in range(ADA_SLOTS)]
    h2_free = [signal(f"h2_free{n}") for n in range(2)]
    w1, w2 = i["w1"][0], i["w2"][0]
    out_k, out_v, out_u = o["new_k_prompt"][0, 0], o["new_v_prompt"][0, 0], o["new_pool_prompt"][0, 0]
    sk, sv, su = o["new_k_sample"][0], o["new_v_sample"][0], o["new_pool_sample"][0]
    ck, cv = i["cache_k"][0], i["cache_v"][0]
    ADA = 24
    CHUNKS = ADA // 2
    WHOLE = 8
    ada_bank = [bank[2 + c % 2] if c < 4 else bank[2] for c in range(CHUNKS)]

    def tok(t):
        return slice(t * P, t * P + ROWS[t])

    def load_unit(sp, e, u):
        if u < W1_UNITS:
            j = u // 4
            for kk in range(2):
                k = 2 * (u % 4) + kk
                src = w1[ds(e), k * P:(k + 1) * P, :].rearrange("e p (h c) -> p (e h) c", h=2)
                sp.dma_start(m.raw[:, u, kk * D:(kk + 1) * D].rearrange("p (h c) -> p h c", h=2),
                             src[:, :, j * 512:(j + 1) * 512]).then_inc(m.raw_in[u], 16)
        else:
            f = 2 * (u - W1_UNITS)
            src = w2[ds(e), f * P:(f + 2) * P, :].rearrange("e (k p) n -> p (e k) n", k=2)
            sp.dma_start(m.raw[:, u, :].rearrange("p (k n) -> p k n", k=2), src).then_inc(m.raw_in[u], 16)

    m.load_unit = load_unit

    with nc.Block() as block:

        @block.sync
        def _(sp):
            sp.dma_start(m.crow[0:NS, :], i["c_sample"]).then_inc(s.c_in, 16)
            sp.dma_start(m.crow[NS:NS + 1, :], i["c_prompt"]).then_inc(s.c_in, 16)

            def load_x(t):
                src = i["x_prompt"][0, tok(t), :] if t < TP else i["x_sample"].rearrange("b t d -> (b t) d")
                sp.dma_start(m.xs[0:ROWS[t], t, :], src).then_inc(x_in[t], 16)

            def load_ada(n):
                c, half = n // 2, n % 2
                if n >= ADA_SLOTS:
                    sp.wait_ge(s.ada_used, n - ADA_SLOTS + 1)
                src = i["w_ada"][0, half * 512:(half + 1) * 512, c * 512:(c + 1) * 512]
                sp.dma_start(m.raw[:, n % ADA_SLOTS, :].rearrange("p (k n) -> p k n", k=4),
                             src.rearrange("(k p) n -> p k n", p=P)).then_inc(ada_in[n % ADA_SLOTS], 16)

            def load_bada(q):
                sp.dma_start(m.bada[:], i["b_ada"][0:1, q * D:(q + 1) * D].to_broadcast([9, D])
                             ).then_inc(s.bada_in, 16)

            def store_mod(c):
                k, half = (c - 4) // 2, c % 2
                sp.wait_ge(s.mr_ready, c + 1)
                if c > 4:
                    sp.wait_ge(s.mod_out, 16 * (c - 4))
                sp.dma_start(m.modd[k, :, half * 512:half * 512 + 512], m.mrow[:, c % 2, :]).then_inc(s.mod_out, 16)

            for n in range(ADA_SLOTS):
                load_ada(n)
                load_x(n)
            for t in range(ADA_SLOTS, TT):
                load_x(t)
            sp.wait_ge(s.c_tr, 1)
            load_bada(0)
            for n in range(ADA_SLOTS, ADA):
                load_ada(n)
                if n == 7:
                    sp.dma_start(m.w_in[:], i["w_in"][0].rearrange("(k p) n -> p k n", p=P)).then_inc(s.win_in, 16)
                if n % 4 == 2:
                    sp.wait_ge(s.mr_ready, n // 2 - 1)
                    load_bada(n // 4)
                if n in (12, 14, 16, 18):
                    if n == 12:
                        sp.wait_ge(s.z_ready, TT)
                        sp.wait_ge(s.u_ready, 4)
                    k = n - 12
                    sp.dma_start(m.w_out[:, k:k + 2, :],
                                 i["w_out"][0, k * P:(k + 2) * P, :].rearrange("(k p) n -> p k n", p=P)
                                 ).then_inc(s.wout_in, 16)
                if n >= 14 and n % 2 == 0:
                    store_mod(n // 2 - 3)
            sp.wait_ge(s.bb_out, 32)
            sp.wait_ge(s.mod_out, 32)

            def load_bc(k, dst):
                sp.dma_start(dst[:], m.modd[k, NS:NS + 1, :].to_broadcast([P, D])).then_inc(s.bc_in, 16)

            sp.wait_ge(s.ada_used, ADA)
            load_bc(0, m.gm_bc)
            store_mod(9)
            store_mod(10)
            sp.wait_ge(s.mod_out, 16 * 7)
            load_bc(2, m.g2_bc)
            load_bc(1, m.s2_bc)
            store_mod(11)
            for u in range(ADA_SLOTS):
                load_unit(sp, 0, u)
            sp.wait_ge(s.pms_ready, 1)
            sp.wait_ge(s.dTs_ready, 4)
            sp.wait_ge(s.bias64_tr, 1)
            load_unit(sp, 0, 3)
            sp.wait_ge(s.skew_out, 16)
            sp.wait_ge(s.mr_ready, CHUNKS)
            load_unit(sp, 0, 4)
            load_unit(sp, 0, 5)
            sp.wait_ge(s.s_pv, 1)
            load_unit(sp, 0, 6)
            sp.wait_ge(s.ur_ready, 1)
            sp.dma_start(out_u, m.ulast[:]).then_inc(s.ulast_out, 16)

            def store_rows(t):
                sp.wait_ge(s.h2_ready, t + 1)
                sp.dma_start(m.h2d[tok(t), :], m.h2[0:ROWS[t], t % 2, :]).then_inc(h2_free[t % 2], 16)
                sp.dma_start(y_rows(o, t), m.xs[0:ROWS[t], t, :]).then_inc(s.x1_out, 16)

            for t in range(3):
                store_rows(t)
            sp.wait_ge(s.xo_ready, TT)
            for u in range(7, UNITS):
                load_unit(sp, 0, u)
            for t in range(3, TT):
                store_rows(t)
            sp.wait_ge(s.ulast_out, 16)
            sp.wait_ge(s.x1_out, TT * 16)
            sp.wait_ge(h2_free[0], 3 * 16)
            sp.wait_ge(h2_free[1], 2 * 16)

        @block.gpsimd
        def _(gp):
            gp.memset(m.ident[:], 0.0).then_inc(s.pad_ready, 1)
            gp.wait_ge(s.pad_ready, 1)
            gp.affine_select(out=m.ident[:], in_=m.ident[:], compare_op=ALU.not_equal, fill=1.0, base=0,
                             pattern=[[-1, P]], channel_multiplier=1).then_inc(s.ident_ready, 1)
            gp.wait_ge(s.ident_ready, 1)
            gp.memset(m.relb[NE:NE + 1, :], 1.0).then_inc(s.pad_ready, 1)
            for dst, src in ((m.relb[0:NE, :], i["rel_bias"]),
                             (m.rel64[0:NE], i["rel_bias"].unsqueeze(1).to_broadcast([NE, NS, NH])),
                             (m.rel64[NE:NE + 1], i["sinks"].unsqueeze(1).to_broadcast([1, NS, NH])),
                             (m.oh_line[:], i["oh_line"]), (m.oh_s[:], i["oh_s"]),
                             (m.sinks_bc[:], i["sinks"].to_broadcast([P, NH])),
                             (m.qn_bc[:], i["q_norm"].to_broadcast([P, HD])),
                             (m.kn_bc[:], i["k_norm"].to_broadcast([P, HD])),
                             (m.br_bc[:], i["b_router"].to_broadcast([P, NE])),
                             (m.rec[:].rearrange("p g c -> p (g c)"),
                              i["rec"].rearrange("g c -> (g c)").unsqueeze(0).to_broadcast([P, 4 * (BUF + 1)])),
                             (m.w_pool[:], i["w_pool"][0].rearrange("g k n -> k g n")),
                             (m.sp[:], i["state_pool"][0].rearrange("b t c -> (b t) c"))):
                gp.dma_start(dst, src).then_inc(s.small_in, 16)
            gp.wait_ge(s.pad_ready, 2)
            gp.memset(m.U[:, :, 0:BUF], 0.0).then_inc(s.pad_ready, 1)
            gp.wait_ge(s.pad_ready, 3)
            gp.memset(m.zero[:], 0.0).then_inc(s.zeros_ready, 1)
            gp.wait_ge(s.zeros_ready, 1)
            gp.memset(m.tab[:, :, 0], OOB).then_inc(s.tab_init, 1)
            gp.wait_ge(s.tab_init, 1)
            gp.memset(m.tab[:, :, 1], 0).then_inc(s.tab_init, 1)
            gp.wait_ge(s.tab_init, 2)
            gp.dma_start(m.tabd, m.tab[:].rearrange("p c w -> p (c w)")).then_inc(s.tab_out, 16)
            gp.wait_ge(s.win_in, 16)
            gp.dma_start(m.bb[:, 0:2 * D], i["b1"][0]).then_inc(s.bb_in, 16)
            gp.dma_start(m.bb[:, 2 * D:3 * D], i["b2"][0]).then_inc(s.bb_in, 16)
            for t in range(TT):
                gp.dma_start(m.yd[tok(t), :], m.zero[0:ROWS[t], :]).then_inc(s.zero_out, 16)
            gp.dma_start(sk[:, 0:P - 1], ck[:, 1:P]).then_inc(s.new_out, 16)
            gp.dma_start(sv[:, 0:P - 1], cv[:, 1:P]).then_inc(s.new_out, 16)
            gp.dma_start(su[:, 0:BUF - 1], i["state_pool"][0, :, 1:BUF]).then_inc(s.new_out, 16)
            gp.wait_ge(s.line_ready, NH)
            gp.dma_start(m.skew.rearrange("h (p n) -> p h n", n=LINE), m.line[:]).then_inc(s.skew_out, 16)
            gp.dma_start(m.Kc[:], ck.rearrange("b j g d -> j b (g d)")).then_inc(s.kv_in, 16)
            gp.dma_start(m.Vc[:], cv.rearrange("b j g d -> j b (g d)")).then_inc(s.kv_in, 16)
            gp.wait_ge(s.skew_out, 16)
            gp.wait_ge(s.x_tr, 2 * TT)
            for h in range(NH):
                src = m.skew[h, P - 1:P - 1 + P * (LINE - 1)].rearrange("(p n) -> p n", n=LINE - 1)
                gp.dma_start(m.bias[:, h, :], src[:, 0:2 * P]).then_inc(s.bias_in, 16)
            gp.wait_ge(s.bb_lo_done, 1)
            gp.dma_start(m.bd[:, 0, :], m.bb_hi[:]).then_inc(s.bb_out, 16)
            gp.dma_start(m.bd[:, 1, :], m.bb_lo[:]).then_inc(s.bb_out, 16)
            gp.wait_ge(s.bb_out, 32)
            gp.dma_start(m.nf[:], i["norm_ffn"].to_broadcast([9, D])).then_inc(s.nf_in, 16)
            gp.wait_ge(s.kv_in, 32)
            gp.wait_ge(s.qk_ready, TT)
            gp.wait_ge(s.vt_ready, TT)
            gp.dma_start(m.Kc[0:1, :, :], m.kn[0:NS, 1, :]).then_inc(s.newkv_in, 16)
            gp.dma_start(m.Vc[0:1, :, :], m.vt[0:NS, TP, :]).then_inc(s.newkv_in, 16)
            gp.dma_start(sk[:, P - 1].rearrange("b g d -> b (g d)"), m.kn[0:NS, 1, :]).then_inc(s.new_out, 16)
            gp.dma_start(sv[:, P - 1].rearrange("b g d -> b (g d)"), m.vt[0:NS, TP, :]).then_inc(s.new_out, 16)
            gp.dma_start(out_k.rearrange("t g d -> t (g d)"), m.kn[:, 0, :]).then_inc(s.new_out, 16)
            gp.dma_start(out_v.rearrange("t g d -> t (g d)"), m.vt[:, TP - 1, :]).then_inc(s.new_out, 16)
            gp.wait_ge(s.us_rows, 1)
            gp.dma_start(su[:, BUF - 1], m.uslast[:]).then_inc(s.new_out, 16)
            gp.wait_ge(s.qk_tr, TT)
            gp.wait_ge(s.small_in, 12 * 16)
            n = 0
            for g, w in enumerate(WINDOWS):
                gp.wait_ge(s.U_ready, g + 1)
                src = m.U[:, g, :]
                step, k = 1, 0
                while step < w:
                    dst = (m.la, m.lb)[k % 2]
                    lo_ = 2 * step - 1
                    if n:
                        gp.wait_ge(s.pool_step, n)
                    if g:
                        gp.wait_ge(s.pooled, g)
                    gp.tensor_tensor(dst[:, lo_:], src[:, lo_:], src[:, lo_ - step:BUF + SEQ - step],
                                     ALU.add).then_inc(s.pool_step, 1)
                    n += 1
                    src, step, k = dst, 2 * step, k + 1
                gp.wait_ge(s.pool_step, n)
                gp.tensor_scalar(src[:, 2 * BUF + 1:], src[:, 2 * BUF + 1:], 1.0 / w, None,
                                 ALU.mult).then_inc(s.pool_step, 1)
                gp.wait_ge(s.pool_step, n + 1)
                gp.tensor_tensor(src[:, BUF:2 * BUF + 1], src[:, BUF:2 * BUF + 1], m.rec[:, g, :],
                                 ALU.mult).then_inc(s.pool_step, 1)
                n += 2
                gp.wait_ge(s.pool_step, n)
                if g:
                    gp.wait_ge(s.pm_ready, g)
                gp.tensor_tensor(m.dT[:], src[:, BUF:], m.U[:, g, BUF:], ALU.subtract).then_inc(s.pooled, 1)
            gp.wait_ge(s.pooled, 4)
            gp.wait_ge(s.ur_tr, 1)
            gp.wait_ge(s.new_out, 8 * 16)
            gp.memset(m.ones_b[:], 1.0).then_inc(s.r_init, 1)
            gp.wait_ge(s.r_init, 1)
            gp.memset(m.tri[:], 1.0).then_inc(s.r_init, 1)
            gp.wait_ge(s.r_init, 2)
            gp.affine_select(out=m.tri[:], in_=m.tri[:], compare_op=ALU.is_gt, fill=0.0, base=0,
                             pattern=[[1, P]], channel_multiplier=-1).then_inc(s.r_init, 1)
            gp.wait_ge(s.r_init, 3)
            gp.iota(m.iota_e[:], pattern=[[1, NE]], base=0, channel_multiplier=0,
                    allow_small_or_imprecise_dtypes=True).then_inc(s.r_init, 1)
            gp.wait_ge(s.r_init, 4)
            gp.iota(m.tok_no[:], pattern=[[P, TT]], base=0, channel_multiplier=1).then_inc(s.r_init, 1)
            gp.wait_ge(s.r_init, 5)
            gp.iota(m.iota_o[:], pattern=[[1, NOVER + 1]], base=0, channel_multiplier=0,
                    allow_small_or_imprecise_dtypes=True).then_inc(s.r_init, 1)
            gp.wait_ge(s.r_init, 6)
            gp.iota(m.iota_c[:], pattern=[[NE, NOVER + 1]], base=NE - (TCOL - 1), channel_multiplier=0,
                    allow_small_or_imprecise_dtypes=True).then_inc(s.r_init, 1)
            gp.wait_ge(s.r_init, 7)
            gp.iota(m.eid[:], pattern=[[1, NCOL + 1]], base=-1, channel_multiplier=0).then_inc(s.r_init, 1)
            gp.wait_ge(s.r_init, 8)
            gp.iota(m.cols[:], pattern=[[1, NCOL]], base=-1, channel_multiplier=0).then_inc(s.r_init, 1)
            gp.wait_ge(s.r_init, 9)
            gp.memset(m.cols[:, 0:1], TCOL - 1).then_inc(s.r_init, 1)
            gp.wait_ge(s.r_init, 10)
            gp.memset(m.mask[:], 0.0).then_inc(s.r_init, 1)
            gp.wait_ge(s.r_init, 11)
            gp.memset(m.zero_e[:], 0.0).then_inc(s.r_init, 1)
            gp.wait_ge(s.r_init, 12)
            gp.tensor_copy(m.pay[:, :, :, 0], m.tok_no[:].unsqueeze(2).to_broadcast([P, TT, TOPK])
                           ).then_inc(s.r_init, 1)
            gp.wait_ge(s.mod_out, 8 * 16)
            gp.wait_ge(s.sc_used, 4 * TP)
            gp.wait_ge(s.pm_ready, 4)
            for v, dst in ((0, m.gm_s), (2, m.g2_s), (1, m.s2_s)):
                gp.dma_start(dst[:], m.modd[v, 0:NS, :]).then_inc(s.bcs_in, 16)
            gp.dma_start(m.w_router[:], i["w_router"][0].rearrange("(k p) n -> p k n", p=P)).then_inc(s.wr_in, 16)
            gp.wait_ge(s.tab_out, 16)
            places = m.tabd.rearrange("p (c w) -> (p c) w", w=2)
            for t in range(TT):
                gp.wait_ge(s.dest_ready, t + 1)
                gp.wait_ge(s.pay_ready, t + 1)
                for k in range(TOPK):
                    gp.indirect_dma_start(places, bass.IndirectOffsetOnAxis(ap=m.dest[0:ROWS[t], t, k:k + 1], axis=0),
                                          m.pay[0:ROWS[t], t, k, :], None).then_inc(s.scattered, 16)
            gp.wait_ge(s.scattered, TT * TOPK * 16)
            gp.dma_start(m.tab[:].rearrange("p c w -> p (c w)"), m.tabd).then_inc(s.tab_in, 16)
            gp.wait_ge(s.tab_in, 16)
            gp.wait_ge(s.zero_out, TT * 16)
            gp.wait_ge(s.bb_out, 32)

        @block.scalar
        def _(act):
            for r, name, n in ((0, "norm_mix", 8), (8, "pool_scale", 4)):
                act.dma_start(m.vrow[r:r + n, :], i[name][0].rearrange("(a b) -> a b", b=P)).then_inc(s.vecs_in, 16)
            act.wait_ge(s.c_in, 32)
            nc.scalar.activation(m.crow[:], m.crow[:], ACT.Silu).then_inc(s.c_act, 1)

            def norm_x(t):
                R = ROWS[t]
                act.wait_ge(x_in[t], 16)
                if t >= 2:
                    act.wait_ge(s.x_tr, 2 * t - 2)
                if t:
                    act.wait_ge(s.xn_ready, t)
                nc.scalar.activation(m.xn[0:R, t % 2, :], m.xs[0:R, t, :], ACT.Square,
                                     accum_out=m.ssq[0:R, t:t + 1]).then_inc(s.ssq_ready, 1)
                act.wait_ge(s.ssq_ready, t + 1)
                act.wait_ge(s.eps_ready, 1)
                nc.scalar.activation(m.rstd[0:R, t:t + 1], m.ssq[0:R, t:t + 1], ACT.Sqrt, scale=1.0 / D,
                                     bias=m.eps[0:R, :]).then_inc(s.rms_ready, 1)
                act.wait_ge(s.rstd_ready, t + 1)
                nc.scalar.activation(m.xn[0:R, t % 2, :], m.xs[0:R, t, :], ACT.Copy,
                                     scale=m.rstd[0:R, t:t + 1]).then_inc(s.xn_ready, 1)

            def take_x(t):
                act.wait_ge(s.x_tr, 2 * t + 1)
                R = ROWS[t]
                nc.scalar.copy(m.hT[:, 0:4, tok(t)],
                               bank[0][:].rearrange("p (k n) -> p k n", k=4)[:, :, 0:R]).then_inc(s.xT_act, 1)

            for t in range(TT):
                norm_x(t)
                if t:
                    take_x(t - 1)
            take_x(TP)
            act.wait_ge(s.bb_in, 32)
            nc.scalar.copy(m.bb_hi[:], m.bb[:]).then_inc(s.bb_hi_done, 1)
            def take_qT(t):
                act.wait_ge(s.qk_tr, t + 1)
                if not t:
                    act.wait_ge(s.zero_out, TT * 16)
                nc.scalar.copy(m.qT[:, :, tok(t)],
                               bank[0][:].rearrange("p (k n) -> p k n", k=4)[:, :, 0:ROWS[t]]).then_inc(s.qT_ready, 1)

            for t in range(TT):
                R, zq, zk = ROWS[t], bank[4 + 2 * (t % 2)], bank[5 + 2 * (t % 2)]
                act.wait_ge(s.z_ready, t + 1)
                if t:
                    act.wait_ge(s.hss_ready, t)
                nc.scalar.activation(m.sq[0:R, 0:512], zq[0:R, :], ACT.Square).then_inc(s.sq_ready, 1)
                nc.scalar.activation(m.sq[0:R, 512:640], zk[0:R, 0:KVW], ACT.Square).then_inc(s.sq_ready, 1)
                nc.scalar.copy(m.vt[0:R, t, :], zk[0:R, KVW:2 * KVW]).then_inc(s.vt_ready, 1)
                act.wait_ge(s.hss_ready, t + 1)
                if t:
                    act.wait_ge(s.qk_ready, t)
                nc.scalar.activation(m.hrs[0:R, :], m.hss[0:R, :], ACT.Sqrt, scale=1.0 / HD,
                                     bias=m.eps[0:R, :]).then_inc(s.hrms_ready, 1)
                if t:
                    take_qT(t - 1)
            take_qT(TP)
            for g in range(4):
                act.wait_ge(s.u_ready, g + 1)
                if not g:
                    act.wait_ge(s.pad_ready, 3)
                nc.scalar.copy(m.U[:, g, BUF:], bank[4 + g][:]).then_inc(s.U_ready, 1)

            def exps(t):
                act.wait_ge(s.sm_ready, t + 1)
                if t:
                    act.wait_ge(s.o_ready, t)
                c0 = 0 if t else P
                for h in range(NH):
                    e = nc.scalar.activation(m.Pb[:, h, c0:], m.Pb[:, h, c0:], ACT.Exp, bias=m.negm[:, h:h + 1],
                                             accum_out=m.den[:, h:h + 1])
                    if h % 2:
                        e.then_inc(s.p_ready, 1)
                nc.scalar.activation(m.esink[:], m.esink[:], ACT.Exp).then_inc(s.e_ready, 1)

            def split_ada(n):
                if n < ADA:
                    act.wait_ge(ada_in[n % ADA_SLOTS], 16 * (n // ADA_SLOTS + 1))
                    if n < WHOLE + 2:
                        act.wait_ge(s.dTs_ready, 4)
                        act.wait_ge(s.skew_out, 16)
                    else:
                        act.wait_ge(s.ada_used, n - 1)
                    nc.scalar.copy(m.whi[:, n % 2, :], m.raw[:, n % ADA_SLOTS, :]).then_inc(s.ada_hi, 1)

            def take_PT(t, pairs):
                for j in pairs:
                    act.wait_ge(s.pt_tr, 4 * t + j + 1)
                    if 4 * t + j >= 2:
                        act.wait_ge(s.pv_done, 4 * t + j - 1)
                    if t:
                        nc.scalar.copy(m.PT[:, j % 2, :], bank[j % 2][:]).then_inc(s.pt_ev, 1)
                    else:
                        nc.scalar.copy(m.PT[:, j % 2, :].rearrange("p (a b n) -> p a b n", a=2, b=2)[:, :, 1, :],
                                       bank[j % 2][:].rearrange("p (a b n) -> p a b n", a=2, b=2)[:, :, 1, :]
                                       ).then_inc(s.pt_ev, 1)

            def take_attn(t):
                act.wait_ge(s.at_tr, t + 1)
                nc.scalar.copy(m.mixT[:, 0:4, tok(t)],
                               bank[3][:].rearrange("p (k n) -> p k n", k=4)).then_inc(s.at_ev, 1)

            split_ada(WHOLE)
            for t in range(TP):
                n = WHOLE + 4 * t
                exps(t)
                split_ada(n + 1)
                if t:
                    take_attn(t - 1)
                take_PT(t, (0, 1))
                split_ada(n + 2)
                take_PT(t, (2, 3))
                act.wait_ge(s.pm_ready, t + 1)
                nc.scalar.activation(m.mixT[:, 4 + t, 0:SEQ], bank[2][:], ACT.Copy,
                                     scale=m.vecsT[:, 8 + t:9 + t]).then_inc(s.pm_done, 1)
                split_ada(n + 3)
                split_ada(n + 4)
            take_attn(TP - 1)
            act.wait_ge(s.pms_ready, 1)
            for g in range(4):
                nc.scalar.activation(m.mixT[:, 4 + g, SEQ:TOK], bank[2][:, g * NS:(g + 1) * NS], ACT.Copy,
                                     scale=m.vecsT[:, 8 + g:9 + g]).then_inc(s.pms_done, 1)

            def squares(t):
                R = ROWS[t]
                act.wait_ge(s.x1_ready, t + 1)
                if t:
                    act.wait_ge(s.ss2_ready, t)
                nc.scalar.activation(m.junk[0:R, :], m.xs[0:R, t, :], ACT.Square,
                                     accum_out=m.ss2[0:R, t:t + 1]).then_inc(s.ss2_ready, 1)
                act.wait_ge(s.ss2_ready, t + 1)
                nc.scalar.activation(m.rs2[0:R, t:t + 1], m.ss2[0:R, t:t + 1], ACT.Sqrt, scale=1.0 / D,
                                     bias=m.eps[0:R, :]).then_inc(s.rms2_ready, 1)

            def take_h2T(t):
                for half in range(2):
                    act.wait_ge(s.h2_tr, 2 * t + half + 1)
                    if t and not half:
                        act.wait_ge(s.rt_ready, t)
                    nc.scalar.copy(m.h2T[:, 4 * half:4 * half + 4, 0:ROWS[t]],
                                   bank[half][:].rearrange("p (k n) -> p k n", k=4)[:, :, 0:ROWS[t]]
                                   ).then_inc(s.h2T_ready, 1)

            def gate_exps(t):
                act.wait_ge(s.gate_in, t + 1)
                nc.scalar.activation(m.gates[0:ROWS[t], t, :], m.gates[0:ROWS[t], t, :], ACT.Exp,
                                     accum_out=m.gsum[0:ROWS[t], t:t + 1]).then_inc(s.gate_exp, 1)

            squares(0)
            act.wait_ge(s.s_step, 2)
            nc.scalar.activation(m.P64[:], m.P64[:], ACT.Exp, bias=m.s64[:, 1:2],
                                 accum_out=m.s64[:, 2:3]).then_inc(s.s_exp, 1)
            act.wait_ge(s.s_step, 3)
            nc.scalar.activation(m.s64[:, 3:4], m.s64[:, 3:4], ACT.Exp).then_inc(s.s_exp, 1)
            for t in range(1, TP):
                take_h2T(t - 1)
                squares(t)
                if t >= 2:
                    gate_exps(t - 2)
            take_h2T(3)
            gate_exps(2)
            gate_exps(3)
            squares(TP)
            take_h2T(TP)
            gate_exps(TP)

        @block.vector
        def _(v):
            steps = [0]

            def step(ins):
                ins.then_inc(s.vector_step, 1)
                steps[0] += 1
                v.wait_ge(s.vector_step, steps[0])

            v.memset(m.eps[:], EPS).then_inc(s.eps_ready, 1)
            v.wait_ge(s.vecs_tr, 1)
            v.tensor_copy(m.vecsT[:], bank[7][:, 0:12]).then_inc(s.vecs_ready, 1)
            v.wait_ge(s.c_tr, 1)
            v.tensor_copy(m.cT[:].rearrange("p k n -> p (k n)"), bank[6][:, 0:72]).then_inc(s.cT_ready, 1)
            def mod_row(c):
                v.wait_ge(s.ada_used, 2 * c + 2)
                v.wait_ge(s.bada_in, 16 * (c // 2 + 1))
                if c >= 2:
                    if c < 6:
                        v.wait_ge(s.mt_tr, c - 1)
                    else:
                        v.wait_ge(s.mod_out, 16 * (c - 5))
                added = v.tensor_tensor(m.mrow[:, c % 2, :], ada_bank[c][0:9, :], m.bada[:, c % 2 * 512:c % 2 * 512 + 512],
                                        ALU.add)
                if c >= WHOLE // 2:
                    step(added)
                    added = v.tensor_tensor(m.mrow[:, c % 2, :], m.mrow[:, c % 2, :], ada_bank[c][32:41, :], ALU.add)
                if c in (8, 9):
                    step(added)
                    v.wait_ge(s.nf_in, 16)
                    added = v.scalar_tensor_tensor(m.mrow[:, c % 2, :], m.mrow[:, c % 2, :], 1.0,
                                                   m.nf[:, c % 2 * 512:c % 2 * 512 + 512], ALU.add, ALU.mult)
                added.then_inc(s.mr_ready, 1)

            for t in range(TT):
                R = ROWS[t]
                v.wait_ge(s.rms_ready, t + 1)
                v.reciprocal(m.rstd[0:R, t:t + 1], m.rstd[0:R, t:t + 1]).then_inc(s.rstd_ready, 1)
                if t:
                    v.wait_ge(s.x_tr, 2 * t)
                    v.tensor_copy(m.hT[:, 4:8, tok(t - 1)],
                                  bank[1][:].rearrange("p (k n) -> p k n", k=4)).then_inc(s.xT_dve, 1)
                if t in (2, TP):
                    mod_row(t // 2 - 1)
            v.wait_ge(s.x_tr, 2 * TT)
            v.tensor_copy(m.hT[:, 4:8, tok(TP)],
                          bank[1][:].rearrange("p (k n) -> p k n", k=4)[:, :, 0:NS]).then_inc(s.xT_dve, 1)
            v.wait_ge(s.small_in, 12 * 16)
            v.wait_ge(s.pad_ready, 2)
            v.tensor_copy(m.relrep[:], m.relb[:].unsqueeze(2).to_broadcast([NE + 1, NH, P])).then_inc(s.rel_ready, 1)
            mod_row(2)
            for h in range(NH):
                v.wait_ge(s.line_tr, h + 1)
                if not h:
                    v.wait_ge(s.c_tr, 1)
                v.tensor_copy(m.line[:, h, :], bank[4 + h % 2][:, 0:LINE]).then_inc(s.line_ready, 1)
            v.wait_ge(s.bias64_tr, 1)
            v.tensor_copy(m.bias64[:], bank[6][0:64, 0:P + 1]).then_inc(s.bias64_ready, 1)
            mod_row(3)
            v.wait_ge(s.mt_tr, 4)
            v.tensor_copy(m.modT[:].rearrange("p c n -> p (c n)"), bank[7][:, 0:144]).then_inc(s.modT_ready, 1)
            v.wait_ge(s.modT_ready, 1)
            v.wait_ge(s.vecs_ready, 1)
            v.scalar_tensor_tensor(m.g1T[:], m.modT[:, 8:16, :], 1.0,
                                   m.vecsT[:, 0:8].unsqueeze(2).to_broadcast([P, 8, 9]),
                                   ALU.add, ALU.mult).then_inc(s.g1_ready, 1)
            v.wait_ge(s.g1_ready, 1)
            v.wait_ge(s.xT_act, TT)
            v.wait_ge(s.xT_dve, TT)
            v.tensor_tensor(m.hT[:, :, SEQ:TOK], m.hT[:, :, SEQ:TOK], m.g1T[:, :, 0:NS],
                            ALU.mult).then_inc(s.hT_half, 1)
            for k in range(KC):
                v.tensor_scalar(m.hT[:, k, 0:SEQ], m.hT[:, k, 0:SEQ], m.g1T[:, k, 8:9], m.modT[:, k, 8:9],
                                ALU.mult, ALU.add).then_inc(s.h_ready, 1)
            v.wait_ge(s.hT_half, 1)
            v.tensor_tensor(m.hT[:, :, SEQ:TOK], m.hT[:, :, SEQ:TOK], m.modT[:, 0:8, 0:NS],
                            ALU.add).then_inc(s.h_ready, 1)
            v.wait_ge(s.bb_hi_done, 1)
            v.tensor_tensor(m.bb_lo[:], m.bb[:], m.bb_hi[:].bitcast(F32), ALU.subtract).then_inc(s.bb_lo_done, 1)
            def take_kT(t):
                v.wait_ge(s.qk_tr, t + 1)
                v.tensor_copy(m.kT[:, :, tok(t)], bank[1][:, 0:2 * P].rearrange("p (k n) -> p k n", k=2)
                              [:, :, 0:ROWS[t]]).then_inc(s.kT_ready, 1)

            for t in range(TT):
                R, zq, zk = ROWS[t], bank[4 + 2 * (t % 2)], bank[5 + 2 * (t % 2)]
                v.wait_ge(s.sq_ready, 2 * t + 2)
                if t:
                    v.wait_ge(s.hrs_ready, t)
                v.tensor_reduce(m.hss[0:R, :], m.sq[0:R, :].rearrange("p (h d) -> p h d", d=HD), AX_X,
                                ALU.add).then_inc(s.hss_ready, 1)
                v.wait_ge(s.hrms_ready, t + 1)
                v.reciprocal(m.hrs[0:R, :], m.hrs[0:R, :]).then_inc(s.hrs_ready, 1)
                v.wait_ge(s.hrs_ready, t + 1)
                if t:
                    v.wait_ge(s.qk_tr, t)
                v.tensor_tensor(m.qn[0:R, :].rearrange("p (h d) -> p h d", d=HD),
                                zq[0:R, :].rearrange("p (h d) -> p h d", d=HD),
                                m.hrs[0:R, 0:NH].unsqueeze(2).to_broadcast([R, NH, HD]), ALU.mult).then_inc(s.qn_raw, 1)
                keys = m.kn[0:R, t // TP, :].rearrange("p (g d) -> p g d", d=HD)
                v.tensor_tensor(keys, zk[0:R, 0:KVW].rearrange("p (g d) -> p g d", d=HD),
                                m.hrs[0:R, NH:].unsqueeze(2).to_broadcast([R, NKV, HD]), ALU.mult).then_inc(s.kn_raw, 1)
                v.wait_ge(s.qn_raw, t + 1)
                v.tensor_tensor(m.qn[0:R, :].rearrange("p (h d) -> p h d", d=HD),
                                m.qn[0:R, :].rearrange("p (h d) -> p h d", d=HD),
                                m.qn_bc[0:R, :].unsqueeze(1).to_broadcast([R, NH, HD]), ALU.mult)
                v.wait_ge(s.kn_raw, 2 * t + 1)
                v.tensor_tensor(keys, keys, m.kn_bc[0:R, :].unsqueeze(1).to_broadcast([R, NKV, HD]),
                                ALU.mult).then_inc(s.kn_raw, 1)
                v.wait_ge(s.kn_raw, 2 * t + 2)
                v.tensor_copy(m.kd[0:R, :, 0, :], keys)
                v.tensor_copy(m.kd[0:R, :, 1, :], keys).then_inc(s.qk_ready, 1)
                if t:
                    take_kT(t - 1)
            v.wait_ge(s.z_ready, TT)
            v.tensor_copy(m.uslast[:], bank[3][0:NS, :]).then_inc(s.us_rows, 1)
            take_kT(TP)
            v.wait_ge(s.us_tr, 1)
            v.tensor_copy(m.Us[:].rearrange("p g n -> p (g n)"), bank[3][:, 0:4 * NS]).then_inc(s.Us_ready, 1)
            v.wait_ge(s.sp_tr, 1)
            v.tensor_copy(m.spT[:].rearrange("p g b t -> p g (b t)"),
                          bank[0][:, 0:480].rearrange("p (g n) -> p g n", g=4)).then_inc(s.spT_ready, 1)
            v.wait_ge(s.spT_ready, 1)
            for g, w in enumerate(WINDOWS):
                v.tensor_reduce(m.dTs[:, g, :], m.spT[:, g, :, BUF + 1 - w:], AX_X, ALU.add).then_inc(s.spool_step, 1)
            v.wait_ge(s.spool_step, 4)
            v.wait_ge(s.Us_ready, 1)
            v.tensor_tensor(m.dTs[:], m.dTs[:], m.Us[:], ALU.add).then_inc(s.spool_step, 1)
            v.wait_ge(s.spool_step, 5)
            for g, w in enumerate(WINDOWS):
                v.scalar_tensor_tensor(m.dTs[:, g, :], m.dTs[:, g, :], 1.0 / w, m.Us[:, g, :], ALU.mult,
                                       ALU.subtract).then_inc(s.dTs_ready, 1)
            v.wait_ge(s.bb_out, 32)
            step(v.memset(m.c2[:].bitcast(F32), 0.0))
            step(v.tensor_copy(m.c2[:, :, 0:9], m.cT[:]))
            v.tensor_tensor(m.c2[:, :, 32:41], m.cT[:], m.c2[:, :, 0:9].bitcast(F32), ALU.subtract).then_inc(s.c2_ready, 1)

            def low_ada(n):
                if n < ADA:
                    v.wait_ge(s.ada_hi, n - WHOLE + 1)
                    v.tensor_tensor(m.wlo[:, n % ADA_SLOTS, :], m.raw[:, n % ADA_SLOTS, :],
                                    m.whi[:, n % 2, :].bitcast(F32), ALU.subtract).then_inc(s.ada_lo, 1)

            def scores(t, banks):
                c0 = 0 if t else P
                if not t and 0 in banks:
                    v.wait_ge(s.bias_in, NH * 16)
                for j in banks:
                    v.wait_ge(s.sc_ready, 4 * t + j + 1)
                    g, odd = j // 2, j % 2
                    heads = slice(4 * g + odd, 4 * g + odd + 3, 2)
                    if t:
                        v.wait_ge(s.pt_tr, 4 * (t - 1) + 2 * g + 2)
                    v.scalar_tensor_tensor(m.Pb[:, heads, c0:],
                                           bank[4 + j][:].rearrange("p (a n) -> p a n", a=2)[:, :, c0:],
                                           HD ** -0.5, m.bias[:, heads, c0:], ALU.mult,
                                           ALU.add).then_inc(s.sc_used, 1)

            def maxima(t):
                c0 = 0 if t else P
                v.wait_ge(s.sc_used, 4 * t + 4)
                step(v.tensor_reduce(m.m8[:], m.Pb[:, :, c0:], AX_X, ALU.max))
                step(v.tensor_tensor(m.m8[:], m.m8[:], m.sinks_bc[:], ALU.max))
                v.tensor_scalar(m.negm[:], m.m8[:], -1.0, None, ALU.mult)
                v.tensor_tensor(m.esink[:], m.sinks_bc[:], m.m8[:], ALU.subtract).then_inc(s.sm_ready, 1)

            def sums(t):
                v.wait_ge(s.e_ready, t + 1)
                step(v.tensor_tensor(m.den[:], m.den[:], m.esink[:], ALU.add))
                if t:
                    v.wait_ge(s.attn_ready, t)
                v.reciprocal(m.rden[:], m.den[:]).then_inc(s.o_ready, 1)

            def normed(t):
                v.wait_ge(s.o_ready, t + 1)
                v.wait_ge(s.pv_done, 4 * t + 4)
                if t:
                    v.wait_ge(s.at_tr, t)
                else:
                    v.wait_ge(s.new_out, 8 * 16)
                    v.wait_ge(s.us_tr, 1)
                v.tensor_tensor(m.attn[:].rearrange("p (h d) -> p h d", d=HD),
                                bank[3][:].rearrange("p (h d) -> p h d", d=HD),
                                m.rden[:].unsqueeze(2).to_broadcast([P, NH, HD]), ALU.mult).then_inc(s.attn_ready, 1)

            low_ada(WHOLE)
            scores(0, range(4))
            maxima(0)
            for t in range(TP):
                n = WHOLE + 4 * t
                low_ada(n + 1)
                if t + 1 < TP:
                    scores(t + 1, (0, 1))
                low_ada(n + 2)
                mod_row(2 * t + 4)
                if t + 1 < TP:
                    scores(t + 1, (2, 3))
                sums(t)
                if t + 1 < TP:
                    maxima(t + 1)
                low_ada(n + 3)
                normed(t)
                low_ada(n + 4)
                mod_row(2 * t + 5)
            for half in range(2):
                v.wait_ge(s.kc_tr, half + 1)
                v.tensor_copy(m.KcT[:, 4 * half:4 * half + 4, :].rearrange("p k n -> p (k n)"),
                              bank[4 + half][:]).then_inc(s.kcT_ready, 1)
            v.wait_ge(s.qT_ready, TT)
            for g in range(NKV):
                for q in range(GROUP):
                    src = 64 * (q % 2)
                    v.tensor_copy(m.qsT[64 * g:64 * g + 64, g, :, q],
                                  m.qT[src:src + 64, 2 * g + q // 2, SEQ:TOK]).then_inc(s.qs_ready, 1)
            v.wait_ge(s.s_sc, 1)
            for g in range(NKV):
                v.tensor_copy(m.sT[:].rearrange("p (b g q) -> p g b q", g=NKV, q=GROUP)[:, g],
                              bank[6 + g][:, 0:64].rearrange("p (b g q) -> p g b q", g=NKV, q=GROUP)[:, g]
                              ).then_inc(s.s_scT, 1)
            v.wait_ge(s.ur_tr, 1)
            v.wait_ge(s.mod_out, 8 * 16)
            v.tensor_copy(m.ulast[:], bank[0][0:BUF, :]).then_inc(s.ur_ready, 1)
            def sample_softmax():
                v.wait_ge(s.s_tr, 1)
                v.wait_ge(s.bias64_ready, 1)
                v.scalar_tensor_tensor(m.P64[:], bank[3][0:64, 0:P], HD ** -0.5, m.bias64[:, 0:P], ALU.mult,
                                       ALU.add).then_inc(s.s_soft, 1)
                v.wait_ge(s.s_soft, 1)
                v.tensor_reduce(m.s64[:, 0:1], m.P64[:], AX_X, ALU.max).then_inc(s.s_soft, 1)
                v.wait_ge(s.s_soft, 2)
                v.tensor_tensor(m.s64[:, 0:1], m.s64[:, 0:1], m.bias64[:, P:P + 1], ALU.max).then_inc(s.s_step, 1)
                v.wait_ge(s.s_step, 1)
                v.tensor_scalar(m.s64[:, 1:2], m.s64[:, 0:1], -1.0, None, ALU.mult).then_inc(s.s_step, 1)
                v.tensor_tensor(m.s64[:, 3:4], m.bias64[:, P:P + 1], m.s64[:, 0:1], ALU.subtract).then_inc(s.s_step, 1)
                v.wait_ge(s.s_exp, 2)
                v.tensor_tensor(m.s64[:, 2:3], m.s64[:, 2:3], m.s64[:, 3:4], ALU.add).then_inc(s.s_soft, 1)
                v.wait_ge(s.s_soft, 3)
                v.reciprocal(m.s64[:, 4:5], m.s64[:, 2:3]).then_inc(s.s_soft, 1)
                v.wait_ge(s.s_soft, 4)
                v.tensor_scalar(m.P64[:], m.P64[:], m.s64[:, 4:5], None, ALU.mult).then_inc(s.s_norm, 1)

            def sample_probs():
                v.wait_ge(s.s_ptr, 1)
                v.tensor_copy(m.PTs[:], bank[3][:, 0:64]).then_inc(s.s_pts, 1)

            def sample_rows():
                v.wait_ge(s.s_pv, 1)
                for half in range(2):
                    v.tensor_copy(m.mixT[64 * half:64 * half + 64, 0:4, SEQ:TOK],
                                  bank[3][0:64, 128:192].rearrange("p (b c a) -> p c b a", b=NS, a=2)[:, :, :, half]
                                  ).then_inc(s.s_mix, 1)

            def route(t):
                R = ROWS[t]
                v.wait_ge(s.rt_ready, t + 1)
                v.tensor_tensor(m.logits[0:R, t, :], bank[2][0:R, 0:NE], m.br_bc[0:R, :],
                                ALU.add).then_inc(s.logit_ready, 1)
                v.wait_ge(s.logit_ready, t + 1)
                step(v.max(m.v8[0:R, t, :], m.logits[0:R, t, :]))
                step(v.max_index(m.i8[0:R, t, :], m.v8[0:R, t, :], m.logits[0:R, t, :]))
                step(v.tensor_copy(m.idx[0:R, t, :], m.i8[0:R, t, 0:TOPK]))
                v.tensor_tensor(m.gates[0:R, t, :], m.v8[0:R, t, 0:TOPK], m.v8[0:R, t, 0:1].to_broadcast([R, TOPK]),
                                ALU.subtract).then_inc(s.gate_in, 1)
                step(v.tensor_tensor(m.ohk[0:R, t], m.iota_e[0:R, :].unsqueeze(1).to_broadcast([R, TOPK, NE]),
                                     m.idx[0:R, t, :].unsqueeze(2).to_broadcast([R, TOPK, NE]), ALU.is_equal))
                with nc.allow_low_precision("counts up to 1"):
                    v.tensor_reduce(m.mask[0:R, t, :], m.ohk[0:R, t].rearrange("p k e -> p e k"), AX_X,
                                    ALU.add).then_inc(s.mask_ready, 1)

            def place(t):
                R = ROWS[t]
                v.wait_ge(s.pos_ready, t + 1)
                pos, blk, flat = bank[3][0:R, t * NE:(t + 1) * NE], m.blk[0:R, t, :], m.flat[0:R, t, :]
                step(v.tensor_scalar(blk, pos, float(SL), None, ALU.is_ge))
                for j in range(2, BLOCKS):
                    step(v.scalar_tensor_tensor(blk, pos, float(j * SL), blk, ALU.is_ge, ALU.add))
                step(v.scalar_tensor_tensor(flat, blk, float(NE - SL * TCOL), m.iota_e[0:R, :], ALU.mult, ALU.add))
                step(v.scalar_tensor_tensor(flat, pos, float(TCOL), flat, ALU.mult, ALU.add))
                step(v.tensor_tensor(m.picked[0:R, t], m.ohk[0:R, t], flat.unsqueeze(1).to_broadcast([R, TOPK, NE]),
                                     ALU.mult))
                step(v.tensor_reduce(m.dest_f[0:R, t, :], m.picked[0:R, t], AX_X, ALU.add))
                v.tensor_copy(m.dest[0:R, t, :], m.dest_f[0:R, t, :]).then_inc(s.dest_ready, 1)
                v.wait_ge(s.gate_exp, t + 1)
                step(v.reciprocal(m.gsum[0:R, t:t + 1], m.gsum[0:R, t:t + 1]))
                v.tensor_tensor(m.pay[0:R].bitcast(F32)[:, t, :, 1], m.gates[0:R, t, :],
                                m.gsum[0:R, t:t + 1].to_broadcast([R, TOPK]), ALU.mult).then_inc(s.pay_ready, 1)

            def mixed(t):
                R = ROWS[t]
                gm, g2, s2 = (m.gm_bc, m.g2_bc, m.s2_bc) if t < TP else (m.gm_s, m.g2_s, m.s2_s)
                v.wait_ge(s.xo_ready, t + 1)
                if t in (0, TP):
                    v.wait_ge(s.bc_in if not t else s.bcs_in, 3 * 16)
                if t >= 2:
                    v.wait_ge(s.h2_tr, 2 * (t - 1))
                    v.wait_ge(h2_free[t % 2], 16 * (t // 2))
                for half in range(2):
                    cs = slice(512 * half, 512 * half + 512)
                    step(v.tensor_tensor(m.h2[0:R, t % 2, cs], bank[4 + 2 * (t % 2) + half][0:R, :], gm[0:R, cs],
                                         ALU.mult))
                v.tensor_tensor(m.xs[0:R, t, :], m.xs[0:R, t, :], m.h2[0:R, t % 2, :], ALU.add).then_inc(s.x1_ready, 1)
                v.wait_ge(s.rms2_ready, t + 1)
                v.reciprocal(m.rs2[0:R, t:t + 1], m.rs2[0:R, t:t + 1]).then_inc(s.rs2_ready, 1)
                v.wait_ge(s.rs2_ready, t + 1)
                step(v.scalar_tensor_tensor(m.h2[0:R, t % 2, :], m.xs[0:R, t, :], m.rs2[0:R, t:t + 1], g2[0:R, :],
                                            ALU.mult, ALU.mult))
                v.tensor_tensor(m.h2[0:R, t % 2, :], m.h2[0:R, t % 2, :], s2[0:R, :], ALU.add).then_inc(s.h2_ready, 1)

            mixed(0)
            sample_softmax()
            sample_probs()
            mixed(1)
            v.wait_ge(s.r_init, 13)
            route(0)
            sample_rows()
            for t in range(2, TP):
                mixed(t)
                route(t - 1)
                place(t - 2)
            route(3)
            place(2)
            place(3)
            mixed(TP)
            route(TP)
            place(TP)
            v.wait_ge(s.cnt_ready, 1)
            step(v.tensor_copy(m.cnt[:], bank[2][0:1, 192:192 + NE]))
            step(v.tensor_scalar(m.nov[:], m.cnt[:], float(SL), None, ALU.is_gt))
            for j in range(2, BLOCKS):
                step(v.scalar_tensor_tensor(m.nov[:], m.cnt[:], float(j * SL), m.nov[:], ALU.is_gt, ALU.add))
            step(v.tensor_tensor_scan(m.ends[:], m.nov[:], m.zero_e[:], 0.0, ALU.add, ALU.add))
            step(v.tensor_tensor(m.starts[:], m.ends[:], m.nov[:], ALU.subtract))
            over = m.iota_o[:].unsqueeze(2).to_broadcast([1, NOVER + 1, NE])
            step(v.tensor_tensor(m.behind[:], over, m.ends[:].unsqueeze(1).to_broadcast([1, NOVER + 1, NE]), ALU.is_ge))
            step(v.tensor_reduce(m.ovf[:, 0], m.behind[:], AX_X, ALU.add))
            v.tensor_scalar(m.eid[:, NE + 1:NE + 1 + NOVER + 1], m.ovf[:, 0], float(NE - 1), None, ALU.min)
            step(v.tensor_tensor(m.begun[:], over, m.starts[:].unsqueeze(1).to_broadcast([1, NOVER + 1, NE]), ALU.is_ge))
            step(v.tensor_tensor(m.begun[:], m.begun[:], m.behind[:], ALU.subtract))
            step(v.tensor_reduce(m.ovf[:, 1], m.begun[:], AX_X, ALU.add))
            step(v.scalar_tensor_tensor(m.starts[:], m.starts[:], -float(NE), m.iota_e[0:1, :], ALU.mult, ALU.add))
            step(v.tensor_tensor(m.begun[:], m.begun[:], m.starts[:].unsqueeze(1).to_broadcast([1, NOVER + 1, NE]),
                                 ALU.mult))
            step(v.tensor_reduce(m.ovf[:, 2], m.begun[:], AX_X, ALU.add))
            step(v.tensor_tensor(m.ovf[:, 1], m.ovf[:, 1], m.iota_c[:], ALU.mult))
            step(v.scalar_tensor_tensor(m.ovf[:, 1], m.ovf[:, 1], float(TCOL - 1), m.ovf[:, 2], ALU.add, ALU.add))
            v.tensor_copy(m.cols[:, NE + 1:NE + 1 + NOVER + 1], m.ovf[:, 1])
            v.tensor_copy(m.eid[:, NCOL:NCOL + 1], m.ends[:, NE - 1:NE]).then_inc(m.eid_ready, 1)

        @block.tensor
        def _(pe):
            mm, tr = nc.tensor.matmul, nc.tensor.transpose
            pe.wait_ge(s.ident_ready, 1)
            pe.wait_ge(s.vecs_in, 2 * 16)
            tr(bank[7][:, 0:12], m.vrow[:], m.ident[0:12, 0:12]).then_inc(s.vecs_tr, 1)
            pe.wait_ge(s.c_act, 1)
            for k in range(KC):
                last = tr(bank[6][:, 9 * k:9 * k + 9], m.crow[:, k * P:(k + 1) * P], m.ident[0:9, 0:9])
            last.then_inc(s.c_tr, 1)
            pe.wait_ge(s.cT_ready, 1)

            def ada(n):
                c, half = n // 2, n % 2
                if n < WHOLE:
                    pe.wait_ge(ada_in[n % ADA_SLOTS], 16 * (n // ADA_SLOTS + 1))
                else:
                    pe.wait_ge(s.c2_ready, 1)
                    pe.wait_ge(s.ada_lo, n - WHOLE + 1)
                    if half == 0 and c % 2:
                        pe.wait_ge(s.pm_done, (c - WHOLE // 2) // 2 + 1)
                if not half and c >= 2:
                    pe.wait_ge(s.mr_ready, c - 1 if c < 4 else c)
                for k in range(4):
                    first, final = half == 0 and k == 0, half == 1 and k == 3
                    if n >= WHOLE:
                        cs = m.c2[:, 4 * half + k, :]
                        mm(bank[2][:], cs, m.whi[:, n % 2, k * 512:(k + 1) * 512], start=first, stop=False)
                        last = mm(bank[2][:], cs, m.wlo[:, n % ADA_SLOTS, k * 512:(k + 1) * 512],
                                  start=False, stop=final)
                        continue
                    last = mm(ada_bank[c][0:9, :], m.cT[:, 4 * half + k, :], m.raw[:, n % ADA_SLOTS, k * 512:(k + 1) * 512],
                              start=first, stop=final)
                last.then_inc(s.ada_used, 1)

            def turn_x(t):
                R = ROWS[t]
                pe.wait_ge(s.xn_ready, t + 1)
                for half in range(2):
                    if t:
                        pe.wait_ge((s.xT_act, s.xT_dve)[half], t)
                    for k in range(4):
                        c = 4 * half + k
                        last = tr(bank[half][:, k * P:k * P + R], m.xn[0:R, t % 2, c * P:(c + 1) * P],
                                  m.ident[0:R, 0:R])
                    last.then_inc(s.x_tr, 1)

            def turn_mod(c):
                pe.wait_ge(s.mr_ready, c + 1)
                for b in range(4):
                    last = tr(bank[7][:, (4 * c + b) * 9:(4 * c + b + 1) * 9], m.mrow[:, c % 2, b * P:(b + 1) * P],
                              m.ident[0:9, 0:9])
                last.then_inc(s.mt_tr, 1)

            for t in range(TT):
                ada(t)
                if t == TP:
                    pe.wait_ge(s.vecs_ready, 1)
                    turn_mod(0)
                turn_x(t)
            ada(TT)
            turn_mod(1)
            pe.wait_ge(s.rel_ready, 1)
            for h in range(NH):
                if h >= 2:
                    pe.wait_ge(s.line_ready, h - 1)
                mm(bank[4 + h % 2][:, 0:LINE], m.relrep[:, h, :], m.oh_line[:, 0:LINE], start=True,
                   stop=True).then_inc(s.line_tr, 1)
            mm(bank[6][0:64, 0:P + 1], m.rel64[:].rearrange("p b h -> p (b h)"), m.oh_s[:], start=True,
               stop=True).then_inc(s.bias64_tr, 1)
            turn_mod(2)
            ada(6)
            ada(7)
            turn_mod(3)
            def turn_qk(t):
                R = ROWS[t]
                pe.wait_ge(s.qk_ready, t + 1)
                if t:
                    pe.wait_ge(s.qT_ready, t)
                    pe.wait_ge(s.kT_ready, t)
                else:
                    pe.wait_ge(s.xT_act, TT)
                    pe.wait_ge(s.xT_dve, TT)
                for c in range(4):
                    tr(bank[0][:, c * P:c * P + R], m.qn[0:R, c * P:(c + 1) * P], m.ident[0:R, 0:R])
                for g in range(NKV):
                    last = tr(bank[1][:, g * P:g * P + R], m.kd[0:R, g, :, :].rearrange("p a d -> p (a d)"),
                              m.ident[0:R, 0:R])
                last.then_inc(s.qk_tr, 1)

            pe.wait_ge(s.win_in, 16)
            pe.wait_ge(s.bias64_ready, 1)
            for t in range(TT):
                R, b = ROWS[t], 4 + 2 * (t % 2)
                if t == 1:
                    pe.wait_ge(s.modT_ready, 1)
                if t == TP:
                    pe.wait_ge(s.h_ready, KC + 1)
                if t >= 2:
                    pe.wait_ge(s.qk_ready, t - 1)
                    pe.wait_ge(s.vt_ready, t - 1)
                for k in range(KC):
                    if not t:
                        pe.wait_ge(s.h_ready, k + 1)
                    mm(bank[b][0:R, :], m.hT[:, k, tok(t)], m.w_in[:, k, 0:512], start=(k == 0), stop=(k == KC - 1))
                    last = mm(bank[b + 1][0:R, 0:256], m.hT[:, k, tok(t)], m.w_in[:, k, 512:768], start=(k == 0),
                              stop=(k == KC - 1))
                if t == TP:
                    pe.wait_ge(s.mr_ready, 4)
                    for k in range(KC):
                        last = mm(bank[3][0:R, :], m.hT[:, k, tok(t)], m.w_in[:, k, 768:1280], start=(k == 0),
                                  stop=(k == KC - 1))
                last.then_inc(s.z_ready, 1)
                if t:
                    turn_qk(t - 1)
            pe.wait_ge(s.vt_ready, TT)
            for g in range(4):
                if not g:
                    pe.wait_ge(s.qk_ready, TT)
                for k in range(KC):
                    last = mm(bank[4 + g][:], m.w_in[:, k, 768 + g * P:768 + (g + 1) * P], m.hT[:, k, 0:SEQ],
                              start=(k == 0), stop=(k == KC - 1))
                last.then_inc(s.u_ready, 1)
            turn_qk(TP)
            pe.wait_ge(s.us_rows, 1)
            for g in range(4):
                last = tr(bank[3][:, g * NS:(g + 1) * NS], m.uslast[:, g * P:(g + 1) * P], m.ident[0:NS, 0:NS])
            last.then_inc(s.us_tr, 1)
            pe.wait_ge(s.qT_ready, TT)
            for g in range(4):
                last = tr(bank[0][:, g * 120:(g + 1) * 120], m.sp[:, g * P:(g + 1) * P], m.ident[0:120, 0:120])
            last.then_inc(s.sp_tr, 1)

            def score(t):
                c0 = 0 if t else P
                pe.wait_ge(s.qT_ready, t + 1)
                pe.wait_ge(s.kT_ready, t + 1)
                for j in range(4):
                    if t:
                        pe.wait_ge(s.sc_used, 4 * (t - 1) + j + 1)
                    else:
                        pe.wait_ge(s.U_ready, j + 1)
                    g, odd = j // 2, j % 2
                    half = slice(64 * odd, 64 * odd + 64)
                    for a in range(2):
                        last = mm(bank[4 + j][:, a * 256 + c0:a * 256 + 256], m.qT[half, 2 * g + a, tok(t)],
                                  m.kT[half, g, t * P - P + c0:t * P + P], start=True, stop=True)
                    last.then_inc(s.sc_ready, 1)

            def turn_P(t, j):
                pe.wait_ge(s.p_ready, 4 * t + j + 1)
                if 4 * t + j >= 2:
                    pe.wait_ge(s.pt_ev, 4 * t + j - 1)
                else:
                    pe.wait_ge(s.spT_ready, 1)
                    pe.wait_ge(s.kT_ready, TT)
                for a in range(2):
                    for kb in range(0 if t else 1, 2):
                        last = tr(bank[j % 2][:, (2 * a + kb) * P:(2 * a + kb + 1) * P],
                                  m.Pb[:, 2 * j + a, kb * P:(kb + 1) * P], m.ident[:])
                last.then_inc(s.pt_tr, 1)

            def values(t, j):
                pe.wait_ge(s.pt_ev, 4 * t + j + 1)
                if not j:
                    if t:
                        pe.wait_ge(s.at_ev, t)
                    else:
                        pe.wait_ge(s.Us_ready, 1)
                for a in range(2):
                    h = 2 * j + a
                    g = h // GROUP
                    for kb in range(0 if t else 1, 2):
                        last = mm(bank[3][:, h * HD:(h + 1) * HD], m.PT[:, j % 2, (2 * a + kb) * P:(2 * a + kb + 1) * P],
                                  m.vt[:, t - 1 + kb, g * HD:(g + 1) * HD], start=(kb == (0 if t else 1)),
                                  stop=(kb == 1))
                last.then_inc(s.pv_done, 1)

            def turn_attn(t):
                pe.wait_ge(s.attn_ready, t + 1)
                for c in range(4):
                    last = tr(bank[3][:, c * P:(c + 1) * P], m.attn[:, c * P:(c + 1) * P], m.ident[:])
                last.then_inc(s.at_tr, 1)

            score(0)
            for t in range(TP):
                if t + 1 < TP:
                    score(t + 1)
                ada(4 * t + 8)
                turn_P(t, 0)
                if t:
                    turn_attn(t - 1)
                turn_P(t, 1)
                values(t, 0)
                ada(4 * t + 9)
                turn_P(t, 2)
                values(t, 1)
                turn_P(t, 3)
                pe.wait_ge(s.pooled, t + 1)
                pe.wait_ge(s.mr_ready, 2 * t + 5)
                mm(bank[2][:], m.w_pool[:, t, :], m.dT[:], start=True, stop=True).then_inc(s.pm_ready, 1)
                values(t, 2)
                ada(4 * t + 10)
                values(t, 3)
                ada(4 * t + 11)
            turn_attn(TP - 1)
            pe.wait_ge(s.newkv_in, 32)
            pe.wait_ge(s.sc_used, 4 * TP)
            for half in range(2):
                for b in range(4):
                    last = tr(bank[4 + half][:, b * P:(b + 1) * P], m.Kc[:, 4 * half + b, :], m.ident[:])
                last.then_inc(s.kc_tr, 1)
            pe.wait_ge(s.pt_ev, 4 * TP)
            for g in range(4):
                last = tr(bank[0][0:BUF, g * P:(g + 1) * P], m.U[:, g, SEQ:SEQ + BUF], m.ident[:])
            last.then_inc(s.ur_tr, 1)
            pe.wait_ge(s.dTs_ready, 4)
            pe.wait_ge(s.mr_ready, CHUNKS)
            for g in range(4):
                last = mm(bank[2][:, g * NS:(g + 1) * NS], m.w_pool[:, g, :], m.dTs[:, g, :], start=True, stop=True)
            last.then_inc(s.pms_ready, 1)
            pe.wait_ge(s.kcT_ready, 2)
            pe.wait_ge(s.qs_ready, NH)
            for b in range(NS):
                for g in range(NKV):
                    c = (b * NKV + g) * GROUP
                    last = mm(bank[6 + g][:, c:c + GROUP], m.KcT[64 * g:64 * g + 64, b, :], m.qsT[64 * g:64 * g + 64, g, b, :],
                              start=True, stop=True)
            last.then_inc(s.s_sc, 1)
            pe.wait_ge(s.wout_in, 64)
            pe.wait_ge(s.pm_done, 4)
            pe.wait_ge(s.pms_done, 4)

            def sample_values():
                pe.wait_ge(s.s_pts, 1)
                for b in range(NS):
                    for g in range(NKV):
                        c = (b * NKV + g) * GROUP
                        last = mm(bank[3][0:64, 128 + c:128 + c + GROUP], m.Vc[:, b, g * HD:(g + 1) * HD],
                                  m.PTs[:, c:c + GROUP], start=True, stop=True)
                last.then_inc(s.s_pv, 1)

            def mix_out(t, halves=(0, 1)):
                R, b = ROWS[t], 4 + 2 * (t % 2)
                if t >= 2 and 0 in halves:
                    pe.wait_ge(s.x1_ready, t - 1)
                if t == TP:
                    pe.wait_ge(s.s_mix, 2)
                for k in range(KC):
                    for half in halves:
                        last = mm(bank[b + half][0:R, :], m.mixT[:, k, tok(t)], m.w_out[:, k, 512 * half:512 * half + 512],
                                  start=(k == 0), stop=(k == KC - 1))
                if 1 in halves:
                    last.then_inc(s.xo_ready, 1)

            def turn_h2(t):
                R = ROWS[t]
                pe.wait_ge(s.h2_ready, t + 1)
                if t:
                    pe.wait_ge(s.h2T_ready, 2 * t)
                else:
                    pe.wait_ge(s.ur_ready, 1)
                for half in range(2):
                    for k in range(4):
                        c = 4 * half + k
                        last = tr(bank[half][:, k * P:k * P + R], m.h2[0:R, t % 2, c * P:(c + 1) * P], m.ident[0:R, 0:R])
                    last.then_inc(s.h2_tr, 1)

            def router(t):
                R = ROWS[t]
                pe.wait_ge(s.h2T_ready, 2 * t + 2)
                pe.wait_ge(s.wr_in, 16)
                if t:
                    pe.wait_ge(s.logit_ready, t)
                for k in range(KC):
                    last = mm(bank[2][0:R, 0:NE], m.h2T[:, k, 0:R], m.w_router[:, k, :], start=(k == 0), stop=(k == KC - 1))
                last.then_inc(s.rt_ready, 1)

            def positions(t):
                pe.wait_ge(s.mask_ready, t + 1)
                if t:
                    pe.wait_ge(s.dest_ready, t)
                else:
                    pe.wait_ge(s.s_mix, 2)
                for b in range(t + 1):
                    last = mm(bank[3][:, t * NE:(t + 1) * NE], (m.ones_b if b < t else m.tri)[:], m.mask[:, b, :],
                              start=(b == 0), stop=(b == t))
                last.then_inc(s.pos_ready, 1)

            pe.wait_ge(s.kcT_ready, 2)
            mix_out(0)
            pe.wait_ge(s.s_scT, NKV)
            tr(bank[3][0:64, 0:P], m.sT[:], m.ident[:]).then_inc(s.s_tr, 1)
            mix_out(1)
            pe.wait_ge(s.s_norm, 1)
            tr(bank[3][:, 0:64], m.P64[:], m.ident[0:64, 0:64]).then_inc(s.s_ptr, 1)
            turn_h2(0)
            router(0)
            mix_out(2)
            turn_h2(1)
            router(1)
            sample_values()
            mix_out(3)
            positions(0)
            turn_h2(2)
            router(2)
            mix_out(TP, (0,))
            positions(1)
            turn_h2(3)
            router(3)
            mix_out(TP, (1,))
            positions(2)
            positions(3)
            turn_h2(TP)
            router(TP)
            positions(TP)
            pe.wait_ge(s.logit_ready, TT)
            for t in range(TT):
                last = mm(bank[2][:, 192:192 + NE], m.ones_b[:], m.mask[:, t, :], start=(t == 0), stop=(t == TP))
            last.then_inc(s.cnt_ready, 1)

    return sems


def experts(nc, m):
    bank, i, o = m.bank, m.i, m.o
    sem = m.sem
    hi_done, lo_done, unit_used = sem("hi_done"), sem("lo_done"), sem("unit_used")
    gu_used, gmin_ready = sem("gu_used"), sem("gmin_ready")
    tables_in = sem("tables_in")
    silu_ready, act_ready, ta_tr = sem("silu_ready"), sem("act_ready"), sem("ta_tr")
    ah_done, al_done = sem("ah_done"), sem("al_done")
    tx_tr, xh_done, xl_done = sem("tx_tr"), sem("xh_done"), sem("xl_done")
    xg_in, idx_ready, col_ready = sem("xg_in"), sem("idx_ready"), sem("col_ready")
    bhl_in, b2_used, out_zero, out_ev = sem("bhl_in"), sem("b2_used"), sem("out_zero"), sem("out_ev")
    gathers, stores = sem("gathers"), sem("stores")
    scat_done, summed, ones_ready, xg_init = sem("scat_done"), sem("summed"), sem("ones_ready"), sem("xg_init")
    gf_in, f_ready, f_out = sem("gf_in"), sem("f_ready"), sem("f_out")
    y_in = [sem(f"y_in{t}") for t in range(TT)]
    gate_up = ((bank[0], bank[1]), (bank[2], bank[3]))
    outb, bank_a, bank_x = (bank[4], bank[5]), bank[6], bank[7]
    halves = (slice(0, 512), slice(512, 1024))

    def tok(t):
        return slice(t * P, t * P + ROWS[t])

    def passes(eng, body, first=0):
        with eng.Fori(first, NE) as p:
            body(p, p)
        extra = eng.value_load(m.eid[0:1, NCOL:NCOL + 1], min_val=0, max_val=NOVER)
        with eng.Fori(0, NOVER // 4) as four:
            with eng.If(four * 4 < extra):
                with eng.Fori(0, 4) as q:
                    with eng.If(four * 4 + q < extra):
                        body(four * 4 + q + NE, None)
        return extra + NE

    with nc.Block() as block:

        @block.sync
        def _(sp):
            def load(p, e):
                if e is None:
                    e = sp.value_load(m.eid[0:1, ds(p + 1)], min_val=0, max_val=NE - 1)
                for u in range(UNITS):
                    sp.wait_ge(lo_done, p * UNITS + (u + 1 - UNITS))
                    m.load_unit(sp, e, u)

            n = passes(sp, load, 1)
            sp.wait_ge(lo_done, n * UNITS)
            sp.dma_start(m.gf[:, 0, :], m.modd[3, NS:NS + 1, :].to_broadcast([P, D])).then_inc(gf_in, 16)
            sp.dma_start(m.gf[0:NS, 1, :], m.modd[3, 0:NS, :]).then_inc(gf_in, 16)
            sp.wait_ge(summed, 1)
            for t in range(TT):
                sp.dma_start(m.yf[0:ROWS[t], t, :], m.yd[tok(t), :]).then_inc(y_in[t], 16)

        @block.gpsimd
        def _(gp):
            limit = gp.to_reg(TOK - 1)
            gp.memset(m.ones2[:].bitcast(F32), 1.0).then_inc(ones_ready, 1)
            gp.wait_ge(ones_ready, 1)

            gp.tensor_copy(m.idx_g[:], m.tab[:, 0:1, 0]).then_inc(idx_ready, 1)
            gp.wait_ge(idx_ready, 1)
            gp.wait_ge(xg_init, 1)
            gp.indirect_dma_start(m.xg[:], None, m.h2d, bass.IndirectOffsetOnAxis(ap=m.idx_g[:], axis=0),
                                  bounds_check=limit, oob_is_err=False).then_inc(xg_in, 16)
            gp.dma_start(m.bhl[:], m.bd[0]).then_inc(bhl_in, 16)

            def store(p):
                gp.wait_ge(out_ev, p + 1)
                gp.sem_inc(stores, 1)
                gp.indirect_dma_start(m.yd, bass.IndirectOffsetOnAxis(ap=m.col_s[:, 0:1], axis=0), m.ost[:], None,
                                      bounds_check=limit, oob_is_err=False,
                                      compute_op=ALU.add).then_inc(scat_done, 16)
                gp.wait_ge(scat_done, p * 16 + 16)

            def one(p, e):
                was = gp.value_load(m.cols[0:1, ds(p)], min_val=0, max_val=TCOL - 1)
                will = gp.value_load(m.cols[0:1, ds(p + 2)], min_val=0, max_val=TCOL - 1)
                nxt = gp.value_load(m.eid[0:1, ds(p + 2)], min_val=0, max_val=NE - 1)
                gp.tensor_copy(m.col_s[:], m.tab[:, ds(was), :].rearrange("p c w -> p (c w)")).then_inc(col_ready, 1)
                gp.wait_ge(col_ready, p + 1)
                gp.wait_ge(xg_in, p * 16 + 16)
                gp.tensor_copy(m.idx_g[:], m.tab[:, ds(will), 0]).then_inc(idx_ready, 1)
                gp.wait_ge(idx_ready, p + 2)
                gp.wait_ge(tx_tr, p * 2 + 2)
                gp.sem_inc(gathers, 1)
                gp.indirect_dma_start(m.xg[:], None, m.h2d, bass.IndirectOffsetOnAxis(ap=m.idx_g[:], axis=0),
                                      bounds_check=limit, oob_is_err=False).then_inc(xg_in, 16)
                store(p)
                gp.wait_ge(b2_used, p + 1)
                gp.dma_start(m.bhl[:], m.bd[ds(nxt), :, :].rearrange("e a n -> (e a) n")).then_inc(bhl_in, 16)

            n = passes(gp, one)
            was = gp.value_load(m.cols[0:1, ds(n)], min_val=0, max_val=TCOL - 1)
            gp.tensor_copy(m.col_s[:], m.tab[:, ds(was), :].rearrange("p c w -> p (c w)")).then_inc(col_ready, 1)
            store(n)
            gp.sem_inc(summed, 1)
            for t in range(TT):
                gp.wait_ge(f_ready, t + 1)
                gp.dma_start(y_rows(o, t), m.yf[0:ROWS[t], t, :], accum_op=ALU.add).then_inc(f_out, 16)
            gp.wait_ge(f_out, TT * 16)

        @block.scalar
        def _(act):
            def high(p, u):
                act.wait_ge(m.raw_in[u], (p + 1) * (32 if u < W1_UNITS else 16))
                act.wait_ge(unit_used, p * UNITS + (u + 1))
                nc.scalar.copy(m.hi[:, u % HL, :], m.raw[:, u, :]).then_inc(hi_done, 1)

            def high_x(p, half):
                act.wait_ge(tx_tr, p * 2 + (half + 1))
                nc.scalar.copy(m.xTh[:, 4 * half:4 * half + 4, :].rearrange("p k n -> p (k n)"),
                               bank_x[:]).then_inc(xh_done, 1)

            def gated(p):
                act.wait_ge(col_ready, p + 1)
                act.wait_ge(unit_used, p * UNITS + HL)
                for half in range(2):
                    ins = nc.scalar.activation(m.ost[:, halves[half]], outb[half][:], ACT.Copy,
                                               scale=m.col_s[:, 1:2].bitcast(F32))
                ins.then_inc(out_ev, 1)

            def swish(p, j):
                act.wait_ge(gmin_ready, p * 2 + (j + 1))
                nc.scalar.activation(m.gate[:], m.gate[:], ACT.Silu, scale=ALPHA).then_inc(silu_ready, 1)

            def high_a(p, j):
                act.wait_ge(ta_tr, p * 2 + (j + 2))
                nc.scalar.activation(m.aTh[:, 4 * j:4 * j + 4, :].rearrange("p k n -> p (k n)"), bank_a[:], ACT.Copy,
                                     scale=1.0 / ALPHA).then_inc(ah_done, 1)

            def one(p, e, first=False):
                for u in range(3):
                    high(p, u)
                    if first and u == 1:
                        high_x(p, 0)
                        high_x(p, 1)
                gated(p)
                for u in range(3, 8):
                    high(p, u)
                swish(p, 0)
                high(p, 8)
                high(p, 9)
                high_a(p, 0)
                high(p, 10)
                swish(p, 1)
                high(p, 11)
                high_x(p + 1, 0)
                high_a(p, 1)
                high_x(p + 1, 1)

            act.wait_ge(ones_ready, 1)
            nc.scalar.activation(m.ost[0:2, 0:P], m.ones2[:].bitcast(F32), ACT.Silu).then_inc(tables_in, 1)
            act.wait_ge(tables_in, 1)
            act.wait_ge(out_zero, 1)
            one(0, 0, True)
            n = passes(act, one, 1)
            gated(n)

        @block.vector
        def _(v):
            def low(p, u):
                v.wait_ge(hi_done, p * UNITS + (u + 1))
                v.tensor_tensor(m.lo[:, u % HL, :], m.raw[:, u, :], m.hi[:, u % HL, :].bitcast(F32),
                                ALU.subtract).then_inc(lo_done, 1)

            def low_x(p, half):
                v.wait_ge(xh_done, p * 2 + (half + 1))
                ks = slice(4 * half, 4 * half + 4)
                v.tensor_tensor(m.xTl[:, ks, :].rearrange("p k n -> p (k n)"), bank_x[:],
                                m.xTh[:, ks, :].bitcast(F32).rearrange("p k n -> p (k n)"),
                                ALU.subtract).then_inc(xl_done, 1)

            def limit(p, j):
                gate, upb = gate_up[j]
                v.wait_ge(unit_used, p * UNITS + (4 * (j + 1) + HL))
                v.wait_ge(act_ready, p * 2 + (j + 1))
                v.tensor_scalar(m.gate[:], gate[:], LIMIT, None, ALU.min).then_inc(gmin_ready, 1)
                v.wait_ge(ta_tr, p * 2 + (j + 1))
                v.tensor_scalar(m.up[:], upb[:], LIMIT, -LIMIT, ALU.min, ALU.max).then_inc(gu_used, 1)

            def glu(p, j):
                v.wait_ge(gu_used, p * 2 + (j + 3))
                v.wait_ge(silu_ready, p * 2 + (j + 1))
                v.scalar_tensor_tensor(m.up[:], m.up[:], 1.0, m.gate[:], ALU.add, ALU.mult).then_inc(act_ready, 1)

            def low_a(p, j):
                v.wait_ge(ah_done, p * 2 + (j + 1))
                ks = slice(4 * j, 4 * j + 4)
                v.scalar_tensor_tensor(m.aTl[:, ks, :].rearrange("p k n -> p (k n)"), bank_a[:], 1.0 / ALPHA,
                                       m.aTh[:, ks, :].bitcast(F32).rearrange("p k n -> p (k n)"), ALU.mult,
                                       ALU.subtract).then_inc(al_done, 1)

            def one(p, e, first=False):
                for u in range(7):
                    low(p, u)
                    if first and not u:
                        low_x(p, 0)
                        low_x(p, 1)
                limit(p, 0)
                low(p, 7)
                glu(p, 0)
                low(p, 8)
                low(p, 9)
                low_a(p, 0)
                limit(p, 1)
                low(p, 10)
                glu(p, 1)
                low_x(p + 1, 0)
                low(p, 11)
                low_a(p, 1)
                low_x(p + 1, 1)

            v.memset(m.xg[:], 0.0).then_inc(xg_init, 1)
            v.memset(outb[0][:], 0.0)
            v.memset(outb[1][:], 0.0).then_inc(out_zero, 1)
            one(0, 0, True)
            passes(v, one, 1)
            v.wait_ge(gf_in, 32)
            for t in range(TT):
                R = ROWS[t]
                v.wait_ge(y_in[t], 16)
                v.tensor_tensor(m.yf[0:R, t, :], m.yf[0:R, t, :], m.gf[0:R, t // TP, :], ALU.mult).then_inc(f_ready, 1)

        @block.tensor
        def _(pe):
            mm, tr = nc.tensor.matmul, nc.tensor.transpose

            def turn_x(p, half):
                if not half:
                    pe.wait_ge(xg_in, p * 16 + 16)
                pe.wait_ge(xl_done, p * 2 + half)
                for k in range(4):
                    c = 4 * half + k
                    last = tr(bank_x[:, k * P:(k + 1) * P], m.xg[:, c * P:(c + 1) * P], m.ident[:])
                last.then_inc(tx_tr, 1)

            def turn_a(p, j):
                pe.wait_ge(act_ready, p * 2 + (j + 2))
                pe.wait_ge(al_done, p * 2 + (j + 1))
                for k in range(4):
                    last = tr(bank_a[:, k * P:(k + 1) * P], m.up[:, k * P:(k + 1) * P], m.ident[:])
                last.then_inc(ta_tr, 1)

            def products(banks, h, l, w, c, last_one):
                for b in range(2):
                    mm(banks[b][:], h, m.hi[:, w, c + 512 * b:c + 512 * b + 512], start=False, stop=False)
                for b in range(2):
                    mm(banks[b][:], h, m.lo[:, w, c + 512 * b:c + 512 * b + 512], start=False, stop=False)
                for b in range(2):
                    ins = mm(banks[b][:], l, m.hi[:, w, c + 512 * b:c + 512 * b + 512], start=False, stop=last_one)
                return ins

            def up_unit(p, u):
                j = u // 4
                pe.wait_ge(lo_done, p * UNITS + (u + 1))
                for kk in range(2):
                    k = 2 * (u % 4) + kk
                    last = products(gate_up[j], m.xTh[:, k, :], m.xTl[:, k, :], u % HL, kk * D, k == KC - 1)
                last.then_inc(unit_used, 1)

            def down_half(p, u, kk):
                k = 2 * (u - W1_UNITS) + kk
                if not kk:
                    pe.wait_ge(lo_done, p * UNITS + (u + 1))
                    pe.wait_ge(al_done, p * 2 + (2 if u < 10 else 3))
                return products(outb, m.aTh[:, k, :], m.aTl[:, k, :], u % HL, kk * D, k == KC - 1)

            def bias(banks, c0, c1):
                mm(banks[0][:], m.ones2[:], m.bhl[:, c0:c0 + 512], start=True, stop=False)
                return mm(banks[1][:], m.ones2[:], m.bhl[:, c1:c1 + 512], start=True, stop=False)

            def one(p, e):
                pe.wait_ge(xl_done, p * 2 + 2)
                pe.wait_ge(bhl_in, p * 16 + 16)
                for j in range(2):
                    pe.wait_ge(gu_used, p * 2 + (j + 1))
                    bias(gate_up[j], 512 * j, D + 512 * j)
                    for u in range(4 * j, 4 * j + 4):
                        if u == 7:
                            turn_a(p, 0)
                        up_unit(p, u)
                pe.wait_ge(out_ev, p + 1)
                bias(outb, 2 * D, 2 * D + 512).then_inc(b2_used, 1)
                down_half(p, 8, 0)
                down_half(p, 8, 1).then_inc(unit_used, 1)
                turn_x(p + 1, 0)
                down_half(p, 9, 0)
                down_half(p, 9, 1).then_inc(unit_used, 1)
                turn_a(p, 1)
                turn_x(p + 1, 1)
                down_half(p, 10, 0)
                down_half(p, 10, 1).then_inc(unit_used, 1)
                down_half(p, 11, 0)
                down_half(p, 11, 1).then_inc(unit_used, 1)

            pe.sem_inc(unit_used, HL)
            pe.sem_inc(gu_used, 2)
            pe.sem_inc(act_ready, 1)
            pe.sem_inc(ta_tr, 1)
            pe.sem_inc(al_done, 1)
            pe.wait_ge(ones_ready, 1)
            pe.wait_ge(xg_in, 16)
            for half in range(2):
                if half:
                    pe.wait_ge(xl_done, 1)
                for k in range(4):
                    c = 4 * half + k
                    last = tr(bank_x[:, k * P:(k + 1) * P], m.xg[:, c * P:(c + 1) * P], m.ident[:])
                last.then_inc(tx_tr, 1)
            passes(pe, one)


OUTS = [("y_prompt", (1, SEQ, D)), ("y_sample", (NS, 1, D)), ("new_k_prompt", (1, 1, P, NKV, HD)),
        ("new_v_prompt", (1, 1, P, NKV, HD)), ("new_pool_prompt", (1, 1, BUF, PW)),
        ("new_k_sample", (1, NS, P, NKV, HD)), ("new_v_sample", (1, NS, P, NKV, HD)),
        ("new_pool_sample", (1, NS, BUF, PW))]


def distance_bucket():
    n = np.arange(P)
    far = np.log(np.maximum(n, 1).astype(np.float32) / np.float32(16)) / np.float32(np.log(128 / 16)) * np.float32(16)
    return np.where(n < 16, n, np.minimum(16 + far.astype(np.int32), NE - 1))


def constants():
    bucket = distance_bucket()
    line = np.zeros((NE + 1, 3 * P), np.float32)
    line[NE, :] = NEG
    for d in range(P):
        line[:, 2 * P - 1 - d] = 0.0
        line[bucket[d], 2 * P - 1 - d] = 1.0
    samples = np.zeros((NE + 1, P + 1), np.float32)
    for c in range(P):
        samples[bucket[(P - c) % P], c] = 1.0
    samples[NE, P] = 1.0
    rec = np.array([[1.0 / min(c + 1, w) for c in range(BUF + 1)] for w in WINDOWS], np.float32)
    return {"oh_line": line, "oh_s": samples, "rec": rec}


def kernel(**inputs):
    import concourse.bacc as bacc
    from concourse.bass_utils import run_bass_kernel_spmd

    nc = bacc.Bacc("TRN2", target_bir_lowering=False, num_devices=1)
    arrays, ins, outs = {}, {}, {}
    for name, a in {**inputs, **constants()}.items():
        a = np.ascontiguousarray(a)
        arrays[f"in_{name}"] = a
        ins[name] = nc.dram_tensor(f"in_{name}", a.shape, mybir.dt.from_np(a.dtype), kind="ExternalInput").ap()
    for name, shape in OUTS:
        outs[name] = nc.dram_tensor(f"out_{name}", shape, F32, kind="ExternalOutput").ap()
    build(nc, ins, outs)
    r = run_bass_kernel_spmd(nc, [arrays], core_ids=[0])
    return tuple(r.results[0][f"out_{name}"] for name, _ in OUTS)
```
